# Optimizing a Trainium2 kernel written in Bass

```python
import math
import jax
import jax.numpy as jnp
from jax import lax
import numpy as np

D_MODEL = 2048
BATCH = 1
SEQ = 512
DEPTH = 1
DEC_BATCH = 8
DEC_SEQ = 4
PAST_LEN = 256
PAGE_SIZE = 128

HEAD_DIM = 128
CONV_A_WIDTH = D_MODEL // 4
CONV_A_K = 3
NSA_HEADS = D_MODEL // (2 * HEAD_DIM)
NSA_KV_HEADS = 2
NSA_REP = NSA_HEADS // NSA_KV_HEADS
NSA_WIDTH = NSA_HEADS * HEAD_DIM
CMP_BLOCK = 32
CMP_STRIDE = 16
CMP_HIDDEN = 2 * HEAD_DIM
SLC_BLOCK = 64
N_SELECT = 16
WINDOW = 512
Q_BLOCK = 128
KV_SLOTS = 4
GDN_HEADS = D_MODEL // (4 * HEAD_DIM)
GDN_WIDTH = GDN_HEADS * HEAD_DIM
GDN_CONV_K = 4
GDN_CHUNK = 64
MIX_WIDTH = CONV_A_WIDTH + NSA_WIDTH + GDN_WIDTH
REL_BUCKETS = 32
REL_MAX_DIST = 1024
D_FF = 11 * D_MODEL // 4
FFN_CONV_K = 3
EPS = 1e-6
NEG_INF = -1e30
FORCE_SCORE = 1e4
IN_SPLITS = (CONV_A_WIDTH, CONV_A_WIDTH, CONV_A_WIDTH,
             NSA_WIDTH, 6 * NSA_KV_HEADS * HEAD_DIM, 3 * NSA_HEADS,
             3 * GDN_WIDTH, GDN_HEADS, GDN_HEADS, GDN_WIDTH)
IN_WIDTH = sum(IN_SPLITS)

kernel_name = 'hybrid_conv_nsa_gdn_decoder_step'

def rmsnorm(x, g):
    xf = x.astype(jnp.float32)
    y = xf * lax.rsqrt(jnp.mean(xf * xf, axis=-1, keepdims=True) + EPS)
    return (y * g.astype(jnp.float32)).astype(x.dtype)

def l2norm(x):
    xf = x.astype(jnp.float32)
    return (xf * lax.rsqrt(jnp.sum(xf * xf, axis=-1, keepdims=True) + EPS)).astype(x.dtype)

def masked_softmax(s, mask):
    s = jnp.where(mask, s, NEG_INF)
    m = jnp.max(s, axis=-1, keepdims=True)
    e = jnp.where(mask, jnp.exp(s - m), 0.0)
    z = jnp.sum(e, axis=-1, keepdims=True)
    return e / jnp.where(z > 0, z, 1.0)

def split_proj(z):
    offs = []
    acc = 0
    for s in IN_SPLITS[:-1]:
        acc += s
        offs.append(acc)
    return jnp.split(z, offs, axis=-1)

def causal_dwconv(x, hist, w):
    K = w.shape[0]
    T = x.shape[1]
    xx = jnp.concatenate([hist.astype(x.dtype), x], axis=1)
    out = xx[:, 0:T] * w[0]
    for i in range(1, K):
        out = out + xx[:, i:i + T] * w[i]
    return out, xx[:, T:]

def rel_bucket(dist):
    n = jnp.maximum(dist, 0)
    exact = REL_BUCKETS // 2
    nf = jnp.maximum(n, 1).astype(jnp.float32)
    far = exact + (jnp.log(nf / exact) / math.log(REL_MAX_DIST / exact)
                   * (REL_BUCKETS - exact)).astype(jnp.int32)
    return jnp.where(n < exact, n, jnp.minimum(far, REL_BUCKETS - 1))

def compress_blocks(rows, pe, w1, w2):
    Bn, L = rows.shape[:2]
    nc = (L - CMP_BLOCK) // CMP_STRIDE + 1
    idx = CMP_STRIDE * jnp.arange(nc)[:, None] + jnp.arange(CMP_BLOCK)[None, :]
    blk = rows[:, idx] + pe[:, None, :]
    blk = jnp.swapaxes(blk, 2, 3).reshape(Bn, nc, NSA_KV_HEADS, CMP_BLOCK * HEAD_DIM)
    return jax.nn.gelu(blk @ w1) @ w2

def cmp_attend(q, q_pos, kc, vc, rel_bias):
    T = q.shape[1]
    nc = kc.shape[1]
    ends = CMP_STRIDE * jnp.arange(nc) + CMP_BLOCK - 1
    dist = q_pos[:, None] - ends[None, :]
    s = jnp.einsum('btgrd,bcgd->bgrtc', q, kc).astype(jnp.float32)
    bias = rel_bias[rel_bucket(dist)].reshape(T, nc, NSA_KV_HEADS, NSA_REP).transpose(2, 3, 0, 1)
    p = masked_softmax(s + bias.astype(jnp.float32), dist >= 0)
    o = jnp.einsum('bgrtc,bcgd->btgrd', p.astype(vc.dtype), vc)
    return o, p

def select_blocks(p_cmp, q_pos, n_slc):
    nc = p_cmp.shape[-1]
    cs = CMP_STRIDE * jnp.arange(nc)
    ss = SLC_BLOCK * jnp.arange(n_slc)
    overlap = ((cs[:, None] < ss[None, :] + SLC_BLOCK)
               & (cs[:, None] + CMP_BLOCK > ss[None, :])).astype(jnp.float32)
    imp = jnp.einsum('bgrtc,cs->bgts', p_cmp, overlap)
    cur = (q_pos // SLC_BLOCK)[:, None]
    blk = jnp.arange(n_slc)[None, :]
    forced = (blk == 0) | (blk == cur) | (blk == cur - 1)
    imp = jnp.where(forced, FORCE_SCORE, imp)
    imp = jnp.where(blk <= cur, imp, -1.0)
    _, idx = lax.top_k(imp, min(N_SELECT, n_slc))
    return idx

def to_blocks(rows, n_slc):
    Bn, L = rows.shape[:2]
    rows = jnp.pad(rows, ((0, 0), (0, n_slc * SLC_BLOCK - L), (0, 0), (0, 0)))
    return rows.reshape(Bn, n_slc, SLC_BLOCK, NSA_KV_HEADS, HEAD_DIM).transpose(0, 3, 1, 2, 4)

def slc_attend(q, q_pos, idx, kb, vb, rel_bias):
    Bn, T = q.shape[:2]
    n_sel = idx.shape[-1]
    bi = jnp.arange(Bn)[:, None, None]
    gi = jnp.arange(NSA_KV_HEADS)[None, :, None]
    flat = idx.reshape(Bn, NSA_KV_HEADS, T * n_sel)
    ks = kb[bi, gi, flat].reshape(Bn, NSA_KV_HEADS, T, n_sel * SLC_BLOCK, HEAD_DIM)
    vs = vb[bi, gi, flat].reshape(Bn, NSA_KV_HEADS, T, n_sel * SLC_BLOCK, HEAD_DIM)
    s = jnp.einsum('btgrd,bgtmd->bgrtm', q, ks).astype(jnp.float32)
    kpos = (idx[..., None] * SLC_BLOCK + jnp.arange(SLC_BLOCK)).reshape(Bn, NSA_KV_HEADS, T, n_sel * SLC_BLOCK)
    dist = q_pos[None, None, :, None] - kpos
    tbl = rel_bias.reshape(REL_BUCKETS, NSA_KV_HEADS, NSA_REP).transpose(1, 0, 2)
    bias = tbl[jnp.arange(NSA_KV_HEADS)[None, :, None, None], rel_bucket(dist)]
    s = s + jnp.moveaxis(bias, -1, 2).astype(jnp.float32)
    p = masked_softmax(s, (dist >= 0)[:, :, None])
    return jnp.einsum('bgrtm,bgtmd->btgrd', p.astype(vs.dtype), vs)

def win_attend_banded(q, k, v, rel_bias):
    Bn, T = q.shape[:2]
    nqb = T // Q_BLOCK
    span = WINDOW + Q_BLOCK
    kp = jnp.pad(k, ((0, 0), (WINDOW, 0), (0, 0), (0, 0)))
    vp = jnp.pad(v, ((0, 0), (WINDOW, 0), (0, 0), (0, 0)))
    kidx = Q_BLOCK * jnp.arange(nqb)[:, None] + jnp.arange(span)[None, :]
    kw = kp[:, kidx]
    vw = vp[:, kidx]
    qb = q.reshape(Bn, nqb, Q_BLOCK, NSA_KV_HEADS, NSA_REP, HEAD_DIM)
    s = jnp.einsum('bnqgrd,bnkgd->bgrnqk', qb, kw).astype(jnp.float32)
    qpos = Q_BLOCK * jnp.arange(nqb)[:, None] + jnp.arange(Q_BLOCK)[None, :]
    kpos = kidx - WINDOW
    dist = qpos[:, :, None] - kpos[:, None, :]
    mask = (dist >= 0) & (dist <= WINDOW) & (kpos[:, None, :] >= 0)
    bias = rel_bias[rel_bucket(dist)].reshape(nqb, Q_BLOCK, span, NSA_KV_HEADS, NSA_REP).transpose(3, 4, 0, 1, 2)
    p = masked_softmax(s + bias.astype(jnp.float32), mask)
    o = jnp.einsum('bgrnqk,bnkgd->bnqgrd', p.astype(vw.dtype), vw)
    return o.reshape(Bn, T, NSA_KV_HEADS, NSA_REP, HEAD_DIM)

def win_attend_direct(q, q_pos, k, v, k_pos, rel_bias):
    T = q.shape[1]
    nk = k.shape[1]
    s = jnp.einsum('btgrd,bkgd->bgrtk', q, k).astype(jnp.float32)
    dist = q_pos[:, None] - k_pos[None, :]
    mask = (dist >= 0) & (dist <= WINDOW)
    bias = rel_bias[rel_bucket(dist)].reshape(T, nk, NSA_KV_HEADS, NSA_REP).transpose(2, 3, 0, 1)
    p = masked_softmax(s + bias.astype(jnp.float32), mask)
    return jnp.einsum('bgrtk,bkgd->btgrd', p.astype(v.dtype), v)

def nsa_mixer(q, q_pos, rows, win_k, win_v, win_pos, gates, k_norm_g, cmp_pe, cmp_w1, cmp_w2, rel_bias):
    Bn, T = q.shape[:2]
    L = rows.shape[1]
    kc = rmsnorm(compress_blocks(rows[:, :, 0], cmp_pe[0], cmp_w1[0], cmp_w2[0]), k_norm_g)
    vc = compress_blocks(rows[:, :, 1], cmp_pe[1], cmp_w1[1], cmp_w2[1])
    o_cmp, p_cmp = cmp_attend(q, q_pos, kc, vc, rel_bias)
    n_slc = -(-L // SLC_BLOCK)
    idx = select_blocks(p_cmp, q_pos, n_slc)
    kb = to_blocks(rows[:, :, 2], n_slc)
    vb = to_blocks(rows[:, :, 3], n_slc)
    if win_pos is None:
        nqb = T // Q_BLOCK
        q_blocks = jnp.moveaxis(q.reshape(Bn, nqb, Q_BLOCK, NSA_KV_HEADS, NSA_REP, HEAD_DIM), 1, 0)
        i_blocks = jnp.moveaxis(idx.reshape(Bn, NSA_KV_HEADS, nqb, Q_BLOCK, idx.shape[-1]), 2, 0)
        p_blocks = q_pos.reshape(nqb, Q_BLOCK)
        o_slc = lax.map(lambda a: slc_attend(a[0], a[2], a[1], kb, vb, rel_bias), (q_blocks, i_blocks, p_blocks))
        o_slc = jnp.moveaxis(o_slc, 0, 1).reshape(Bn, T, NSA_KV_HEADS, NSA_REP, HEAD_DIM)
        o_win = win_attend_banded(q, win_k, win_v, rel_bias)
    else:
        o_slc = slc_attend(q, q_pos, idx, kb, vb, rel_bias)
        o_win = win_attend_direct(q, q_pos, win_k, win_v, win_pos, rel_bias)
    o = (gates[:, :, 0, :, :, None] * o_cmp + gates[:, :, 1, :, :, None] * o_slc
         + gates[:, :, 2, :, :, None] * o_win)
    return o.reshape(Bn, T, NSA_WIDTH)

def gated_delta_chunked(q, k, v, g, beta, s0):
    f32 = jnp.float32
    Bn, T, H, DK = q.shape
    DV = v.shape[-1]
    C = min(GDN_CHUNK, T)
    Tp = -(-T // C) * C
    pad = Tp - T

    def prep(a):
        a = a.astype(f32)
        a = jnp.pad(a, [(0, 0), (0, pad)] + [(0, 0)] * (a.ndim - 2))
        a = a.reshape((Bn, Tp // C, C) + a.shape[2:])
        return jnp.moveaxis(jnp.moveaxis(a, 3, 2), 1, 0)

    q, k, v, g, beta = prep(q), prep(k), prep(v), prep(g), prep(beta)
    gc = jnp.cumsum(g, axis=-1)
    tri_incl = jnp.tril(jnp.ones((C, C), bool))
    tri_strict = jnp.tril(jnp.ones((C, C), bool), -1)
    decay = jnp.exp(jnp.where(tri_incl, gc[..., :, None] - gc[..., None, :], -jnp.inf))
    kb = k * beta[..., None]
    low = jnp.where(tri_strict, jnp.einsum('nbhid,nbhjd->nbhij', kb, k) * decay, 0.0)
    a_mat = low + jnp.eye(C, dtype=f32)
    u = lax.linalg.triangular_solve(a_mat, v * beta[..., None], left_side=True, lower=True, unit_diagonal=True)
    w = lax.linalg.triangular_solve(a_mat, kb * jnp.exp(gc)[..., None], left_side=True, lower=True, unit_diagonal=True)
    qk = jnp.where(tri_incl, jnp.einsum('nbhid,nbhjd->nbhij', q, k) * decay, 0.0)

    def step(S, xs):
        q_c, k_c, u_c, w_c, g_c, qk_c = xs
        v_new = u_c - jnp.einsum('bhcd,bhde->bhce', w_c, S)
        o = (jnp.einsum('bhcd,bhde->bhce', q_c * jnp.exp(g_c)[..., None], S)
             + jnp.einsum('bhij,bhje->bhie', qk_c, v_new))
        g_last = g_c[..., -1]
        S = (S * jnp.exp(g_last)[..., None, None]
             + jnp.einsum('bhcd,bhce->bhde', k_c * jnp.exp(g_last[..., None] - g_c)[..., None], v_new))
        return S, o

    S, o = lax.scan(step, s0.astype(f32), (q, k, u, w, gc, qk))
    o = jnp.swapaxes(jnp.moveaxis(o, 0, 1), 2, 3).reshape(Bn, Tp, H, DV)[:, :T]
    return o, S

def gdn_mixer(qkv, a_in, b_in, z, hist, s0, conv_w, a_log, dt_bias, norm_g):
    Bn, T = qkv.shape[:2]
    u, new_hist = causal_dwconv(qkv, hist, conv_w)
    u = jax.nn.silu(u)
    q, k, v = jnp.split(u, 3, axis=-1)
    q = l2norm(q.reshape(Bn, T, GDN_HEADS, HEAD_DIM)) * HEAD_DIM ** -0.5
    k = l2norm(k.reshape(Bn, T, GDN_HEADS, HEAD_DIM))
    v = v.reshape(Bn, T, GDN_HEADS, HEAD_DIM)
    beta = jax.nn.sigmoid(b_in.astype(jnp.float32))
    g = -jnp.exp(a_log.astype(jnp.float32)) * jax.nn.softplus(a_in.astype(jnp.float32) + dt_bias.astype(jnp.float32))
    o, s_new = gated_delta_chunked(q, k, v, g, beta, s0)
    o = rmsnorm(o.astype(z.dtype), norm_g) * jax.nn.silu(z.reshape(Bn, T, GDN_HEADS, HEAD_DIM))
    return o.reshape(Bn, T, GDN_WIDTH), new_hist, s_new.astype(s0.dtype)

def trunk_layer(x, pos, past_rows, win_buf, hist_a, hist_gdn, s_gdn, hist_ffn, rel_bias, lw):
    (norm_mix_g, w_in, conv_a_w, q_norm_g, k_norm_g, cmp_pe, cmp_w1, cmp_w2,
     gdn_conv_w, gdn_a_log, gdn_dt_bias, gdn_norm_g, out_norm_a, out_norm_b, w_out,
     norm_ffn_g, ffn_up, ffn_conv_w, ffn_down) = lw
    Bn, T, _ = x.shape
    (a_b, a_c, a_h, nq, nkv, ngate, gqkv, ga, gb, gz) = split_proj(rmsnorm(x, norm_mix_g) @ w_in)
    conv_out, new_hist_a = causal_dwconv(a_c * a_h, hist_a, conv_a_w)
    y_a = a_b * conv_out
    q = rmsnorm(nq.reshape(Bn, T, NSA_KV_HEADS, NSA_REP, HEAD_DIM), q_norm_g) * HEAD_DIM ** -0.5
    kv = nkv.reshape(Bn, T, 3, 2, NSA_KV_HEADS, HEAD_DIM)
    rows = jnp.stack([kv[:, :, 0, 0], kv[:, :, 0, 1], rmsnorm(kv[:, :, 1, 0], k_norm_g), kv[:, :, 1, 1]], axis=2)
    win_rows = jnp.stack([rmsnorm(kv[:, :, 2, 0], k_norm_g), kv[:, :, 2, 1]], axis=2)
    gates = jax.nn.sigmoid(ngate.astype(jnp.float32)).reshape(Bn, T, 3, NSA_KV_HEADS, NSA_REP).astype(x.dtype)
    if past_rows is None:
        full_rows = rows
        win_all = win_rows
        win_pos = None
        new_win = win_rows[:, -min(WINDOW, T):]
    else:
        past_len = past_rows.shape[1]
        wb = win_buf.shape[1]
        full_rows = jnp.concatenate([past_rows, rows], axis=1)
        win_all = jnp.concatenate([win_buf, win_rows], axis=1)
        win_pos = past_len - wb + jnp.arange(wb + T)
        new_win = win_all[:, -min(WINDOW, past_len + T):]
    y_b = nsa_mixer(q, pos, full_rows, win_all[:, :, 0], win_all[:, :, 1], win_pos, gates,
                    k_norm_g, cmp_pe, cmp_w1, cmp_w2, rel_bias)
    y_c, new_hist_gdn, s_new = gdn_mixer(gqkv, ga, gb, gz, hist_gdn, s_gdn,
                                         gdn_conv_w, gdn_a_log, gdn_dt_bias, gdn_norm_g)
    mix = jnp.concatenate([rmsnorm(y_a, out_norm_a), rmsnorm(y_b, out_norm_b), y_c], axis=-1)
    h = x + mix @ w_out
    up = rmsnorm(h, norm_ffn_g) @ ffn_up
    up, new_hist_ffn = causal_dwconv(up, hist_ffn, ffn_conv_w)
    ga_f, gv_f = jnp.split(up, 2, axis=-1)
    out = h + (jax.nn.silu(ga_f) * gv_f) @ ffn_down
    return out, (rows, new_win, new_hist_a, new_hist_gdn, s_new, new_hist_ffn)

def setup_inputs(seed: int = 0) -> dict:
    key = jax.random.key(seed)
    ks = iter(jax.random.split(key, 40))
    f32 = jnp.float32

    def nrm(shape, scale):
        return scale * jax.random.normal(next(ks), shape, f32)

    def gain(shape):
        return 1.0 + nrm(shape, 0.02)

    n_pages = PAST_LEN // PAGE_SIZE
    n_used = DEC_BATCH * n_pages
    n_pool = n_used + max(1, n_used // 4)
    wb = min(WINDOW, PAST_LEN)
    x_prompt = nrm((BATCH, SEQ, D_MODEL), 1.0)
    x_sample = nrm((DEC_BATCH, DEC_SEQ, D_MODEL), 1.0)
    cache_kv = nrm((DEPTH, n_pool, PAGE_SIZE, KV_SLOTS, NSA_KV_HEADS, HEAD_DIM), 1.0)
    cache_win = nrm((DEPTH, DEC_BATCH, wb, 2, NSA_KV_HEADS, HEAD_DIM), 1.0)
    state_conv_a = nrm((DEPTH, DEC_BATCH, CONV_A_K - 1, CONV_A_WIDTH), 1.0)
    state_gdn_conv = nrm((DEPTH, DEC_BATCH, GDN_CONV_K - 1, 3 * GDN_WIDTH), 1.0)
    state_gdn = nrm((DEPTH, DEC_BATCH, GDN_HEADS, HEAD_DIM, HEAD_DIM), 0.1)
    state_ffn_conv = nrm((DEPTH, DEC_BATCH, FFN_CONV_K - 1, 2 * D_FF), 1.0)
    page_table = jax.random.permutation(next(ks), n_pool)[:n_used].reshape(DEC_BATCH, n_pages).astype(jnp.int32)
    rel_bias = nrm((REL_BUCKETS, NSA_HEADS), 0.5)
    dt = jnp.exp(jax.random.uniform(next(ks), (DEPTH, GDN_HEADS), f32, math.log(1e-3), math.log(1e-1)))
    return {
        'x_prompt': x_prompt,
        'x_sample': x_sample,
        'cache_kv': cache_kv,
        'cache_win': cache_win,
        'state_conv_a': state_conv_a,
        'state_gdn_conv': state_gdn_conv,
        'state_gdn': state_gdn,
        'state_ffn_conv': state_ffn_conv,
        'page_table': page_table,
        'rel_bias': rel_bias,
        'norm_mix_g': gain((DEPTH, D_MODEL)),
        'w_in': nrm((DEPTH, D_MODEL, IN_WIDTH), D_MODEL ** -0.5),
        'conv_a_w': nrm((DEPTH, CONV_A_K, CONV_A_WIDTH), CONV_A_K ** -0.5),
        'q_norm_g': gain((DEPTH, HEAD_DIM)),
        'k_norm_g': gain((DEPTH, HEAD_DIM)),
        'cmp_pe': nrm((DEPTH, 2, CMP_BLOCK, HEAD_DIM), 0.1),
        'cmp_w1': nrm((DEPTH, 2, CMP_BLOCK * HEAD_DIM, CMP_HIDDEN), (CMP_BLOCK * HEAD_DIM) ** -0.5),
        'cmp_w2': nrm((DEPTH, 2, CMP_HIDDEN, HEAD_DIM), CMP_HIDDEN ** -0.5),
        'gdn_conv_w': nrm((DEPTH, GDN_CONV_K, 3 * GDN_WIDTH), GDN_CONV_K ** -0.5),
        'gdn_a_log': jnp.log(jax.random.uniform(next(ks), (DEPTH, GDN_HEADS), f32, 1.0, 16.0)),
        'gdn_dt_bias': dt + jnp.log(-jnp.expm1(-dt)),
        'gdn_norm_g': gain((DEPTH, HEAD_DIM)),
        'out_norm_a': gain((DEPTH, CONV_A_WIDTH)),
        'out_norm_b': gain((DEPTH, NSA_WIDTH)),
        'w_out': nrm((DEPTH, MIX_WIDTH, D_MODEL), MIX_WIDTH ** -0.5),
        'norm_ffn_g': gain((DEPTH, D_MODEL)),
        'ffn_up': nrm((DEPTH, D_MODEL, 2 * D_FF), D_MODEL ** -0.5),
        'ffn_conv_w': nrm((DEPTH, FFN_CONV_K, 2 * D_FF), FFN_CONV_K ** -0.5),
        'ffn_down': nrm((DEPTH, D_FF, D_MODEL), D_FF ** -0.5),
    }

def reference(x_prompt, x_sample, cache_kv, cache_win, state_conv_a, state_gdn_conv, state_gdn,
              state_ffn_conv, page_table, rel_bias, norm_mix_g, w_in, conv_a_w, q_norm_g, k_norm_g,
              cmp_pe, cmp_w1, cmp_w2, gdn_conv_w, gdn_a_log, gdn_dt_bias, gdn_norm_g, out_norm_a,
              out_norm_b, w_out, norm_ffn_g, ffn_up, ffn_conv_w, ffn_down):
    Bp, T = x_prompt.shape[:2]
    Ds, Ts = x_sample.shape[:2]
    past_len = page_table.shape[1] * cache_kv.shape[2]
    pos_p = jnp.arange(T)
    pos_s = past_len + jnp.arange(Ts)
    dt = x_prompt.dtype
    xp, xs = x_prompt, x_sample
    st_p, st_s = [], []
    for l in range(DEPTH):
        lw = (norm_mix_g[l], w_in[l], conv_a_w[l], q_norm_g[l], k_norm_g[l], cmp_pe[l], cmp_w1[l], cmp_w2[l],
              gdn_conv_w[l], gdn_a_log[l], gdn_dt_bias[l], gdn_norm_g[l], out_norm_a[l], out_norm_b[l], w_out[l],
              norm_ffn_g[l], ffn_up[l], ffn_conv_w[l], ffn_down[l])
        xp, sp = trunk_layer(
            xp, pos_p, None, None,
            jnp.zeros((Bp, CONV_A_K - 1, CONV_A_WIDTH), dt),
            jnp.zeros((Bp, GDN_CONV_K - 1, 3 * GDN_WIDTH), dt),
            jnp.zeros((Bp, GDN_HEADS, HEAD_DIM, HEAD_DIM), dt),
            jnp.zeros((Bp, FFN_CONV_K - 1, 2 * D_FF), dt),
            rel_bias, lw)
        past_rows = cache_kv[l, page_table].reshape(Ds, past_len, KV_SLOTS, NSA_KV_HEADS, HEAD_DIM)
        xs, ss = trunk_layer(
            xs, pos_s, past_rows, cache_win[l], state_conv_a[l], state_gdn_conv[l], state_gdn[l],
            state_ffn_conv[l], rel_bias, lw)
        st_p.append(sp)
        st_s.append(ss)
    kv_rows_prompt = jnp.stack([s[0] for s in st_p])
    kv_rows_sample = jnp.stack([s[0] for s in st_s])
    win_prompt = jnp.stack([s[1] for s in st_p])
    win_sample = jnp.stack([s[1] for s in st_s])
    conv_a_prompt = jnp.stack([s[2] for s in st_p])
    conv_a_sample = jnp.stack([s[2] for s in st_s])
    gdn_conv_prompt = jnp.stack([s[3] for s in st_p])
    gdn_conv_sample = jnp.stack([s[3] for s in st_s])
    gdn_state_prompt = jnp.stack([s[4] for s in st_p])
    gdn_state_sample = jnp.stack([s[4] for s in st_s])
    ffn_conv_prompt = jnp.stack([s[5] for s in st_p])
    ffn_conv_sample = jnp.stack([s[5] for s in st_s])
    return (xp, xs, kv_rows_prompt, kv_rows_sample, win_prompt, win_sample, conv_a_prompt, conv_a_sample,
            gdn_conv_prompt, gdn_conv_sample, gdn_state_prompt, gdn_state_sample, ffn_conv_prompt, ffn_conv_sample)


_drawn_inputs = setup_inputs


def setup_inputs(seed=0):
    import zlib

    import numpy as np

    out = dict(_drawn_inputs(seed))
    spreads = {}
    factors = {'q_norm_g': 8.0,
     'k_norm_g': 3.973,
     'gdn_norm_g': 8.0,
     'out_norm_a': 6.822,
     'out_norm_b': 5.023}
    for name, (base, spread) in spreads.items():
        noise = np.random.default_rng([zlib.crc32(name.encode()), seed]).standard_normal(out[name].shape)
        drawn = base * np.exp(spread * noise) if base else spread * noise
        out[name] = jnp.asarray(drawn.astype(out[name].dtype))
    for name, factor in factors.items():
        out[name] = (out[name] * factor).astype(out[name].dtype)
    return out
```

```python
import math
from contextlib import ExitStack

import numpy as np
import concourse.bass as bass
from concourse import mybir

F32 = mybir.dt.float32
I32 = mybir.dt.int32
ALU = mybir.AluOpType
ACT = mybir.ActivationFunctionType
AX = mybir.AxisListType.X

P = 128
DM = 2048
KC = DM // P
TP, NB, TS = 512, 8, 4
NS = NB * TS
NT = TP + NS
HALF = (256, NT - 256)
QH, G, REP = 8, 2, 4
GH = 4
PAST, PAGE = 256, 128
KEYS = PAST + TS
CB, CS = 32, 16
NCP, NCS = (TP - CB) // CS + 1, (KEYS - CB) // CS + 1
DFF = 5632
FC = DFF // P
NPOOL = 20
EPS = 1e-6
NEG = -1e30
SLOTS = 4
UNIT = KC * P
DT = 11
DU = FC // DT
N_A, N_KVQ, N_GZ = 12, 20, 16
PROJ = N_A + N_KVQ + N_GZ
U_CMP = PROJ
U_OUT = U_CMP + 8
U_UP = U_OUT + KC
U_DN = U_UP + 2 * FC
ROW3, SEG3 = 2 + TP + NB * (2 + TS), 2 + TS
ROW4, SEG4 = 3 + TP + NB * (3 + TS), 3 + TS
TAB = 640

C_ONE, C_ID, C_TRI, C_SU = 0, 128, 256, 384
C_LEV = 512
C_GRP, C_TRIB, C_SUB = C_LEV + 7 * 128, C_LEV + 7 * 128 + 32, C_LEV + 7 * 128 + 64
C_BM = C_SUB + 32
C_VAL = C_BM + 8
C_EPS = C_VAL + 7
NCONST = C_EPS + 3
G_MIX, G_FFN, G_OA, G_OB, G_Q, G_K, G_GDN = 0, 16, 32, 36, 44, 45, 46


def shape_constants():
    c = np.zeros((P, NCONST), np.float32)
    row, col = np.arange(P)[:, None], np.arange(P)[None, :]
    c[:, C_ONE:C_ONE + P] = 1
    c[:, C_ID:C_ID + P] = row == col
    c[:, C_TRI:C_TRI + P] = row <= col
    c[:, C_SU:C_SU + P] = row < col
    for s in range(7):
        same, split = row >> (s + 1) == col >> (s + 1), row >> s != col >> s
        c[:, C_LEV + s * P:C_LEV + (s + 1) * P] = same & split & (row < col)
    r, q = row[:NS], col[:, :NS]
    c[:NS, C_GRP:C_GRP + NS] = r // TS == q // TS
    c[:NS, C_TRIB:C_TRIB + NS] = (r // TS == q // TS) & (r <= q)
    c[:NS, C_SUB:C_SUB + NS] = (r // TS == q // TS) & (r < q)
    c[:NS, C_BM:C_BM + NB] = r // TS == np.arange(NB)[None, :]
    c[:, C_VAL:C_VAL + 7] = row >= CB - 1 + CS * np.arange(7)[None, :]
    c[:, C_EPS:C_EPS + 3] = [EPS, P * EPS, 1.0]
    dist = TP - 1 - np.arange(TAB)
    n = np.maximum(dist, 0)
    nf = np.maximum(n, 1).astype(np.float32)
    far = 16 + (np.log(nf / np.float32(16)) / np.float32(math.log(64)) * np.float32(16)).astype(np.int32)
    bucket = np.where(n < 16, n, np.minimum(far, 31))
    onehot = ((np.arange(32)[:, None] == bucket[None, :]) & (dist >= 0)[None, :]).astype(np.float32)
    neg = np.broadcast_to(np.where(dist >= 0, 0.0, NEG).astype(np.float32), (QH, TAB))
    return c, onehot, np.ascontiguousarray(neg)


class Steps:

    def __init__(self, sem, names, base=0):
        self.sem, self.names, self.base = sem, names, base

    def after(self, name, rnd=0):
        return self.base + rnd * len(self.names) + self.names.index(name) + 1

    def end(self, rounds):
        return self.base + rounds * len(self.names)


def build(nc, A, O):
    ctx = ExitStack()
    with ctx:
        words = 53150
        arena = ctx.enter_context(nc.sbuf_tensor("arena", [P, words], F32))
        ptab = ctx.enter_context(nc.sbuf_tensor("ptab", [1, 16], I32))
        ps = ctx.enter_context(nc.psum_tensor("ps", [P, 8 * 512], F32))
        table_dram = nc.dram_tensor("bias_table", (QH, TAB), F32, kind="Internal").ap()
        h_dram = nc.dram_tensor("h_spill", (P, KC, NT), F32, kind="Internal").ap()

        def sem(name):
            return ctx.enter_context(nc.semaphore(name))

        def at(off, n, parts=P):
            assert off + n <= words
            return arena[0:parts, off:off + n]

        def bank(i, n=512, parts=P, off=0):
            return ps[0:parts, i * 512 + off:i * 512 + off + n]

        XN = 0
        MIX = XN + KC * NT
        KVQ = MIX + KC * NT
        GA = KVQ + N_KVQ * NT
        Z = GA + N_A * ROW4
        BF = Z + GH * NT
        RING = BF + QH * 512
        CST = RING + SLOTS * UNIT
        GAIN = CST + NCONST
        CW = GAIN + 47
        SMALL = CW + 12 + 48

        xn = at(XN, KC * NT).rearrange("p (k t) -> p k t", k=KC)
        mix = at(MIX, KC * NT).rearrange("p (k t) -> p k t", k=KC)
        kvq = at(KVQ, N_KVQ * NT).rearrange("p (k t) -> p k t", k=N_KVQ)
        abuf = at(GA, N_A * NT).rearrange("p (k t) -> p k t", k=N_A)
        gbuf = at(GA, N_A * ROW4).rearrange("p (k t) -> p k t", k=N_A)
        zbuf = at(Z, GH * NT).rearrange("p (k t) -> p k t", k=GH)
        slot = [at(RING + s * UNIT, UNIT).rearrange("p (k n) -> p k n", n=P) for s in range(SLOTS)]
        cst = at(CST, NCONST)
        gain = at(GAIN, 47)
        aw = at(CW, 12).rearrange("p (c k) -> p c k", k=3)
        gw = at(CW + 12, 48).rearrange("p (c k) -> p c k", k=4)
        ones, ident, tri = cst[:, C_ONE:C_ONE + P], cst[:, C_ID:C_ID + P], cst[:, C_TRI:C_TRI + P]
        su = cst[:, C_SU:C_SU + P]
        eps1, eps128, one = (cst[:, C_EPS + i:C_EPS + i + 1] for i in range(3))

        pos = [SMALL]

        def small(n, parts=P):
            pos[0] += n
            return at(pos[0] - n, n, parts)

        sm = small(160).rearrange("p (c n) -> p c n", c=5)
        gdn_in = small(8)
        soft = small(20)
        soft2 = small(20)
        gdec = small(20)
        gc = small(20)
        gl = small(20)
        egc, ekd, beg = small(20), small(20), small(20)
        biasS = small(G * KEYS, 16).rearrange("p (g k) -> p g k", g=G)
        pe_t = small(2 * CB).rearrange("p (k j) -> p k j", k=2)
        kcT = small(2 * NCP + 16 * NCS)
        vcP = small(G * P, NCP).rearrange("p (g d) -> p g d", g=G)
        pebs = small(4)
        mx, zz, rz = small(16), small(16), small(16)
        assert pos[0] <= words, pos[0]

        wsmall = at(BF, 512).rearrange("p (k n) -> p k n", k=KC)
        xa = at(BF + 512, ROW3)
        acc_a = at(BF + 512 + ROW3, ROW3 - 2)
        o = BF + 512 + 2 * ROW3 - 2
        hist_a = at(o, 64).rearrange("p (c b k) -> p c b k", c=4, b=NB)
        hist_g = at(o + 64, 288).rearrange("p (c b k) -> p c b k", c=N_A, b=NB)
        tail_a = at(o + 352, 72).rearrange("p (c n) -> p c n", c=4)
        tail_g = at(o + 424, 324).rearrange("p (c n) -> p c n", c=N_A)
        assert o + 748 <= RING
        nrm_sq = [at(Z, NT), at(Z + NT, NT)]
        rs1 = at(Z + 2 * NT, NT)

        ut = at(XN, N_A * NT).rearrange("p (k t) -> p k t", k=N_A)
        cacc = [at(XN + N_A * NT, ROW4 - 3), at(XN + N_A * NT + ROW4, ROW4 - 3)]
        names = ["decT", "kbT", "eg", "qeg", "nl", "qk", "X", "XT", "CT", "T1", "vb", "kbeg", "kd"]
        W = {n: at(GA + 512 * i, 512) for i, n in enumerate(names)}
        for i, n in enumerate(["nwT", "vnew", "S", "oT", "sq", "rs"]):
            W[n] = at(RING + 512 * i, 512)
        S_smp = at(RING + 3072, 4096).rearrange("p (b h e) -> p b h e", b=NB, h=GH)
        vm = [at(RING + 7168, 1024, NS), at(GA, 1024, NS)]
        hn_sq = [at(GA, NT), at(GA + NT, NT)]
        hn_rs = [at(GA + 2 * NT, NT), at(GA + 3 * NT, NT)]
        relb, onehot = at(KVQ, QH, 32), at(KVQ + 8, TAB, 32)
        negt, tabs = at(KVQ + 8 + TAB, TAB, QH), at(KVQ + 8 + 2 * TAB, TAB, QH)

        def heads(w, n=P, parts=P):
            return W[w][0:parts, 0:GH * n].rearrange("p (h i) -> p h i", h=GH)

        crT = at(XN, 8192).rearrange("p (k b g t) -> p k b g t", k=2, b=NB, g=G)
        flip = at(XN + 8256, P + 16)
        w2 = at(BF, 512).rearrange("p (k c d) -> p k c d", k=2, c=2)
        NCOL = G * NCP + 16 * NCS
        hid = at(BF + 512, 4 * NCOL).rearrange("p (k c n) -> p k c n", k=2, c=2)
        csq, crs = at(BF + 2048, NCOL), at(BF + 2560, NCOL)
        vcS = at(Z, 2048, NCS).rearrange("p (q d) -> p q d", d=P)

        bfull = at(BF, QH * 512).rearrange("p (h x) -> p h x", h=QH)
        PTc = at(GA, 4096, NCP).rearrange("p (h t) -> p h t", h=QH)
        VN = at(GA + 4096, 2048).rearrange("p (k g j d) -> p k g j d", k=2, g=G, j=4)
        sS = [at(RING + 512 * i, 512) for i in range(2)]
        pP = [at(RING + 1024 + 512 * i, 512) for i in range(2)]
        pT = [at(RING + 2048 + 512 * i, 512) for i in range(2)]
        o = RING + 3072
        s_S = at(o, 8 * KEYS, 16).rearrange("p (q k) -> p q k", k=KEYS)
        s_PT = at(o + 2080, 256)
        s_PN = at(o + 2336, 128, TS)
        s_VN = at(o + 2464, 1024, TS).rearrange("p (q d) -> p q d", d=P)
        grow = at(o + 3488, 768).rearrange("p (k n) -> p k n", k=3)
        ys = at(o + 4256, 256)
        qs = at(o + 4512, 256).rearrange("p (b n) -> p b n", b=NB)
        ytmp = at(o + 4768, 256)
        assert 3072 + 4768 + 256 <= SLOTS * UNIT
        kbuf = [at(XN + i * 4128, 2080).rearrange("p (b g k) -> p b g k", b=4, g=G) for i in range(2)]
        vbuf = [at(XN + i * 4128 + 2080, 2048).rearrange("p (b j g d) -> p b j g d", b=4, j=2, g=G) for i in range(2)]

        hbuf = at(KVQ, KC * NT).rearrange("p (k t) -> p k t", k=KC)
        xin = [at(Z + i * NT, NT) for i in range(2)]
        act = at(MIX, FC * NT).rearrange("p (k t) -> p k t", k=FC)
        f = MIX + FC * NT
        fx = [at(f + ROW3 * i, ROW3) for i in range(4)]
        assert f + 4 * ROW3 <= Z
        facc = [at(Z + (ROW3 - 2) * i, ROW3 - 2) for i in range(4)]
        hist = at(Z + 2240, 88 * 16).rearrange("p (u b k) -> p u b k", u=88, b=NB)
        tail = at(Z + 2240 + 1408, 88 * 18).rearrange("p (u n) -> p u n", u=88)
        fw = at(Z + 2240 + 1408 + 1584, 264).rearrange("p (u k) -> p u k", u=88)
        assert 2240 + 1408 + 1584 + 264 <= 2176 + 4096
        hin = [at(f + NT * i, NT) for i in range(2)]
        yout = [at(f + NT * (2 + i), NT) for i in range(2)]

        s_x, s_cst, s_tab = sem("x_loaded"), sem("constants_loaded"), sem("table_inputs_loaded")
        w_ready = [sem(f"weights_in_slot{s}") for s in range(SLOTS)]
        units = sem("units_multiplied")
        proj_evac = sem("proj_evacuated")
        n_sq, n_mm, n_rs, n_mul = (sem(n) for n in ("norm_squared", "norm_summed", "norm_rstd", "norm_scaled"))
        gates_mm, conv_a, a_free = sem("gates_summed"), sem("conv_a_done"), sem("conv_a_buffer_read")
        gconv_in, gconv_dve, gconv_act = sem("gdn_conv_rows_set"), sem("gdn_conv_tap"), sem("gdn_conv_silu")
        tails = sem("conv_tails_copied")
        nh_sq, nh_mm, nh_rs, nh_mul = (sem(n) for n in ("hnorm_squared", "hnorm_summed", "hnorm_rstd", "hnorm_scaled"))
        g_pe, g_act, g_dve = sem("gdn_pe"), sem("gdn_act"), sem("gdn_dve")
        st_in, gdn_stored = sem("states_loaded"), sem("gdn_states_stored")
        c_in, c_pe, c_act, c_dve = sem("cache_loaded"), sem("cmp_pe"), sem("cmp_act"), sem("cmp_dve")
        t_pe, t_dve, t_out, bs_in, bf_in = sem("table_summed"), sem("table_ready"), sem("table_stored"), sem("sample_bias_loaded"), sem("bias_loaded")
        turned_pe, turned = sem("bias_turned"), sem("bias_turned_copied")
        v_pe, v_act = sem("values_transposed"), sem("values_copied")
        ac_pe, ac_act, ac_dve = sem("acmp_pe"), sem("acmp_act"), sem("acmp_dve")
        a_s, a_m, a_e, a_p, a_t, a_pt, a_y, a_ye = (sem(n) for n in (
            "scores_ready", "max_ready", "exp_ready", "probs_ready", "probs_transposed", "probsT_copied",
            "head_summed", "head_evacuated"))
        kv_in, k_new = [sem("kv_loaded0"), sem("kv_loaded1")], sem("new_keys_copied")
        s_pe, s_act, s_dve = sem("smp_pe"), sem("smp_act"), sem("smp_dve")
        x_in, h_add = [sem("x_reloaded0"), sem("x_reloaded1")], sem("h_added")
        h_out, f_in = sem("h_stored"), sem("ffn_small_loaded")
        up_evac, up_hist, up_tail, up_conv, up_silu, up_act = (sem(n) for n in (
            "up_evacuated", "up_history", "up_tail", "up_conv", "up_silu", "up_gated"))
        h_in, dn_evac, y_out = [sem("h_reloaded0"), sem("h_reloaded1")], sem("y_ready"), [sem("y_stored0"), sem("y_stored1")]
        stored = sem("outputs_stored")
        d_chain, a_chain, p_chain = sem("dve_done"), sem("act_done"), sem("pool_done")

        LV, LVS = 7, 2
        t1, t2 = [[f"t1_{s}", f"t2_{s}"] for s in range(LV)], [[f"ct_{s}", f"x_{s}"] for s in range(LV)]
        PRE_PE, PRE_ACT, PRE_DVE = 1, 3, 5
        GP = Steps(g_pe, ["rows", "gram", "nat"] + sum(t1, []) + ["w", "v", "o", "n"], PRE_PE)
        GC = Steps(g_act, ["dec", "nat"] + [x[0] for x in t1] + ["w", "v", "o", "n"], PRE_ACT)
        GD = Steps(g_dve, ["dec", "kb", "low", "xinit"] + sum(t2, []) + ["s", "y"], PRE_DVE)
        GPS = Steps(g_pe, ["rows", "gram", "nat"] + sum(t1[:LVS], []) + ["w", "v", "vt", "o", "n", "ds0", "ds1", "ds2", "ds3"], GP.end(4))
        GCS = Steps(g_act, ["dec", "nat"] + [x[0] for x in t1[:LVS]] + ["w", "v", "vt", "o", "n"], GC.end(4))
        GDS = Steps(g_dve, ["dec", "kb", "low", "xinit"] + sum(t2[:LVS], []) + ["smul", "vm0", "y", "vm1", "add0", "vm2", "add1", "vm3", "add2", "add3"], GD.end(4))

        def steps(t):
            return (GP, GC, GD, t) if t < 4 else (GPS, GCS, GDS, 0)

        HEADS = [(ut[:, h], None, float(P), eps128) for h in range(GH)]
        HEADS += [(ut[:, GH + h], None, 1.0, eps1) for h in range(GH)]
        HEADS += [(kvq[:, k], G_K, 1.0 / P, eps1) for k in (4, 5, 8, 9)]
        HEADS += [(kvq[:, N_A + h], G_Q, 1.0, eps128) for h in range(QH)]
        GROUPS = [(mix[:, 0:16], xn[:, 0:16], G_MIX), (mix[:, 0:4], mix[:, 0:4], G_OA),
                  (mix[:, 4:12], mix[:, 4:12], G_OB), (hbuf[:, 0:16], xn[:, 0:16], G_FFN)]
        GROUP_N = [16, 4, 8, 16]
        GROUP_0 = [0, 16, 20, 28]
        ATT = [(h, i, kind) for h in range(QH) for i in range(4) for kind in range(2)]

        def halves(x):
            return x[:, 0:256], x[:, 256:NT]

        def rows3(x):
            return x[:, 2:2 + TP], x[:, 2 + TP:ROW3].rearrange("p (b n) -> p b n", n=SEG3)[:, :, 2:SEG3]

        def smp(x):
            return x[:, TP:NT].rearrange("p (b t) -> p b t", t=TS)

        block = ctx.enter_context(nc.Block())

        @block.sync
        def _(e):
            def unit(u, src, n=UNIT):
                e.dma_start(at(RING + (u % SLOTS) * UNIT, n), src).then_inc(w_ready[u % SLOTS], 16)

            for dst, name in ((cst, "consts"), (gain, "gains"), (at(CW, 60), "conv_w"), (wsmall, "w_small"),
                              (gdn_in, "gdn_ab"), (pe_t, "pe_t"), (hist_a, "hist_a"), (hist_g, "hist_g"),
                              (ptab[:], "page_table")):
                e.dma_start(dst, A[name]).then_inc(s_cst, 16)
            for q in range(4):
                e.dma_start(mix[:, 4 * q:4 * q + 4, :], A["x_t"][:, 4 * q:4 * q + 4, :]).then_inc(s_x, 16)
            for s in range(SLOTS):
                unit(s, A["w_proj"][s])
            with e.Fori(1, PROJ // SLOTS) as i:
                for s in range(SLOTS):
                    e.wait_ge(units, SLOTS * i + s - SLOTS + 1)
                    e.dma_start(at(RING + s * UNIT, UNIT), A["w_proj"][SLOTS * i + s]).then_inc(w_ready[s], 16)

            e.wait_ge(units, PROJ)
            e.dma_start(S_smp, A["state_gdn"]).then_inc(st_in, 16)

            e.wait_ge(g_dve, GDS.end(1))
            e.wait_ge(g_pe, GPS.end(1))
            e.wait_ge(g_act, GCS.end(1))
            e.dma_start(O["gdn_sp"], W["S"]).then_inc(gdn_stored, 16)
            e.dma_start(O["gdn_ss"], S_smp).then_inc(gdn_stored, 16)
            e.wait_ge(tails, 2)
            e.dma_start(O["tail_a"], tail_a).then_inc(gdn_stored, 16)
            e.dma_start(O["tail_g"], tail_g).then_inc(gdn_stored, 16)
            e.wait_ge(s_cst, 16 * 9)
            e.wait_ge(gdn_stored, 64)
            e.dma_start(w2, A["w2c"]).then_inc(c_in, 16)
            e.dma_start(flip, A["flip"]).then_inc(c_in, 16)
            pages = [e.value_load(ptab[0:1, q:q + 1], min_val=0, max_val=NPOOL - 1) for q in range(16)]
            for q in range(16):
                b, j = q // 2, q % 2
                for k in range(2):
                    e.dma_start(crT[:, k, b, :, j * PAGE:(j + 1) * PAGE], A["cache_kt"][pages[q], :, k]).then_inc(c_in, 16)
            for u in range(8):
                if u >= SLOTS:
                    e.wait_ge(units, U_CMP + u - SLOTS + 1)
                unit(u, A["w1c"][u])

            for p in range(4):
                kind, bh = p // 2, p % 2
                if p == 0:
                    e.wait_ge(c_pe, 2)
                if p >= 2:
                    e.wait_ge(s_pe, 4 + 4 * (p - 1))
                for b in range(4):
                    for j in range(2):
                        q = 2 * (4 * bh + b) + j
                        kd = kbuf[bh][:, b, :, j * PAGE:(j + 1) * PAGE]
                        vd = vbuf[bh][:, b, j]
                        if kind == 0:
                            e.dma_start(kd, A["cache_kt"][pages[q], :, 2]).then_inc(kv_in[bh], 16)
                            e.dma_start(vd, A["cache_v"][pages[q]]).then_inc(kv_in[bh], 16)
                        else:
                            e.dma_start(kd, A["win_kt"][:, 4 * bh + b, :, j * PAGE:(j + 1) * PAGE]).then_inc(kv_in[bh], 16)
                            e.dma_start(vd, A["win_v"][:, 4 * bh + b, j]).then_inc(kv_in[bh], 16)

            e.wait_ge(s_dve, 16)
            e.wait_ge(s_pe, 20)
            e.wait_ge(a_ye, QH)
            for s in range(SLOTS):
                unit(s, A["w_o"][s])
            with e.Fori(1, KC // SLOTS) as i:
                for s in range(SLOTS):
                    e.wait_ge(units, U_OUT + SLOTS * i + s - SLOTS + 1)
                    e.dma_start(at(RING + s * UNIT, UNIT), A["w_o"][SLOTS * i + s]).then_inc(w_ready[s], 16)
            with e.Fori(0, 2 * FC // SLOTS) as i:
                for s in range(SLOTS):
                    e.wait_ge(units, U_UP + SLOTS * i + s - SLOTS + 1)
                    e.dma_start(at(RING + s * UNIT, UNIT), A["w_up"][SLOTS * i + s]).then_inc(w_ready[s], 16)
            with e.Fori(0, KC) as i:
                for s in range(SLOTS):
                    e.wait_ge(units, U_DN + SLOTS * i + s - SLOTS + 1)
                    e.dma_start(at(RING + s * UNIT, DT * P), A["w_dn"][SLOTS * i + s]).then_inc(w_ready[s], 16)
            e.wait_ge(stored, 16 * 3)
            for q in range(2):
                e.wait_ge(y_out[q], 16 * (KC // 2))

        @block.tensor
        def _(e):
            def mm(out, lhsT, rhs, start=True, stop=True):
                return e.matmul(out, lhsT, rhs, start=start, stop=stop, skip_group_check=True)

            def tr(out, in_):
                n = in_.shape[0]
                return e.transpose(out, in_, ident[0:n, 0:n])

            def unit(banks, s, src, k0=0, n=KC, ktot=KC):
                for k in range(n):
                    lo, hi = halves(src[:, k0 + k])
                    mm(bank(banks, 256), slot[s][:, k], lo, k0 + k == 0, k0 + k == ktot - 1)
                    last = mm(bank(banks + 1, NT - 256), slot[s][:, k], hi, k0 + k == 0, k0 + k == ktot - 1)
                last.then_inc(units, 1)

            def sum_squares(sq, first, last, banks):
                lo, hi = halves(sq)
                mm(bank(banks, 256), ones, lo, first, last)
                return mm(bank(banks + 1, NT - 256), ones, hi, first, last)

            def group_norm(g):
                for k in range(GROUP_N[g]):
                    e.wait_ge(n_sq, GROUP_0[g] + k + 1)
                    sum_squares(nrm_sq[k % 2], k == 0, k == GROUP_N[g] - 1, 4).then_inc(n_mm, 1)

            e.wait_ge(s_tab, 48)
            mm(bank(6, 320, QH), relb, onehot[:, 0:320])
            mm(bank(7, 320, QH), relb, onehot[:, 320:TAB]).then_inc(t_pe, 1)

            e.wait_ge(s_cst, 16 * 9)
            group_norm(0)

            e.wait_ge(n_mul, 16)
            for s in range(SLOTS):
                e.wait_ge(w_ready[s], 16)
                if s >= 2:
                    e.wait_ge(proj_evac, s - 1)
                unit(2 * (s % 2), s, xn)
            with e.Fori(1, PROJ // SLOTS) as i:
                for s in range(SLOTS):
                    e.wait_ge(w_ready[s], 16 * i + 16)
                    e.wait_ge(proj_evac, SLOTS * i + s - 1)
                    unit(2 * (s % 2), s, xn)
            e.wait_ge(t_dve, 1)
            for t in range(5):
                n = P if t < 4 else NS
                for k in range(KC):
                    last = mm(bank(6, 32, n, 32 * t), xn[:, k, P * t:P * t + n], wsmall[:, k], k == 0, k == KC - 1)
            last.then_inc(gates_mm, 1)

            for t in range(len(HEADS)):
                e.wait_ge(nh_sq, t + 1)
                if t >= 2:
                    e.wait_ge(nh_rs, t - 1)
                else:
                    e.wait_ge(proj_evac, PROJ)
                sum_squares(hn_sq[t % 2], True, True, 2 * (t % 2)).then_inc(nh_mm, 1)

            e.wait_ge(g_dve, 3)
            mm(bank(7, 16, P, 0), tri, gdec[:, 0:16])
            mm(bank(7, 4, NS, 16), cst[0:NS, C_TRIB:C_TRIB + NS], gdec[0:NS, 16:20])
            mm(bank(7, 16, P, 32), ones, gdec[:, 0:16])
            mm(bank(7, 4, NS, 48), cst[0:NS, C_GRP:C_GRP + NS], gdec[0:NS, 16:20]).then_inc(g_pe, 1)

            def gdn_tile(t):
                PE_, AC, DV, r = steps(t)
                sample = t == 4
                n = NS if sample else P
                c0 = P * t

                def out(b, h, cols, parts=P):
                    return bank(b, cols, parts, h * cols)

                if t == 0:
                    e.wait_ge(g_dve, PRE_DVE)
                    e.wait_ge(nh_mul, len(HEADS))
                else:
                    e.wait_ge(g_act, GC.after("n", t - 1))
                for h in range(GH):
                    c = 4 * t + h
                    mm(out(0, h, n), gdec[0:n, c:c + 1].broadcast_to([n, P]), cst[0:n, C_TRIB:C_TRIB + n] if sample else tri)
                    last = mm(out(1, h, n), sm[0:n, t, 28 + h:29 + h].broadcast_to([n, P]), ident[0:n, 0:n])
                last.then_inc(g_pe, 1)
                e.wait_ge(g_dve, DV.after("kb", r))
                for h in range(GH):
                    kh = ut[:, GH + h, c0:c0 + n]
                    mm(out(2, h, n, n), kh, heads("kbT", n)[:, h])
                    last = mm(out(3, h, n, n), kh, ut[:, h, c0:c0 + n])
                last.then_inc(g_pe, 1)
                for h in range(GH):
                    tr(out(4, h, P, n), ut[:, GH + h, c0:c0 + n])
                    last = tr(out(5, h, P, n), ut[:, 2 * GH + h, c0:c0 + n])
                last.then_inc(g_pe, 1)
                lv = LVS if sample else LV
                for s in range(lv):
                    e.wait_ge(g_dve, DV.after(f"ct_{s}", r))
                    for h in range(GH):
                        last = mm(out(0, h, n, n), heads("CT", n, n)[:, h], heads("X", n, n)[:, h])
                    last.then_inc(g_pe, 1)
                    e.wait_ge(g_act, AC.after(f"t1_{s}", r))
                    for h in range(GH):
                        mm(out(1, h, n, n), heads("XT", n, n)[:, h], heads("T1", n, n)[:, h])
                    for h in range(GH):
                        last = mm(out(2, h, n, n), heads("T1", n, n)[:, h], heads("XT", n, n)[:, h])
                    last.then_inc(g_pe, 1)
                e.wait_ge(g_dve, DV.after(f"x_{lv - 1}", r))
                e.wait_ge(g_act, AC.after("nat", r))
                for h in range(GH):
                    last = mm(out(3, h, n), heads("kbeg", P, n)[:, h], heads("XT", n, n)[:, h])
                last.then_inc(g_pe, 1)
                e.wait_ge(g_act, AC.after("w", r))
                if not sample:
                    if t > 0:
                        e.wait_ge(g_dve, DV.after("s", r - 1))
                    for h in range(GH):
                        mm(out(4, h, P), heads("XT")[:, h], heads("vb")[:, h], True, False)
                        last = mm(out(4, h, P), heads("nwT")[:, h], heads("S")[:, h], False, True)
                    last.then_inc(g_pe, 1)
                    e.wait_ge(g_act, AC.after("v", r))
                    for h in range(GH):
                        mm(out(5, h, P), heads("S")[:, h], heads("qeg")[:, h], True, False)
                        mm(out(5, h, P), heads("vnew")[:, h], heads("qk")[:, h], False, True)
                    for h in range(GH):
                        last = mm(out(6, h, P), heads("kd")[:, h], heads("vnew")[:, h])
                    last.then_inc(g_pe, 1)
                else:
                    e.wait_ge(st_in, 16)
                    for h in range(GH):
                        mm(out(4, h, n), heads("vb", P, n)[:, h], heads("XT", n, n)[:, h], True, False)
                        for b in range(NB):
                            last = mm(bank(4, TS, P, h * n + TS * b), S_smp[:, b, h], heads("nwT", n)[:, h, TS * b:TS * b + TS], False, b == NB - 1)
                    last.then_inc(g_pe, 1)
                    e.wait_ge(g_act, AC.after("v", r))
                    for h in range(GH):
                        last = tr(out(5, h, P, n), heads("T1", n)[:, h])
                    last.then_inc(g_pe, 1)
                    e.wait_ge(g_act, AC.after("vt", r))
                    for h in range(GH):
                        mm(out(6, h, n), heads("vnew", P, n)[:, h], heads("qk", n, n)[:, h], True, False)
                        for b in range(NB):
                            last = mm(bank(6, TS, P, h * n + TS * b), S_smp[:, b, h], heads("qeg", n)[:, h, TS * b:TS * b + TS], False, b == NB - 1)
                    last.then_inc(g_pe, 1)
                e.wait_ge(g_act, AC.after("o", r))
                mm(bank(7, GH * n), ones, W["sq"][:, 0:GH * n]).then_inc(g_pe, 1)
                if sample:
                    for h in range(GH):
                        e.wait_ge(g_dve, DV.after(f"vm{h}", r))
                        if h >= 2:
                            e.wait_ge(g_dve, DV.after(f"add{h - 2}", r))
                        for q in range(2):
                            last = mm(bank(2 * (h % 2) + q), heads("kd", P, n)[:, h], vm[h % 2][:, 512 * q:512 * q + 512])
                        last.then_inc(g_pe, 1)

            for t in range(5):
                gdn_tile(t)

            e.wait_ge(g_dve, GDS.end(1))
            e.wait_ge(c_in, 16 * 34)
            for k in range(2):
                for hc in range(2):
                    bk = 2 * k + hc
                    for jh in range(2):
                        u = 4 * k + 2 * hc + jh
                        e.wait_ge(w_ready[u % SLOTS], 16 * ((U_CMP + u) // SLOTS + 1))
                        for jj in range(16):
                            j = 16 * jh + jj
                            w = slot[u % SLOTS][:, jj]
                            mm(bank(bk, G * NCP), w, kvq[:, 2 * k:2 * k + 2, j:j + CS * (NCP - 1) + 1:CS], j == 0, j == CB - 1)
                            mm(bank(bk, 16 * NCS, P, G * NCP), w,
                               crT[:, k].rearrange("p b g t -> p (b g) t")[:, :, j:j + CS * (NCS - 1) + 1:CS], False, j == CB - 1)
                            last = mm(bank(bk, 1, P, NCOL), w, pe_t[:, k, j:j + 1], False, j == CB - 1)
                        last.then_inc(units, 1)
                e.wait_ge(units, U_CMP + 4 * k + 4)
                e.sem_inc(c_pe, 1)
            e.wait_ge(c_act, 1)
            for hc in range(2):
                last = mm(bank(4, NCOL), w2[:, 0, hc], hid[:, 0, hc], hc == 0, hc == 1)
            last.then_inc(c_pe, 1)
            e.wait_ge(c_act, 3)
            mm(bank(5, NCOL), ones, csq).then_inc(c_pe, 1)
            for g in range(G):
                for hc in range(2):
                    mm(bank(6, P, NCP, P * g), hid[:, 1, hc, NCP * g:NCP * (g + 1)], w2[:, 1, hc], hc == 0, hc == 1)
            for q in range(16):
                for hc in range(2):
                    c = G * NCP + NCS * q
                    last = mm(bank(q // 4, P, NCS, P * (q % 4)), hid[:, 1, hc, c:c + NCS], w2[:, 1, hc], hc == 0, hc == 1)
            last.then_inc(c_pe, 1)

            e.wait_ge(c_act, 5)
            for kind in range(2):
                for g in range(G):
                    for j in range(4):
                        last = tr(bank(2 * kind + g, P, P, P * j), kvq[:, 6 + 4 * kind + g, P * j:P * j + P])
            last.then_inc(v_pe, 1)

            e.wait_ge(v_act, 1)
            e.wait_ge(bf_in, 16)
            for h in range(QH):
                last = mm(bank(h), flip[:, 0:P], bfull[:, h])
            last.then_inc(turned_pe, 1)
            e.wait_ge(turned, 1)
            e.wait_ge(bs_in, 16 * REP)
            for g in range(G):
                last = mm(bank(g, KEYS, 16), flip[0:16, P:P + 16], biasS[:, g])
            last.then_inc(turned_pe, 1)

            e.wait_ge(c_dve, 1)
            e.wait_ge(turned, 2)
            for i in range(4):
                n = 7 + 8 * i
                if i > 0:
                    e.wait_ge(ac_dve, 2 * i)
                for h in range(QH):
                    last = mm(bank(4, n, P, NCP * h), kvq[:, N_A + h, P * i:P * i + P], kcT[:, NCP * (h // REP):NCP * (h // REP) + n])
                last.then_inc(ac_pe, 1)
                e.wait_ge(ac_dve, 2 * i + 2)
                if i > 0:
                    e.wait_ge(ac_act, 2 * i)
                for h in range(QH):
                    last = tr(bank(5 + h // 4, P, n, P * (h % 4)), sS[0][:, 0:QH * NCP].rearrange("p (h c) -> p h c", h=QH)[:, h, 0:n])
                last.then_inc(ac_pe, 1)
            e.wait_ge(ac_act, 8)

            def score(s):
                h, i, kind = ATT[s]
                if s >= 2:
                    e.wait_ge(a_m, s - 1)
                mm(bank(4 + s % 2, P * (i + 1)), kvq[:, N_A + h, P * i:P * i + P],
                   kvq[:, 4 + 4 * kind + h // REP, 0:P * (i + 1)]).then_inc(a_s, 1)

            def turn(s):
                h, i, kind = ATT[s]
                e.wait_ge(a_p, s + 1)
                if s >= 2:
                    e.wait_ge(a_pt, s - 1)
                for j in range(i + 1):
                    last = tr(bank(2 + s % 2, P, P, P * j), pP[s % 2][:, P * j:P * j + P])
                last.then_inc(a_t, 1)

            def values(s):
                h, i, kind = ATT[s]
                y = bank(h % 2, P, P, P * i)
                if kind == 0:
                    if i == 0 and h >= 2:
                        e.wait_ge(a_ye, h - 1)
                    n = 7 + 8 * i
                    mm(y, vcP[0:n, h // REP], PTc[0:n, h, P * i:P * i + P], True, False)
                e.wait_ge(a_pt, s + 1)
                for j in range(i + 1):
                    last = mm(y, VN[:, kind, h // REP, j], pT[s % 2][:, P * j:P * j + P], False, kind == 1 and j == i)
                last.then_inc(a_y, 1)

            for s in range(len(ATT) + 2):
                if s < len(ATT):
                    score(s)
                if 1 <= s <= len(ATT):
                    turn(s - 1)
                if s >= 2:
                    values(s - 2)

            for kind in range(3):
                for h in range(QH):
                    last = mm(bank(6 + kind // 2, NS, P, 256 * (kind % 2) + NS * h),
                              sm[0:NS, 4, QH * kind + h:QH * kind + h + 1].broadcast_to([NS, P]), ident[0:NS, 0:NS])
            last.then_inc(s_pe, 1)
            e.wait_ge(k_new, 1)
            e.wait_ge(a_ye, QH)
            for q in range(16):
                last = mm(bank(0, NCS, 16, NCS * q), qs[:, q // G, 16 * (q % G):16 * (q % G) + 16],
                          kcT[:, G * NCP + NCS * q:G * NCP + NCS * (q + 1)])
            last.then_inc(s_pe, 1)
            e.wait_ge(s_dve, 2)
            for q in range(16):
                last = tr(bank(1, 16, NCS, 16 * q), s_S.rearrange("p q k -> p (q k)")[:, NCS * q:NCS * q + NCS])
            last.then_inc(s_pe, 1)
            e.wait_ge(s_act, 3)
            for q in range(16):
                last = mm(bank(2, 16, P, 16 * q), vcS[:, q], s_PT[0:NCS, 16 * q:16 * q + 16])
            last.then_inc(s_pe, 1)
            for p in range(4):
                kind, bh = p // 2, p % 2
                e.wait_ge(s_dve, 3 * p + 3)
                e.wait_ge(k_new, p + 2)
                e.wait_ge(kv_in[bh], 16 * 16 * (kind + 1))
                for q in range(8):
                    last = mm(bank(q, KEYS, 16), qs[:, 4 * bh + q // G, 16 * (q % G):16 * (q % G) + 16], kbuf[bh][:, q // G, q % G])
                last.then_inc(s_pe, 1)
                e.wait_ge(s_dve, 3 * p + 4)
                for q in range(8):
                    c = TP + TS * (4 * bh + q // G)
                    last = tr(bank(2 + q // 4, P, TS, P * (q % 4)), kvq[:, 6 + 4 * kind + q % G, c:c + TS])
                last.then_inc(s_pe, 1)
                e.wait_ge(s_dve, 3 * p + 5)
                for q in range(8):
                    for j in range(2):
                        tr(bank(0, 16, P, 32 * q + 16 * j), s_S[:, q, P * j:P * j + P])
                    last = tr(bank(1, 16, TS, 16 * q), s_S[:, q, PAST:KEYS])
                last.then_inc(s_pe, 1)
                e.wait_ge(s_act, 5 + 2 * p)
                for q in range(8):
                    for j in range(2):
                        mm(bank(4, 16, P, 16 * q), vbuf[bh][:, q // G, j, q % G], s_PT[:, 32 * q + 16 * j:32 * q + 16 * j + 16], j == 0, False)
                    last = mm(bank(4, 16, P, 16 * q), s_VN[:, q], s_PN[:, 16 * q:16 * q + 16], False, True)
                last.then_inc(s_pe, 1)

            e.wait_ge(s_dve, 16)
            group_norm(1)
            group_norm(2)

            e.wait_ge(n_mul, GROUP_0[3])
            def out_unit(i, s, first):
                e.wait_ge(w_ready[s], 16 * i + 16 * (U_OUT // SLOTS + 1))
                if not first or s >= 2:
                    e.wait_ge(h_add, SLOTS * i + s - 1)
                unit(2 * (s % 2), s, mix)
            for s in range(SLOTS):
                out_unit(0, s, True)
            with e.Fori(1, KC // SLOTS) as i:
                for s in range(SLOTS):
                    out_unit(i, s, False)
            group_norm(3)

            e.wait_ge(n_mul, GROUP_0[3] + 16)
            def up_unit(i, s, first):
                e.wait_ge(w_ready[s], 16 * i + 16 * (U_UP // SLOTS + 1))
                if not first or s >= 2:
                    e.wait_ge(up_evac, SLOTS * i + s - 1)
                unit(2 * (s % 2), s, xn)
            for s in range(SLOTS):
                up_unit(0, s, True)
            with e.Fori(1, 2 * FC // SLOTS) as i:
                for s in range(SLOTS):
                    up_unit(i, s, False)

            e.wait_ge(up_act, FC)
            e.wait_ge(up_evac, 2 * FC)
            def down(i, first):
                for d in range(2):
                    if not first:
                        e.wait_ge(dn_evac, 2 * i + d - 1)
                    for q in range(DU):
                        e.wait_ge(w_ready[q], 32 * i + 16 * (U_DN // SLOTS + d + 1))
                        unit(2 * d, q, act, DT * q, DT, FC)
            down(0, True)
            with e.Fori(1, KC // 2) as i:
                down(i, False)

        @block.scalar
        def _(e):
            n_chain = [0]

            def link(ins):
                n_chain[0] += 1
                ins.then_inc(a_chain, 1)
                e.wait_ge(a_chain, n_chain[0])

            def rstd(out, sums, scale, eps):
                link(e.activation(out, sums, ACT.Ln, bias=eps, scale=scale))
                return e.activation(out, out, ACT.Exp, scale=-0.5)

            def two_banks(b, n=NT):
                return bank(b, 256), bank(b + 1, NT - 256)

            def rstd_row(out, banks, scale, eps):
                lo, hi = halves(out)
                a, b = two_banks(banks)
                e.activation(lo, a, ACT.Ln, bias=eps, scale=scale)
                link(e.activation(hi, b, ACT.Ln, bias=eps, scale=scale))
                return e.activation(out, out, ACT.Exp, scale=-0.5)

            def group_norm(g):
                src = GROUPS[g][0]
                for k in range(GROUP_N[g]):
                    c = GROUP_0[g] + k
                    if k >= 2:
                        e.wait_ge(n_mm, c - 1)
                    e.activation(nrm_sq[k % 2], src[:, k], ACT.Square).then_inc(n_sq, 1)
                e.wait_ge(n_mm, GROUP_0[g] + GROUP_N[g])
                if g > 0:
                    e.wait_ge(n_mul, GROUP_0[g])
                rstd_row(rs1, 4, 1.0 / (GROUP_N[g] * P), eps1).then_inc(n_rs, 1)

            e.dma_start(relb, A["rel_bias"]).then_inc(s_tab, 16)
            e.dma_start(onehot, A["onehot"]).then_inc(s_tab, 16)
            e.dma_start(negt, A["neg"]).then_inc(s_tab, 16)
            e.wait_ge(t_dve, 1)
            e.dma_start(table_dram, tabs).then_inc(t_out, 16)
            e.dma_start(O["win_old"], A["cache_win"]).then_inc(stored, 16)
            e.wait_ge(t_out, 16)
            for r in range(REP):
                src = bass.AP(table_dram.tensor, r * TAB + PAST - TS, [[1, TS], [REP * TAB, G], [1, KEYS]])
                e.dma_start(biasS[TS * r:TS * r + TS], src).then_inc(bs_in, 16)

            e.wait_ge(s_cst, 16 * 9)
            e.wait_ge(s_x, 64)
            group_norm(0)

            def copy_chunk(banks, dst, func=ACT.Copy):
                lo, hi = halves(dst)
                a, b = two_banks(banks)
                e.activation(lo, a, func)
                return e.activation(hi, b, func)

            for c in range(N_A):
                e.wait_ge(units, c + 1)
                copy_chunk(2 * (c % 2), abuf[:, c]).then_inc(proj_evac, 1)
            with e.Fori(0, N_KVQ // 2) as i:
                for s in range(2):
                    e.wait_ge(units, 2 * i + s + N_A + 1)
                    lo, hi = halves(at(KVQ, N_KVQ * NT).rearrange("p (k t) -> p k t", k=N_KVQ)[:, 2 * i + s])
                    e.activation(lo, bank(2 * s, 256), ACT.Copy)
                    e.activation(hi, bank(2 * s + 1, NT - 256), ACT.Copy).then_inc(proj_evac, 1)
            e.wait_ge(a_free, 1)
            for c in range(N_A):
                e.wait_ge(units, N_A + N_KVQ + c + 1)
                a, b = two_banks(2 * (c % 2))
                e.activation(gbuf[:, c, 3:3 + 256], a, ACT.Copy)
                e.activation(gbuf[:, c, 3 + 256:3 + TP], b[:, 0:256], ACT.Copy)
                e.activation(gbuf[:, c, 3 + TP:ROW4].rearrange("p (b n) -> p b n", n=SEG4)[:, :, 3:SEG4],
                             b[:, 256:NT - 256].rearrange("p (b t) -> p b t", t=TS), ACT.Copy).then_inc(proj_evac, 1)
            e.wait_ge(n_mul, 16)
            for c in range(GH):
                e.wait_ge(units, PROJ - GH + c + 1)
                copy_chunk(2 * (c % 2), zbuf[:, c], ACT.Silu).then_inc(proj_evac, 1)

            def silu_rows(i, s):
                e.wait_ge(gconv_dve, 8 * i + 4 * s + 4)
                c = ut[:, 2 * i + s]
                e.activation(c[:, 0:TP], cacc[s][:, 0:TP], ACT.Silu)
                e.activation(smp(c), at(XN + N_A * NT + s * ROW4 + TP + 3, NB * SEG4).rearrange("p (b n) -> p b n", n=SEG4)[:, :, 0:TS],
                             ACT.Silu).then_inc(gconv_act, 1)
            with e.Fori(0, N_A // 2) as i:
                silu_rows(i, 0)
                silu_rows(i, 1)

            def head_square(t):
                if t >= 2:
                    e.wait_ge(nh_mm, t - 1)
                e.activation(hn_sq[t % 2], HEADS[t][0], ACT.Square).then_inc(nh_sq, 1)
            e.wait_ge(gconv_act, N_A)
            e.wait_ge(proj_evac, PROJ)
            e.wait_ge(tails, 2)
            head_square(0)
            for t in range(len(HEADS)):
                if t + 1 < len(HEADS):
                    head_square(t + 1)
                e.wait_ge(nh_mm, t + 1)
                if t >= 2:
                    e.wait_ge(nh_mul, t - 1)
                rstd_row(hn_rs[t % 2], 2 * (t % 2), HEADS[t][2], HEADS[t][3]).then_inc(nh_rs, 1)
            e.wait_ge(nh_mul, len(HEADS))
            e.dma_start(O["kv_t"], kvq[:, 0:N_A]).then_inc(stored, 16)

            e.wait_ge(g_dve, 1)
            e.activation(sm[:, :, 0:24], sm[:, :, 0:24], ACT.Sigmoid)
            link(e.activation(sm[:, :, 28:32], sm[:, :, 28:32], ACT.Sigmoid))
            e.sem_inc(g_act, 1)
            e.wait_ge(g_dve, 2)
            link(e.activation(soft2, soft2, ACT.Exp))
            e.activation(soft2, soft2, ACT.Ln, bias=one)
            e.activation(gdn_in[:, 0:4], gdn_in[:, 0:4], ACT.Exp).then_inc(g_act, 1)
            e.wait_ge(g_dve, 4)
            e.activation(egc, gc, ACT.Exp)
            e.activation(ekd, ekd, ACT.Exp).then_inc(g_act, 1)

            def gdn_tile(t):
                PE_, AC, DV, r = steps(t)
                n = NS if t == 4 else P
                w = GH * n
                e.wait_ge(g_dve, DV.after("dec", r))
                e.activation(W["decT"][0:n, 0:w], W["decT"][0:n, 0:w], ACT.Exp)
                e.activation(W["eg"][:, 0:w], bank(0, w), ACT.Exp).then_inc(g_act, 1)
                e.wait_ge(g_pe, PE_.after("nat", r))
                for h in range(GH):
                    c = 4 * t + h
                    e.activation(heads("vb", P, n)[:, h], bank(5, P, n, P * h), ACT.Copy, scale=sm[0:n, t, 28 + h:29 + h])
                    e.activation(heads("kbeg", P, n)[:, h], bank(4, P, n, P * h), ACT.Copy, scale=beg[0:n, c:c + 1])
                    last = e.activation(heads("kd", P, n)[:, h], bank(4, P, n, P * h), ACT.Copy, scale=ekd[0:n, c:c + 1])
                last.then_inc(g_act, 1)
                for s in range(LVS if t == 4 else LV):
                    e.wait_ge(g_pe, PE_.after(f"t1_{s}", r))
                    e.activation(W["T1"][0:n, 0:w], bank(0, w, n), ACT.Copy).then_inc(g_act, 1)
                e.wait_ge(g_pe, PE_.after("w", r))
                e.activation(W["nwT"][:, 0:w], bank(3, w), ACT.Copy, scale=-1.0).then_inc(g_act, 1)
                e.wait_ge(g_pe, PE_.after("v", r))
                if t < 4:
                    e.activation(W["vnew"], bank(4), ACT.Copy).then_inc(g_act, 1)
                else:
                    e.activation(W["T1"][:, 0:w], bank(4, w), ACT.Copy).then_inc(g_act, 1)
                    e.wait_ge(g_pe, PE_.after("vt", r))
                    e.activation(W["vnew"][0:n], bank(5, 512, n), ACT.Copy).then_inc(g_act, 1)
                e.wait_ge(g_pe, PE_.after("o", r))
                ob = bank(5 if t < 4 else 6, w)
                e.activation(W["oT"][:, 0:w], ob, ACT.Copy)
                e.activation(W["sq"][:, 0:w], ob, ACT.Square).then_inc(g_act, 1)
                e.wait_ge(g_pe, PE_.after("n", r))
                rstd(W["rs"][:, 0:w], bank(7, w), 1.0 / P, eps1).then_inc(g_act, 1)

            for t in range(5):
                gdn_tile(t)

            for k in range(2):
                e.wait_ge(c_pe, k + 1)
                for hc in range(2):
                    link(e.activation(pebs[:, 2 * k + hc:2 * k + hc + 1], bank(2 * k + hc, 1, P, NCOL), ACT.Copy))
                    last = e.activation(hid[:, k, hc], bank(2 * k + hc, NCOL), ACT.Gelu_apprx_tanh, bias=pebs[:, 2 * k + hc:2 * k + hc + 1])
                last.then_inc(c_act, 1)
            e.wait_ge(c_pe, 3)
            e.activation(kcT, bank(4, NCOL), ACT.Copy)
            e.activation(csq, bank(4, NCOL), ACT.Square).then_inc(c_act, 1)
            e.wait_ge(c_pe, 4)
            rstd(crs, bank(5, NCOL), 1.0 / P, eps1).then_inc(c_act, 1)
            e.wait_ge(c_pe, 5)
            for g in range(G):
                e.activation(vcP[:, g], bank(6, P, NCP, P * g), ACT.Copy)
            e.activation(vcS.rearrange("p q d -> p (q d)"), ps[0:NCS, 0:2048], ACT.Copy).then_inc(c_act, 1)

            e.wait_ge(c_dve, 1)
            e.wait_ge(c_act, 5)
            e.wait_ge(gdn_stored, 64)
            src = bass.AP(table_dram.tensor, 0, [[1, P], [TAB, QH], [1, 512]])
            e.dma_start(bfull, src).then_inc(bf_in, 16)
            e.wait_ge(v_pe, 1)
            for b in range(4):
                last = e.activation(VN[:, b // 2, b % 2].rearrange("p j d -> p (j d)"), bank(b), ACT.Copy)
            last.then_inc(v_act, 1)
            e.wait_ge(turned_pe, 1)
            for h in range(QH):
                last = e.activation(bfull[:, h], bank(h), ACT.Copy)
            last.then_inc(turned, 1)
            e.wait_ge(turned_pe, 2)
            for g in range(G):
                last = e.activation(biasS[:, g], bank(g, KEYS, 16), ACT.Copy)
            last.then_inc(turned, 1)

            sC = sS[0][:, 0:QH * NCP].rearrange("p (h c) -> p h c", h=QH)
            for i in range(4):
                n = 7 + 8 * i
                e.wait_ge(ac_dve, 2 * i + 1)
                e.activation(sC[:, :, 0:n], sC[:, :, 0:n], ACT.Exp).then_inc(ac_act, 1)
                e.wait_ge(ac_pe, 2 * i + 2)
                for q in range(2):
                    last = e.activation(PTc[0:n, 4 * q:4 * q + 4, P * i:P * i + P],
                                        bank(5 + q, 512, n).rearrange("p (h t) -> p h t", h=4), ACT.Copy)
                last.then_inc(ac_act, 1)

            def exps(s):
                n = P * (ATT[s][1] + 1)
                e.wait_ge(a_m, s + 1)
                if s >= 2:
                    e.wait_ge(a_t, s - 1)
                e.activation(pP[s % 2][:, 0:n], sS[s % 2][:, 0:n], ACT.Exp, bias=mx[:, s % 2:s % 2 + 1],
                             accum_out=zz[:, s % 2:s % 2 + 1]).then_inc(a_e, 1)

            def copies(s):
                h, i, kind = ATT[s]
                n = P * (i + 1)
                e.wait_ge(a_t, s + 1)
                if s >= 2:
                    e.wait_ge(a_y, s - 1)
                e.activation(pT[s % 2][:, 0:n], bank(2 + s % 2, n), ACT.Copy).then_inc(a_pt, 1)

            def head_out(h):
                e.wait_ge(a_y, 8 * h + 8)
                e.activation(mix[:, 4 + h, 0:TP], bank(h % 2), ACT.Copy).then_inc(a_ye, 1)

            for s in range(len(ATT) + 2):
                if s < len(ATT):
                    exps(s)
                if 1 <= s <= len(ATT):
                    copies(s - 1)
                if s >= 3 and (s - 3) % 8 == 7:
                    head_out((s - 3) // 8)
            head_out(QH - 1)

            e.wait_ge(s_pe, 1)
            for kind in range(3):
                link(e.activation(grow[:, kind].rearrange("p (b h t) -> p b h t", b=NB, h=QH),
                                  bank(6 + kind // 2, 256, P, 256 * (kind % 2)).rearrange("p (h b t) -> p b h t", h=QH, b=NB), ACT.Copy))
            e.sem_inc(s_act, 1)
            sC2 = s_S.rearrange("p q k -> p (q k)")[:, 0:16 * NCS]
            e.wait_ge(s_dve, 1)
            e.activation(sC2, sC2, ACT.Exp).then_inc(s_act, 1)
            e.wait_ge(s_pe, 3)
            e.activation(s_PT[0:NCS, 0:256], bank(1, 256, NCS), ACT.Copy).then_inc(s_act, 1)
            for p in range(4):
                e.wait_ge(s_dve, 3 * p + 4)
                e.activation(s_S, s_S, ACT.Exp).then_inc(s_act, 1)
                e.wait_ge(s_pe, 4 * p + 7)
                e.activation(s_PT, bank(0, 256), ACT.Copy)
                e.activation(s_PN, bank(1, P, TS), ACT.Copy)
                e.activation(s_VN.rearrange("p q d -> p (q d)"), ps[0:TS, 1024:2048], ACT.Copy).then_inc(s_act, 1)

            group_norm(1)
            group_norm(2)

            e.wait_ge(n_mul, GROUP_0[3])
            for c in range(2):
                e.dma_start(xin[c], A["x_t"][:, c]).then_inc(x_in[c], 16)
            for dst, name in ((hist, "hist_f"), (fw, "ffn_w")):
                e.dma_start(dst, A[name]).then_inc(f_in, 16)
            with e.Fori(1, KC // 2) as i:
                for c in range(2):
                    e.wait_ge(h_add, 2 * i + c - 1)
                    e.dma_start(xin[c], A["x_t"][:, 2 * i + c]).then_inc(x_in[c], 16)
            e.wait_ge(h_add, KC)
            e.dma_start(h_dram, hbuf).then_inc(h_out, 16)
            group_norm(3)

            e.wait_ge(n_mul, GROUP_0[3] + 16)
            def up(i, first):
                for q in range(SLOTS):
                    u = SLOTS * i + q
                    e.wait_ge(units, u + (U_UP + 1))
                    if not first:
                        e.wait_ge(up_conv, 3 * u - 9)
                        e.wait_ge(up_tail, u - 3)
                    prompt, sample = rows3(fx[q])
                    a, b = two_banks(2 * (q % 2))
                    e.activation(prompt[:, 0:256], a, ACT.Copy)
                    e.activation(prompt[:, 256:TP], b[:, 0:256], ACT.Copy)
                    e.activation(sample, b[:, 256:NT - 256].rearrange("p (b t) -> p b t", t=TS), ACT.Copy).then_inc(up_evac, 1)
                    if q % 2:
                        e.wait_ge(up_conv, 3 * u)
                        e.activation(facc[q - 1], facc[q - 1], ACT.Silu).then_inc(up_silu, 1)
            up(0, True)
            with e.Fori(1, FC // 2) as i:
                up(i, False)
            e.wait_ge(up_tail, 2 * FC)
            e.dma_start(O["tail_f"], tail).then_inc(stored, 16)

            e.wait_ge(h_out, 16)
            e.wait_ge(up_act, FC)
            for c in range(2):
                e.dma_start(hin[c], h_dram[:, c]).then_inc(h_in[c], 16)
            with e.Fori(0, KC // 2 - 1) as i:
                for c in range(2):
                    e.wait_ge(dn_evac, 2 * i + c + 1)
                    e.dma_start(O["y_t"][:, 2 * i + c], yout[c]).then_inc(y_out[c], 16)
                    e.dma_start(hin[c], h_dram[:, 2 * i + c + 2]).then_inc(h_in[c], 16)
            for c in range(2):
                e.wait_ge(dn_evac, KC - 1 + c)
                e.dma_start(O["y_t"][:, KC - 2 + c], yout[c]).then_inc(y_out[c], 16)

        @block.vector
        def _(e):
            n_chain = [0]

            def link(ins):
                n_chain[0] += 1
                ins.then_inc(d_chain, 1)
                e.wait_ge(d_chain, n_chain[0])

            def group_norm(g):
                src, dst, col = GROUPS[g]
                e.wait_ge(n_rs, g + 1)
                for k in range(GROUP_N[g]):
                    e.scalar_tensor_tensor(out=dst[:, k], in0=src[:, k], scalar=gain[:, col + k:col + k + 1], in1=rs1,
                                           op0=ALU.mult, op1=ALU.mult).then_inc(n_mul, 1)

            e.memset(xa[:, 0:2], 0.0)
            e.memset(gc, 0.0)
            e.memset(gl, 0.0)
            link(e.memset(sm.rearrange("p c n -> p (c n)"), 0.0))
            e.wait_ge(t_pe, 1)
            e.wait_ge(s_tab, 48)
            e.tensor_tensor(tabs[:, 0:320], bank(6, 320, QH), negt[:, 0:320], ALU.add)
            e.tensor_tensor(tabs[:, 320:TAB], bank(7, 320, QH), negt[:, 320:TAB], ALU.add).then_inc(t_dve, 1)

            e.wait_ge(s_cst, 16 * 9)
            e.wait_ge(s_x, 64)
            group_norm(0)

            e.wait_ge(n_mul, 16)
            up_, us_ = rows3(xa)
            for j in range(4):
                e.wait_ge(proj_evac, 3 * j + 3)
                cc, hh, bb = abuf[:, 3 * j], abuf[:, 3 * j + 1], abuf[:, 3 * j + 2]
                e.tensor_copy(xa[:, 2 + TP:ROW3].rearrange("p (b n) -> p b n", n=SEG3)[:, :, 0:2], hist_a[:, j])
                e.tensor_tensor(up_, cc[:, 0:TP], hh[:, 0:TP], ALU.mult)
                link(e.tensor_tensor(us_, smp(cc), smp(hh), ALU.mult))
                e.tensor_copy(tail_a[:, j, 0:2], xa[:, TP:TP + 2])
                e.tensor_copy(tail_a[:, j, 2:18].rearrange("p (b k) -> p b k", k=2), us_[:, :, 2:4])
                link(e.tensor_scalar(acc_a, xa[:, 0:ROW3 - 2], aw[:, j, 0:1], None, ALU.mult))
                for k in (1, 2):
                    link(e.scalar_tensor_tensor(out=acc_a, in0=xa[:, k:ROW3 - 2 + k], scalar=aw[:, j, k:k + 1], in1=acc_a,
                                                op0=ALU.mult, op1=ALU.add))
                e.tensor_tensor(mix[:, j, 0:TP], acc_a[:, 0:TP], bb[:, 0:TP], ALU.mult)
                link(e.tensor_tensor(smp(mix[:, j]), at(BF + 512 + ROW3 + 2 + TP, NB * SEG3).rearrange("p (b n) -> p b n", n=SEG3)[:, :, 0:TS],
                                     smp(bb), ALU.mult))
            e.sem_inc(a_free, 1)
            e.sem_inc(tails, 1)

            e.wait_ge(gconv_in, 1)
            e.wait_ge(proj_evac, PROJ - GH)
            e.wait_ge(units, PROJ)
            e.wait_ge(gates_mm, 1)
            def gconv(i, s, first):
                if not first:
                    e.wait_ge(gconv_act, 2 * i + s - 1)
                g = gbuf[:, 2 * i + s]
                e.tensor_scalar(cacc[s], g[:, 0:ROW4 - 3], gw[:, 2 * i + s, 0:1], None, ALU.mult).then_inc(gconv_dve, 1)
                for k in (1, 2, 3):
                    e.wait_ge(gconv_dve, 8 * i + 4 * s + k)
                    e.scalar_tensor_tensor(out=cacc[s], in0=g[:, k:ROW4 - 3 + k], scalar=gw[:, 2 * i + s, k:k + 1], in1=cacc[s],
                                           op0=ALU.mult, op1=ALU.add).then_inc(gconv_dve, 1)
            gconv(0, 0, True)
            gconv(0, 1, True)
            with e.Fori(1, N_A // 2) as i:
                gconv(i, 0, False)
                gconv(i, 1, False)

            for t, (rows, col, _, _) in enumerate(HEADS):
                e.wait_ge(nh_rs, t + 1)
                if col is None:
                    e.tensor_tensor(rows, rows, hn_rs[t % 2], ALU.mult).then_inc(nh_mul, 1)
                else:
                    e.scalar_tensor_tensor(out=rows, in0=rows, scalar=gain[:, col:col + 1], in1=hn_rs[t % 2],
                                           op0=ALU.mult, op1=ALU.mult).then_inc(nh_mul, 1)

            e.wait_ge(gates_mm, 1)
            e.tensor_copy(sm[:, 0:4, :], bank(6, 128).rearrange("p (c n) -> p c n", n=32))
            link(e.tensor_copy(sm[0:NS, 4, :], bank(6, 32, NS, 128)))
            e.sem_inc(g_dve, 1)
            s5 = soft.rearrange("p (c h) -> p c h", h=GH)
            link(e.tensor_tensor(s5, sm[:, :, 24:28], gdn_in[:, 4:8].unsqueeze(1).broadcast_to([P, 5, GH]), ALU.add))
            e.scalar_tensor_tensor(out=soft2, in0=soft, scalar=-1.0, in1=soft, op0=ALU.mult, op1=ALU.min).then_inc(g_dve, 1)
            e.wait_ge(g_act, 2)
            link(e.scalar_tensor_tensor(out=soft, in0=soft, scalar=0.0, in1=soft2, op0=ALU.max, op1=ALU.add))
            e.scalar_tensor_tensor(out=gdec.rearrange("p (c h) -> p c h", h=GH), in0=s5, scalar=-1.0,
                                   in1=gdn_in[:, 0:4].unsqueeze(1).broadcast_to([P, 5, GH]), op0=ALU.mult, op1=ALU.mult).then_inc(g_dve, 1)
            e.wait_ge(g_pe, 1)
            e.tensor_copy(gc[:, 0:16], bank(7, 16))
            e.tensor_copy(gc[0:NS, 16:20], bank(7, 4, NS, 16))
            e.tensor_copy(gl[:, 0:16], bank(7, 16, P, 32))
            link(e.tensor_copy(gl[0:NS, 16:20], bank(7, 4, NS, 48)))
            e.tensor_tensor(ekd, gl, gc, ALU.subtract).then_inc(g_dve, 1)
            e.wait_ge(g_act, 3)
            link(e.memset(W["S"], 0.0))
            e.tensor_tensor(beg.rearrange("p (c h) -> p c h", h=GH), egc.rearrange("p (c h) -> p c h", h=GH), sm[:, :, 28:32],
                            ALU.mult).then_inc(g_dve, 1)

            def gdn_tile(t):
                PE_, AC, DV, r = steps(t)
                sample = t == 4
                n = NS if sample else P
                w, c0 = GH * n, P * t
                msu = (cst[0:n, C_SUB:C_SUB + n] if sample else su).unsqueeze(1).broadcast_to([n, GH, n])
                mtri = (cst[0:n, C_TRIB:C_TRIB + n] if sample else tri).unsqueeze(1).broadcast_to([n, GH, n])

                def b3(i, parts=P):
                    return bank(i, w, parts).rearrange("p (h i) -> p h i", h=GH)

                e.wait_ge(g_pe, PE_.after("rows", r))
                for h in range(GH):
                    last = e.tensor_scalar(heads("decT", n, n)[:, h], bank(0, n, n, n * h), gc[0:n, 4 * t + h:4 * t + h + 1], 0.0,
                                           ALU.subtract, ALU.min)
                last.then_inc(g_dve, 1)
                e.tensor_tensor(heads("kbT", n), ut[:, GH:2 * GH, c0:c0 + n], b3(1), ALU.mult).then_inc(g_dve, 1)
                e.wait_ge(g_act, AC.after("dec", r))
                e.wait_ge(g_pe, PE_.after("gram", r))
                e.tensor_tensor(heads("qeg", n), ut[:, 0:GH, c0:c0 + n], heads("eg", n), ALU.mult)
                e.tensor_tensor(heads("qk", n, n), b3(3, n), heads("decT", n, n), ALU.mult)
                link(e.scalar_tensor_tensor(out=heads("nl", n, n), in0=b3(2, n), scalar=-1.0, in1=heads("decT", n, n), op0=ALU.mult, op1=ALU.mult))
                e.tensor_tensor(heads("qk", n, n), heads("qk", n, n), mtri, ALU.mult)
                link(e.tensor_tensor(heads("nl", n, n), heads("nl", n, n), msu, ALU.mult))
                e.sem_inc(g_dve, 1)
                idb = ident[0:n, 0:n].unsqueeze(1).broadcast_to([n, GH, n])
                e.tensor_copy(heads("X", n, n), idb)
                link(e.tensor_copy(heads("XT", n, n), idb))
                e.sem_inc(g_dve, 1)
                for s in range(LVS if sample else LV):
                    lev = cst[0:n, C_LEV + P * s:C_LEV + P * s + n].unsqueeze(1).broadcast_to([n, GH, n])
                    link(e.tensor_tensor(heads("CT", n, n), heads("nl", n, n), lev, ALU.mult))
                    e.sem_inc(g_dve, 1)
                    e.wait_ge(g_pe, PE_.after(f"t2_{s}", r))
                    e.tensor_tensor(heads("X", n, n), heads("X", n, n), b3(1, n), ALU.add)
                    link(e.tensor_tensor(heads("XT", n, n), heads("XT", n, n), b3(2, n), ALU.add))
                    e.sem_inc(g_dve, 1)

                def y_out_():
                    e.wait_ge(g_act, AC.after("n", r))
                    link(e.scalar_tensor_tensor(out=W["oT"][:, 0:w], in0=W["oT"][:, 0:w], scalar=gain[:, G_GDN:G_GDN + 1], in1=W["rs"][:, 0:w],
                                                op0=ALU.mult, op1=ALU.mult))
                    e.tensor_tensor(mix[:, 12:16, c0:c0 + n], heads("oT", n), zbuf[:, :, c0:c0 + n], ALU.mult).then_inc(g_dve, 1)

                e.wait_ge(g_pe, PE_.after("o", r))
                if not sample:
                    for h in range(GH):
                        last = e.scalar_tensor_tensor(out=heads("S")[:, h], in0=heads("S")[:, h], scalar=heads("eg")[:, h, P - 1:P],
                                                      in1=bank(6, P, P, P * h), op0=ALU.mult, op1=ALU.add)
                    link(last)
                    e.sem_inc(g_dve, 1)
                    y_out_()
                    return

                def vm_(h):
                    e.tensor_tensor(vm[h % 2].rearrange("p (b d) -> p b d", b=NB),
                                    heads("vnew", P, n)[:, h].unsqueeze(1).broadcast_to([n, NB, P]),
                                    cst[0:n, C_BM:C_BM + NB].unsqueeze(2).broadcast_to([n, NB, P]), ALU.mult).then_inc(g_dve, 1)

                def add_(h):
                    e.wait_ge(g_pe, PE_.after(f"ds{h}", r))
                    b = 2 * (h % 2)
                    e.tensor_tensor(S_smp[:, :, h], S_smp[:, :, h],
                                    ps[:, 512 * b:512 * b + 1024].rearrange("p (b d) -> p b d", b=NB), ALU.add).then_inc(g_dve, 1)

                last_decay = W["eg"][:, 0:w].rearrange("p (h b t) -> p b h t", h=GH, t=TS)[:, :, :, TS - 1].unsqueeze(3).broadcast_to([P, NB, GH, P])
                link(e.tensor_tensor(S_smp, S_smp, last_decay, ALU.mult))
                e.sem_inc(g_dve, 1)
                vm_(0)
                y_out_()
                vm_(1)
                add_(0)
                vm_(2)
                add_(1)
                vm_(3)
                add_(2)
                add_(3)

            for t in range(5):
                gdn_tile(t)

            e.wait_ge(c_act, 4)
            e.scalar_tensor_tensor(out=kcT, in0=kcT, scalar=gain[:, G_K:G_K + 1], in1=crs, op0=ALU.mult, op1=ALU.mult).then_inc(c_dve, 1)

            e.wait_ge(turned, 2)
            e.wait_ge(g_act, GCS.end(1))
            sC = sS[0][:, 0:QH * NCP].rearrange("p (h c) -> p h c", h=QH)
            for i in range(4):
                n = 7 + 8 * i
                x0 = CB - 1 + 384 - P * i
                s = sC[:, :, 0:n]
                e.wait_ge(ac_pe, 2 * i + 1)
                if i > 0:
                    e.wait_ge(ac_pe, 2 * i)
                link(e.tensor_tensor(s, bank(4, QH * NCP).rearrange("p (h c) -> p h c", h=QH)[:, :, 0:n],
                                     bfull[:, :, x0:x0 + CS * (n - 1) + 1:CS], ALU.add))
                link(e.tensor_reduce(mx[:, 0:QH], s, AX, ALU.max))
                e.tensor_tensor(s, s, mx[:, 0:QH].unsqueeze(2).broadcast_to([P, QH, n]), ALU.subtract).then_inc(ac_dve, 1)
                e.wait_ge(ac_act, 2 * i + 1)
                if i == 0:
                    link(e.tensor_tensor(s, s, cst[:, C_VAL:C_VAL + n].unsqueeze(1).broadcast_to([P, QH, n]), ALU.mult))
                link(e.tensor_reduce(zz[:, 0:QH], s, AX, ALU.add))
                link(e.tensor_scalar(zz[:, 0:QH], zz[:, 0:QH], 1.0, None, ALU.max))
                link(e.reciprocal(rz[:, 0:QH], zz[:, 0:QH]))
                link(e.tensor_tensor(rz[:, 0:QH], rz[:, 0:QH], sm[:, i, 0:QH], ALU.mult))
                e.tensor_tensor(s, s, rz[:, 0:QH].unsqueeze(2).broadcast_to([P, QH, n]), ALU.mult).then_inc(ac_dve, 1)

            def scores(s):
                h, i, kind = ATT[s]
                n = P * (i + 1)
                e.wait_ge(a_s, s + 1)
                link(e.tensor_tensor(sS[s % 2][:, 0:n], bank(4 + s % 2, n), bfull[:, h, 384 - P * i:512], ALU.add))
                e.tensor_reduce(mx[:, s % 2:s % 2 + 1], sS[s % 2][:, 0:n], AX, ALU.max, negate=True).then_inc(a_m, 1)

            def scale(s):
                h, i, kind = ATT[s]
                n, c = P * (i + 1), s % 2
                e.wait_ge(a_e, s + 1)
                link(e.reciprocal(rz[:, c:c + 1], zz[:, c:c + 1]))
                link(e.tensor_tensor(rz[:, c:c + 1], rz[:, c:c + 1], sm[:, i, QH * (kind + 1) + h:QH * (kind + 1) + h + 1], ALU.mult))
                e.tensor_scalar(pP[c][:, 0:n], pP[c][:, 0:n], rz[:, c:c + 1], None, ALU.mult).then_inc(a_p, 1)

            e.wait_ge(ac_pe, 8)
            for s in range(len(ATT) + 1):
                if s < len(ATT):
                    scores(s)
                if s >= 1:
                    scale(s - 1)

            for h in range(QH):
                last = e.tensor_copy(qs[:, :, TS * h:TS * h + TS], smp(kvq[:, N_A + h]))
            link(last)
            e.sem_inc(k_new, 1)

            def softmax(s, q, n, step):
                link(e.tensor_reduce(mx[0:16, 0:q], s, AX, ALU.max))
                e.tensor_tensor(s, s, mx[0:16, 0:q].unsqueeze(2).broadcast_to([16, q, n]), ALU.subtract).then_inc(s_dve, 1)
                e.wait_ge(s_act, step)
                link(e.tensor_reduce(zz[0:16, 0:q], s, AX, ALU.add))
                link(e.reciprocal(rz[0:16, 0:q], zz[0:16, 0:q]))
                e.tensor_tensor(s, s, rz[0:16, 0:q].unsqueeze(2).broadcast_to([16, q, n]), ALU.mult).then_inc(s_dve, 1)

            e.wait_ge(s_pe, 2)
            sC2 = s_S.rearrange("p q k -> p (q k)")[:, 0:16 * NCS].rearrange("p (q c) -> p q c", c=NCS)
            for g in range(G):
                last = e.tensor_tensor(sC2[:, g::G], bank(0, 16 * NCS, 16).rearrange("p (q c) -> p q c", c=NCS)[:, g::G],
                                       biasS[:, g, CB - 1:CB - 1 + CS * (NCS - 1) + 1:CS].unsqueeze(1).broadcast_to([16, NB, NCS]), ALU.add)
            link(last)
            softmax(sC2, 16, NCS, 2)
            e.wait_ge(s_pe, 4)
            e.tensor_tensor(ys, bank(2, 256), grow[:, 0], ALU.mult).then_inc(s_dve, 1)
            for p in range(4):
                kind, bh = p // 2, p % 2
                for g in range(G):
                    last = e.tensor_copy(kbuf[bh][:, :, g, PAST:KEYS],
                                         smp(kvq[:, 4 + 4 * kind + g])[:, 4 * bh:4 * bh + 4])
                last.then_inc(k_new, 1)
                e.wait_ge(s_pe, 4 * p + 5)
                for g in range(G):
                    last = e.tensor_tensor(s_S[:, g::G], ps[0:16, :].rearrange("p (q n) -> p q n", n=512)[:, g::G, 0:KEYS],
                                           biasS[:, g].unsqueeze(1).broadcast_to([16, 4, KEYS]), ALU.add)
                link(last)
                softmax(s_S, 8, KEYS, 2 * p + 4)
                e.wait_ge(s_pe, 4 * p + 8)
                c = P * bh
                link(e.tensor_tensor(ytmp[:, 0:P], bank(4, P), grow[:, kind + 1, c:c + P], ALU.mult))
                link(e.tensor_tensor(ys[:, c:c + P], ys[:, c:c + P], ytmp[:, 0:P], ALU.add))
                e.sem_inc(s_dve, 1)
            for h in range(QH):
                last = e.tensor_copy(smp(mix[:, 4 + h]), ys.rearrange("p (b n) -> p b n", b=NB)[:, :, TS * h:TS * h + TS])
            e.wait_ge(a_ye, QH)
            last.then_inc(s_dve, 1)

            group_norm(1)
            group_norm(2)

            def h_sum(i, c):
                e.wait_ge(units, 2 * i + (U_OUT + c + 1))
                e.wait_ge(x_in[c], 16 * i + 16)
                for (d, x, b) in zip(halves(hbuf[:, 2 * i + c]), halves(xin[c]), (bank(2 * c, 256), bank(2 * c + 1, NT - 256))):
                    last = e.tensor_tensor(d, b, x, ALU.add)
                last.then_inc(h_add, 1)
            with e.Fori(0, KC // 2) as i:
                h_sum(i, 0)
                h_sum(i, 1)
            e.wait_ge(h_add, KC)
            group_norm(3)

            e.wait_ge(n_mul, GROUP_0[3] + 16)
            e.wait_ge(f_in, 32)
            e.wait_ge(h_out, 16)
            def ffn(i, first):
                for q in range(SLOTS):
                    u = SLOTS * i + q
                    e.wait_ge(up_evac, u + 1)
                    e.wait_ge(up_hist, u + 1)
                    x = fx[q]
                    e.tensor_scalar(facc[q], x[:, 0:ROW3 - 2], fw[:, u, 0:1], None, ALU.mult).then_inc(up_conv, 1)
                    for k in (1, 2):
                        e.wait_ge(up_conv, 3 * u + k)
                        e.scalar_tensor_tensor(out=facc[q], in0=x[:, k:ROW3 - 2 + k], scalar=fw[:, u, k:k + 1], in1=facc[q],
                                               op0=ALU.mult, op1=ALU.add).then_inc(up_conv, 1)
                    if q % 2:
                        j = 2 * i + q // 2
                        e.wait_ge(up_silu, j + 1)
                        e.wait_ge(up_conv, 3 * u + 3)
                        e.tensor_tensor(act[:, j, 0:TP], facc[q - 1][:, 0:TP], facc[q][:, 0:TP], ALU.mult)
                        e.tensor_tensor(smp(act[:, j]), seg(q - 1), seg(q), ALU.mult).then_inc(up_act, 1)

            def seg(q):
                return arena[:, Z + (ROW3 - 2) * q + 2 + TP:Z + (ROW3 - 2) * q + 2 + TP + NB * SEG3].rearrange("p (b n) -> p b n", n=SEG3)[:, :, 0:TS]

            ffn(0, True)
            with e.Fori(1, FC // 2) as i:
                ffn(i, False)

            e.wait_ge(up_act, FC)
            def y_sum(i, c, first):
                e.wait_ge(units, DU * (2 * i + c) + (U_DN + DU))
                e.wait_ge(h_in[c], 16 * i + 16)
                if not first:
                    e.wait_ge(y_out[c], 16 * i)
                for (d, x, b) in zip(halves(yout[c]), halves(hin[c]), (bank(2 * c, 256), bank(2 * c + 1, NT - 256))):
                    last = e.tensor_tensor(d, b, x, ALU.add)
                last.then_inc(dn_evac, 1)
            y_sum(0, 0, True)
            y_sum(0, 1, True)
            with e.Fori(1, KC // 2) as i:
                y_sum(i, 0, False)
                y_sum(i, 1, False)

        @block.gpsimd
        def _(e):
            e.wait_ge(s_cst, 16 * 9)
            e.wait_ge(a_free, 1)
            e.memset(gbuf[:, :, 0:3], 0.0)
            e.tensor_copy(gbuf[:, :, 3 + TP:ROW4].rearrange("p c (b n) -> p c b n", n=SEG4)[:, :, :, 0:3], hist_g).then_inc(p_chain, 1)
            e.wait_ge(p_chain, 1)
            e.sem_inc(gconv_in, 1)
            e.wait_ge(proj_evac, PROJ - GH)
            e.tensor_copy(tail_g[:, :, 0:3], gbuf[:, :, TP:TP + 3])
            e.tensor_copy(tail_g[:, :, 3:27].rearrange("p c (b k) -> p c b k", k=3),
                          gbuf[:, :, 3 + TP:ROW4].rearrange("p c (b n) -> p c b n", n=SEG4)[:, :, :, 4:SEG4]).then_inc(p_chain, 1)
            e.wait_ge(p_chain, 2)
            e.sem_inc(tails, 1)

            e.wait_ge(n_mul, GROUP_0[3] + 16)
            e.wait_ge(f_in, 32)
            for q in range(SLOTS):
                e.memset(fx[q][:, 0:2], 0.0)
            def rows(i, first):
                for q in range(SLOTS):
                    u = SLOTS * i + q
                    if not first:
                        e.wait_ge(up_conv, 3 * u - 9)
                    segs = fx[q][:, 2 + TP:ROW3].rearrange("p (b n) -> p b n", n=SEG3)
                    e.tensor_copy(segs[:, :, 0:2], hist[:, u]).then_inc(up_hist, 1)
                for q in range(SLOTS):
                    u = SLOTS * i + q
                    segs = fx[q][:, 2 + TP:ROW3].rearrange("p (b n) -> p b n", n=SEG3)
                    e.wait_ge(up_evac, u + 1)
                    e.tensor_copy(tail[:, u, 0:2], fx[q][:, TP:TP + 2])
                    e.tensor_copy(tail[:, u, 2:18].rearrange("p (b k) -> p b k", k=2), segs[:, :, 4:SEG3]).then_inc(up_tail, 1)
            rows(0, True)
            with e.Fori(1, FC // 2) as i:
                rows(i, False)


_OUTS = {
    "y_t": (P, KC, NT), "kv_t": (P, N_A, NT), "win_old": (NB, PAST, 2 * G * P), "tail_a": (P, 4, 18), "tail_g": (P, N_A, 27),
    "gdn_sp": (P, GH * P), "gdn_ss": (P, NB, GH, P), "tail_f": (P, 2 * FC, 18),
}


def _cols(w, n):
    k = w.shape[0] // P
    return np.ascontiguousarray(w.reshape(k, P, n, P).transpose(2, 1, 0, 3).reshape(n, P, k * P))


def _feat(a, lead):
    x = a.reshape(*a.shape[:-1], -1, P)
    return np.ascontiguousarray(np.moveaxis(np.moveaxis(x, -1, 0), -1, 1))


def lay_out(x):
    x = {k: np.asarray(v) for k, v in x.items()}
    w = x["w_in"][0]
    o = np.cumsum([0, 512, 512, 512, 1024, 1536, 24, 1536, 4, 4, 512])
    part = [w[:, o[i]:o[i + 1]] for i in range(10)]
    a_b, a_c, a_h, nq, nkv, gate, qkv, ga, gb, gz = part
    abc = np.stack([p.reshape(DM, 4, P) for p in (a_c, a_h, a_b)], axis=2).reshape(DM, 12 * P)
    consts, onehot, neg = shape_constants()
    toks = np.concatenate([x["x_prompt"][0], x["x_sample"].reshape(NS, DM)], axis=0)
    d = {}
    d["x_t"] = np.ascontiguousarray(toks.T.reshape(KC, P, NT).transpose(1, 0, 2))
    d["consts"], d["onehot"], d["neg"] = consts, onehot, neg
    flip = np.zeros((P, P + 16), np.float32)
    flip[:, :P] = np.eye(P)[::-1]
    flip[:16, P:] = np.kron(np.eye(REP), np.eye(TS)[::-1])
    d["flip"] = flip
    d["w_proj"] = _cols(np.concatenate([abc, nkv, nq, qkv, gz], axis=1), PROJ)
    small = np.concatenate([gate, ga, gb], axis=1)
    d["w_small"] = np.ascontiguousarray(small.reshape(KC, P, 32).transpose(1, 0, 2))
    vec = [x[n][0].reshape(-1, P).T for n in ("norm_mix_g", "norm_ffn_g", "out_norm_a", "out_norm_b", "q_norm_g", "k_norm_g", "gdn_norm_g")]
    d["gains"] = np.ascontiguousarray(np.concatenate(vec, axis=1))
    d["conv_w"] = np.concatenate([_feat(x["conv_a_w"][0], 1).reshape(P, 12), _feat(x["gdn_conv_w"][0], 1).reshape(P, 48)], axis=1)
    d["ffn_w"] = _inter(_feat(x["ffn_conv_w"][0], 1))
    d["hist_a"] = _feat(x["state_conv_a"][0], 2)
    d["hist_g"] = _feat(x["state_gdn_conv"][0], 2)
    d["hist_f"] = _inter(_feat(x["state_ffn_conv"][0], 2))
    d["gdn_ab"] = np.ascontiguousarray(np.broadcast_to(np.concatenate([x["gdn_a_log"][0], x["gdn_dt_bias"][0]])[None], (P, 8)))
    d["pe_t"] = np.ascontiguousarray(x["cmp_pe"][0].transpose(2, 0, 1))
    d["page_table"] = np.ascontiguousarray(x["page_table"].reshape(1, 16))
    d["rel_bias"] = x["rel_bias"]
    d["state_gdn"] = np.ascontiguousarray(x["state_gdn"][0].transpose(2, 0, 1, 3))
    kv = x["cache_kv"][0]
    d["cache_kt"] = np.ascontiguousarray(kv[:, :, 0:3].transpose(0, 4, 2, 3, 1))
    d["cache_v"] = np.ascontiguousarray(kv[:, :, 3])
    cw = x["cache_win"][0]
    d["win_kt"] = np.ascontiguousarray(cw[:, :, 0].transpose(3, 0, 2, 1))
    d["win_v"] = np.ascontiguousarray(cw[:, :, 1].reshape(NB, 2, PAGE, G, P).transpose(2, 0, 1, 3, 4))
    d["cache_win"] = cw.reshape(NB, PAST, 2 * G * P)
    w1 = x["cmp_w1"][0].reshape(2, 2, 16, P, 2, P)
    d["w1c"] = np.ascontiguousarray(w1.transpose(0, 4, 1, 3, 2, 5).reshape(8, P, UNIT))
    d["w2c"] = np.ascontiguousarray(x["cmp_w2"][0].reshape(2, 2, P, P).transpose(2, 0, 1, 3).reshape(P, 512))
    d["w_o"] = _cols(x["w_out"][0], KC)
    up = x["ffn_up"][0].reshape(DM, 2, FC, P).transpose(0, 2, 1, 3).reshape(DM, 2 * DFF)
    d["w_up"] = _cols(up, 2 * FC)
    d["w_dn"] = np.ascontiguousarray(_cols(x["ffn_down"][0], KC).reshape(KC, P, DU, DT * P).transpose(0, 2, 1, 3).reshape(KC * DU, P, DT * P))
    return d


def _inter(a):
    return np.ascontiguousarray(a.reshape(P, 2, FC, *a.shape[2:]).swapaxes(1, 2).reshape(P, 2 * FC, *a.shape[2:]))


def take_back(r):
    def feats(a):
        return np.ascontiguousarray(a.transpose(2, 1, 0)).reshape(a.shape[2], -1)

    def tails(a, k):
        f = feats(a)
        return f[:k][None, None], f[k:].reshape(1, NB, k, -1)

    y = feats(r["y_t"])
    kv = feats(r["kv_t"]).reshape(NT, 3, 2, G, P)
    rows, win = kv[:, 0:2].reshape(NT, 4, G, P), kv[:, 2]
    old = r["win_old"].reshape(NB, PAST, 2, G, P)
    win_s = np.concatenate([old, win[TP:].reshape(NB, TS, 2, G, P)], axis=1)
    ca, gv = tails(r["tail_a"], 2), tails(r["tail_g"], 3)
    tf = r["tail_f"].reshape(P, FC, 2, 18).transpose(0, 2, 1, 3).reshape(P, 2 * FC, 18)
    ff = tails(tf, 2)
    sp = r["gdn_sp"].reshape(P, GH, P).transpose(1, 0, 2)[None, None]
    ss = r["gdn_ss"].transpose(1, 2, 0, 3)[None]
    c = np.ascontiguousarray
    return (c(y[:TP][None]), c(y[TP:].reshape(NB, TS, DM)), c(rows[:TP][None, None]), c(rows[TP:].reshape(1, NB, TS, 4, G, P)),
            c(win[:TP][None, None]), c(win_s[None]), c(ca[0]), c(ca[1]), c(gv[0]), c(gv[1]), c(sp), c(ss), c(ff[0]), c(ff[1]))


def kernel(**inputs):
    import concourse.bacc as bacc
    from concourse.bass_utils import run_bass_kernel_spmd

    nc = bacc.Bacc("TRN2", target_bir_lowering=False, num_devices=1)
    arrays, ins, outs = {}, {}, {}
    for name, a in lay_out(inputs).items():
        arrays[f"in_{name}"] = a
        ins[name] = nc.dram_tensor(f"in_{name}", a.shape, mybir.dt.from_np(a.dtype), kind="ExternalInput").ap()
    for name, shape in _OUTS.items():
        outs[name] = nc.dram_tensor(f"out_{name}", shape, F32, kind="ExternalOutput").ap()
    build(nc, ins, outs)
    r = run_bass_kernel_spmd(nc, [arrays], core_ids=[0])
    return take_back({name: r.results[0][f"out_{name}"] for name in _OUTS})
```

```python
import math
from contextlib import ExitStack

import numpy as np
import concourse.bass as bass
from concourse import mybir

F32 = mybir.dt.float32
F32R = mybir.dt.float32r
I32 = mybir.dt.int32
ALU = mybir.AluOpType
ACT = mybir.ActivationFunctionType
AX = mybir.AxisListType.X

P = 128
DM = 2048
KC = DM // P
TP, NB, TS = 512, 8, 4
NS = NB * TS
NT = TP + NS
HALF = (256, NT - 256)
QH, G, REP = 8, 2, 4
GH = 4
PAST, PAGE = 256, 128
KEYS = PAST + TS
CB, CS = 32, 16
NCP, NCS = (TP - CB) // CS + 1, (KEYS - CB) // CS + 1
DFF = 5632
FC = DFF // P
NPOOL = 20
EPS = 1e-6
NEG = -1e30
SLOTS = 4
UNIT = KC * P
DT = 11
DU = FC // DT
N_A, N_KVQ, N_GZ = 12, 20, 16
PROJ = N_A + N_KVQ + N_GZ
U_CMP = PROJ
U_OUT = U_CMP + 8
U_UP = U_OUT + KC
U_DN = U_UP + 2 * FC
HALF_K = KC // 2
H_OUT = 2 * PROJ
H_UP = H_OUT + 2 * KC
H_END = H_UP + 4 * FC
R_CMP = 2 * PROJ // SLOTS
R_OUT = R_CMP + 8 // SLOTS
R_DN = R_OUT + (H_END - H_OUT) // SLOTS
SPILL = 16
DN_ORDER = (2, 3, 1, 0)
ROW3, SEG3 = 2 + TP + NB * (2 + TS), 2 + TS
ROW4, SEG4 = 3 + TP + NB * (3 + TS), 3 + TS
TAB = 640

C_ONE, C_ID, C_TRI, C_SU = 0, 128, 256, 384
C_LEV = 512
C_GRP, C_TRIB, C_SUB = C_LEV + 7 * 128, C_LEV + 7 * 128 + 32, C_LEV + 7 * 128 + 64
C_BM = C_SUB + 32
C_VAL = C_BM + 8
C_EPS = C_VAL + 7
NCONST = C_EPS + 3
G_MIX, G_FFN, G_OA, G_OB, G_Q, G_K, G_GDN = 0, 16, 32, 36, 44, 45, 46


def shape_constants():
    c = np.zeros((P, NCONST), np.float32)
    row, col = np.arange(P)[:, None], np.arange(P)[None, :]
    c[:, C_ONE:C_ONE + P] = 1
    c[:, C_ID:C_ID + P] = row == col
    c[:, C_TRI:C_TRI + P] = row <= col
    c[:, C_SU:C_SU + P] = row < col
    for s in range(7):
        same, split = row >> (s + 1) == col >> (s + 1), row >> s != col >> s
        c[:, C_LEV + s * P:C_LEV + (s + 1) * P] = same & split & (row < col)
    r, q = row[:NS], col[:, :NS]
    c[:NS, C_GRP:C_GRP + NS] = r // TS == q // TS
    c[:NS, C_TRIB:C_TRIB + NS] = (r // TS == q // TS) & (r <= q)
    c[:NS, C_SUB:C_SUB + NS] = (r // TS == q // TS) & (r < q)
    c[:NS, C_BM:C_BM + NB] = r // TS == np.arange(NB)[None, :]
    c[:, C_VAL:C_VAL + 7] = row >= CB - 1 + CS * np.arange(7)[None, :]
    c[:, C_EPS:C_EPS + 3] = [EPS, P * EPS, 1.0]
    dist = TP - 1 - np.arange(TAB)
    n = np.maximum(dist, 0)
    nf = np.maximum(n, 1).astype(np.float32)
    far = 16 + (np.log(nf / np.float32(16)) / np.float32(math.log(64)) * np.float32(16)).astype(np.int32)
    bucket = np.where(n < 16, n, np.minimum(far, 31))
    onehot = ((np.arange(32)[:, None] == bucket[None, :]) & (dist >= 0)[None, :]).astype(np.float32)
    neg = np.broadcast_to(np.where(dist >= 0, 0.0, NEG).astype(np.float32), (QH, TAB))
    return c, onehot, np.ascontiguousarray(neg)


class Steps:

    def __init__(self, sem, names, base=0):
        self.sem, self.names, self.base = sem, names, base

    def after(self, name, rnd=0):
        return self.base + rnd * len(self.names) + self.names.index(name) + 1

    def end(self, rounds):
        return self.base + rounds * len(self.names)


def build(nc, A, O):
    ctx = ExitStack()
    with ctx:
        XN = 0
        MIX = XN + KC * NT
        KVQ = MIX + KC * NT
        GA = KVQ + N_KVQ * NT
        Z = GA + N_A * ROW4
        BF = -(-(Z + GH * NT) // 8) * 8
        RING = BF + QH * 512
        CST = RING + SLOTS * UNIT
        GAIN = CST + NCONST
        CW = GAIN + 47
        SMALL = CW + 12 + 48

        words = 53156
        TN = KVQ + (FC - SPILL) * NT
        hw = HALF_K * P
        with nc.sbuf_tensor("x_hi", [P, KC * NT], F32R) as xhi_t, nc.sbuf_tensor("x_lo", [P, KC * NT], F32R) as xlo_t, \
                nc.sbuf_tensor("gap0", [P, TN - 2 * KC * NT], F32), nc.sbuf_tensor("x_whole", [P, 4 * NT], F32) as tn_t, \
                nc.sbuf_tensor("gap1", [P, BF - TN - 4 * NT], F32), nc.sbuf_tensor("w_gates", [P, 32 * KC], F32) as wsmall_t, \
                nc.sbuf_tensor("gap2", [P, RING - BF - 32 * KC], F32), nc.sbuf_tensor("w_whole", [P, 4 * hw], F32) as raw_t, \
                nc.sbuf_tensor("w_hi", [P, 2 * hw], F32R) as whi_t, nc.sbuf_tensor("w_lo", [P, 2 * hw], F32R) as wlo_t:
            pass
        arena = ctx.enter_context(nc.sbuf_tensor("arena", [P, words], F32))
        ptab = ctx.enter_context(nc.sbuf_tensor("ptab", [1, 16], I32))
        ps = ctx.enter_context(nc.psum_tensor("ps", [P, 8 * 512], F32))
        table_dram = nc.dram_tensor("bias_table", (QH, TAB), F32, kind="Internal").ap()
        ya_dram = nc.dram_tensor("y_a_spill", (P, 4, NT), F32, kind="Internal").ap()
        act_dram = nc.dram_tensor("act_spill", (P, SPILL, NT), F32, kind="Internal").ap()
        h_dram = nc.dram_tensor("h_spill", (P, KC, NT), F32, kind="Internal").ap()

        def sem(name):
            return ctx.enter_context(nc.semaphore(name))

        def at(off, n, parts=P):
            assert off + n <= words
            return arena[0:parts, off:off + n]

        def bank(i, n=512, parts=P, off=0):
            return ps[0:parts, i * 512 + off:i * 512 + off + n]

        mix = at(MIX, KC * NT).rearrange("p (k t) -> p k t", k=KC)
        kvq = at(KVQ, N_KVQ * NT).rearrange("p (k t) -> p k t", k=N_KVQ)
        abuf = at(GA, N_A * NT).rearrange("p (k t) -> p k t", k=N_A)
        gbuf = at(GA, N_A * ROW4).rearrange("p (k t) -> p k t", k=N_A)
        zbuf = at(Z, GH * NT).rearrange("p (k t) -> p k t", k=GH)
        slot = [at(RING + s * UNIT, UNIT).rearrange("p (k n) -> p k n", n=P) for s in range(SLOTS)]
        xhi, xlo = (t[:].rearrange("p (k t) -> p k t", k=KC) for t in (xhi_t, xlo_t))
        raw = [raw_t[:, s * hw:(s + 1) * hw] for s in range(4)]
        whi, wlo = ([t[:, s * hw:(s + 1) * hw] for s in range(2)] for t in (whi_t, wlo_t))
        whi_f = [w.bitcast(F32) for w in whi]
        xhi_f, xlo_f = xhi.bitcast(F32), xlo.bitcast(F32)
        cst = at(CST, NCONST)
        gain = at(GAIN, 47)
        aw = at(CW, 12).rearrange("p (c k) -> p c k", k=3)
        gw = at(CW + 12, 48).rearrange("p (c k) -> p c k", k=4)
        ones, ident, tri = cst[:, C_ONE:C_ONE + P], cst[:, C_ID:C_ID + P], cst[:, C_TRI:C_TRI + P]
        su = cst[:, C_SU:C_SU + P]
        eps1, eps128, one = (cst[:, C_EPS + i:C_EPS + i + 1] for i in range(3))

        pos = [SMALL]

        def small(n, parts=P):
            pos[0] += n
            return at(pos[0] - n, n, parts)

        sm = small(160).rearrange("p (c n) -> p c n", c=5)
        gdn_in = small(8)
        soft = small(20)
        soft2 = small(20)
        gdec = small(20)
        gc = small(20)
        gl = small(20)
        egc, ekd, beg = small(20), small(20), small(20)
        egl = small(16)
        biasS = small(G * KEYS, 16).rearrange("p (g k) -> p g k", g=G)
        kcT = small(2 * NCP + 16 * NCS)
        vcP = small(G * P, NCP).rearrange("p (g d) -> p g d", g=G)
        pebs = small(4)
        mx, zz, rz = small(16), small(16), small(16)
        assert pos[0] <= words, pos[0]

        wsmall = wsmall_t[:].rearrange("p (k n) -> p k n", k=KC)
        xa = at(BF + 512, ROW3)
        acc_a = at(BF + 512 + ROW3, ROW3 - 2)
        o = BF + 512 + 2 * ROW3 - 2
        hist_a = at(o, 64).rearrange("p (c b k) -> p c b k", c=4, b=NB)
        hist_g = at(o + 64, 288).rearrange("p (c b k) -> p c b k", c=N_A, b=NB)
        tail_a = at(o + 352, 72).rearrange("p (c n) -> p c n", c=4)
        tail_g = at(o + 424, 324).rearrange("p (c n) -> p c n", c=N_A)
        assert o + 748 <= BF + 2384
        nrm_sq = [at(Z, NT), at(Z + NT, NT)]
        rs1 = at(Z + 2 * NT, NT)

        ut = at(XN, N_A * NT).rearrange("p (k t) -> p k t", k=N_A)
        cacc = [at(XN + N_A * NT, ROW4 - 3), at(XN + N_A * NT + ROW4, ROW4 - 3)]
        names = ["decT", "kbT", "eg", "qeg", "nl", "qk", "X", "XT", "CT", "T1", "vb", "kbeg", "kd"]
        W = {n: at(GA + 512 * i, 512) for i, n in enumerate(names)}
        for i, n in enumerate(["nwT", "vnew", "S", "oT", "sq", "rs"]):
            W[n] = at(RING + 512 * i, 512)
        free = [MIX + 4 * NT + 512 * i for i in range(8)] + [XN + N_A * NT + 512 * i for i in range(4)]
        free += [BF + 2384 + 512 * i for i in range(3)] + [RING + 7168 + 512 * i for i in range(2)]
        tile_names = [f"{n}{t}" for t in (1, 2, 3) for n in ("X", "XT")]
        tile_names += [f"{n}{t}" for n in ("nl", "qk", "qeg") for t in (1, 2, 3)] + ["CT_odd", "T1_odd"]
        W.update({n: at(a, 512) for n, a in zip(tile_names, free, strict=True)})
        XX = [at(GA + 512 * names.index("X"), 1024)] + [at(free[2 * i], 1024) for i in range(3)]

        def of(n, t):
            return f"{n}{t}" if 0 < t < 4 else n

        CT, T1 = ("CT", "CT_odd"), ("T1", "T1_odd")
        DEC, KB, EG = ("decT", "kbeg"), ("kbT", "vb"), ("eg", "kd")
        VB, KBEG, KD = ("vb", "CT"), ("kbeg", "CT_odd"), ("kd", "T1")
        S_smp = at(RING + 3072, 4096).rearrange("p (b h e) -> p b h e", b=NB, h=GH)
        vm = [at(RING + 7168, 1024, NS), at(GA, 1024, NS)]
        hn_sq = [at(GA, NT), at(GA + NT, NT)]
        hn_rs = [at(GA + 2 * NT, NT), at(GA + 3 * NT, NT)]
        relb, onehot = at(KVQ, QH, 32), at(KVQ + 8, TAB, 32)
        negt, tabs = at(KVQ + 8 + TAB, TAB, QH), at(KVQ + 8 + 2 * TAB, TAB, QH)

        def heads(w, n=P, parts=P):
            return W[w][0:parts, 0:GH * n].rearrange("p (h i) -> p h i", h=GH)

        seg_t = at(XN, 2 * 17 * PAST).rearrange("p (k s t) -> p k s t", k=2, s=17)
        crT = seg_t[:, :, 0:16].rearrange("p k (b g) t -> p k b g t", b=NB)
        flip = at(GA + 6144, P + 16)
        w2 = at(BF, 512).rearrange("p (k c d) -> p k c d", k=2, c=2)
        NCOL = G * NCP + 16 * NCS
        hid = at(BF + 512, 4 * NCOL).rearrange("p (k c n) -> p k c n", k=2, c=2)
        csq, crs = at(BF + 2048, NCOL), at(BF + 2560, NCOL)
        vcS = at(Z, 2048, NCS).rearrange("p (q d) -> p q d", d=P)

        bfull = at(BF, QH * 512).rearrange("p (h x) -> p h x", h=QH)
        PTc = at(GA, 4096, NCP).rearrange("p (h t) -> p h t", h=QH)
        VN = at(GA + 4096, 2048).rearrange("p (k g j d) -> p k g j d", k=2, g=G, j=4)
        sC = at(RING, QH * NCP).rearrange("p (h c) -> p h c", h=QH)
        pS = [at(RING + 1024 * i, 1024).rearrange("p (k t) -> p k t", k=2) for i in range(3)]
        pT = [at(RING + 3072 + 1024 * i, 1024).rearrange("p (k t) -> p k t", k=2) for i in range(2)]
        o = RING + 3072
        s_S = at(o, 8 * KEYS, 16).rearrange("p (q k) -> p q k", k=KEYS)
        s_PT = at(o + 2080, 256)
        s_PN = at(o + 2336, 128, TS)
        s_VN = at(o + 2464, 1024, TS).rearrange("p (q d) -> p q d", d=P)
        grow = at(o + 3488, 768).rearrange("p (k n) -> p k n", k=3)
        ys = at(o + 4256, 256)
        qs = at(o + 4512, 256).rearrange("p (b n) -> p b n", b=NB)
        ytmp = at(o + 4768, 256)
        assert 3072 + 4768 + 256 <= SLOTS * UNIT
        kbuf = [at(XN + i * 4128, 2080).rearrange("p (b g k) -> p b g k", b=4, g=G) for i in range(2)]
        vbuf = [at(XN + i * 4128 + 2080, 2048).rearrange("p (b j g d) -> p b j g d", b=4, j=2, g=G) for i in range(2)]

        hbuf = at(KVQ, KC * NT).rearrange("p (k t) -> p k t", k=KC)
        xin = [at(Z + i * NT, NT) for i in range(2)]
        act = at(KVQ, (FC - SPILL) * NT).rearrange("p (k t) -> p k t", k=FC - SPILL)
        act_first = at(XN, SPILL * NT).rearrange("p (k t) -> p k t", k=SPILL)
        f = TN
        fx = [at(f + ROW3 * i, ROW3) for i in range(4)]
        FACC = f + 4 * ROW3
        facc = [at(FACC + (ROW3 - 2) * i, ROW3 - 2) for i in range(4)]
        o = FACC + 4 * (ROW3 - 2)
        spill = [at(o + NT * i, NT) for i in range(2)]
        o += 2 * NT
        hist = at(o, 2 * FC * 16).rearrange("p (u b k) -> p u b k", u=2 * FC, b=NB)
        tail = at(o + 2 * FC * 16, 2 * FC * 18).rearrange("p (u n) -> p u n", u=2 * FC)
        assert Z + 2 * NT <= o and o + 2 * FC * 34 <= RING
        fw = at(CST + C_LEV, 6 * FC).rearrange("p (u k) -> p u k", u=2 * FC)
        tn = [tn_t[:, NT * i:NT * (i + 1)] for i in range(4)]
        hin = [at(f + NT * i, NT) for i in range(2)]
        yout = [at(f + NT * (2 + i), NT) for i in range(2)]

        s_x, s_cst, s_tab = sem("x_loaded"), sem("constants_loaded"), sem("table_inputs_loaded")
        w_ready = [sem(f"weights_in_slot{s}") for s in range(SLOTS)]
        units = sem("units_multiplied")
        w_hi, w_lo = sem("weights_high_part"), sem("weights_low_part")
        used = sem("first_halves_multiplied")
        proj_evac = sem("proj_evacuated")
        n_sq, n_mm, n_rs, n_mul = (sem(n) for n in ("norm_squared", "norm_summed", "norm_rstd", "norm_scaled"))
        n_hi, n_lo = sem("x_high_part"), sem("x_low_part")
        ya_out, ya_in = sem("y_a_stored"), sem("y_a_reloaded")
        act_out, act_in = [sem("act_stored0"), sem("act_stored1")], sem("act_reloaded")
        gates_mm, conv_a, a_free = sem("gates_summed"), sem("conv_a_done"), sem("conv_a_buffer_read")
        gconv_in, gconv_dve, gconv_act = sem("gdn_conv_rows_set"), sem("gdn_conv_tap"), sem("gdn_conv_silu")
        tails = sem("conv_tails_copied")
        nh_sq, nh_mm, nh_rs, nh_mul = (sem(n) for n in ("hnorm_squared", "hnorm_summed", "hnorm_rstd", "hnorm_scaled"))
        g_pe, g_act, g_dve = sem("gdn_pe"), sem("gdn_act"), sem("gdn_dve")
        r_rows, r_dec, r_kb, r_exp, r_gram, r_low = (sem(n) for n in (
            "decay_rows", "decay_exponents", "beta_k", "decay_exp", "grams", "grams_decayed"))
        l_ct, l_t1p, l_t1c, l_t2, l_x = (sem(n) for n in (
            "level_masked", "level_first_product", "level_first_copied", "level_second_product", "level_added"))
        q_nat, q_vk, q_w, q_nw, q_v, q_vn, q_o, q_s, q_oc, q_n, q_rs, q_y = (sem(n) for n in (
            "kv_token_major", "kv_scaled", "w_product", "w_negated", "v_new_product", "v_new_copied",
            "o_product", "state_updated", "o_copied", "o_squares_summed", "o_rstd", "y_c_done"))
        st_in, gdn_stored = sem("states_loaded"), sem("gdn_states_stored")
        c_in, c_pe, c_act, c_dve = sem("cache_loaded"), sem("cmp_pe"), sem("cmp_act"), sem("cmp_dve")
        t_pe, t_dve, t_out, bs_in, bf_in = sem("table_summed"), sem("table_ready"), sem("table_stored"), sem("sample_bias_loaded"), sem("bias_loaded")
        turned_pe, turned = sem("bias_turned"), sem("bias_turned_copied")
        v_pe, v_act = sem("values_transposed"), sem("values_copied")
        ac_pe, ac_act, ac_dve = sem("acmp_pe"), sem("acmp_act"), sem("acmp_dve")
        a_s, a_m, a_e, a_p, a_t, a_pt, a_y, a_ye = (sem(n) for n in (
            "scores_ready", "max_ready", "exp_ready", "probs_ready", "probs_transposed", "probsT_copied",
            "head_summed", "head_evacuated"))
        kv_in, k_new = [sem("kv_loaded0"), sem("kv_loaded1")], sem("new_keys_copied")
        s_pe, s_act, s_dve = sem("smp_pe"), sem("smp_act"), sem("smp_dve")
        x_in, h_add = [sem("x_reloaded0"), sem("x_reloaded1")], sem("h_added")
        h_out, f_in = sem("h_stored"), sem("ffn_small_loaded")
        up_evac, up_hist, up_tail, up_conv, up_silu, up_act = (sem(n) for n in (
            "up_evacuated", "up_history", "up_tail", "up_conv", "up_silu", "up_gated"))
        h_in, dn_evac, y_out = [sem("h_reloaded0"), sem("h_reloaded1")], sem("y_ready"), [sem("y_stored0"), sem("y_stored1")]
        stored = sem("outputs_stored")
        d_chain, a_chain, p_chain = sem("dve_done"), sem("act_done"), sem("pool_done")

        LV, LVS = 7, 2
        t1, t2 = [[f"t1_{s}", f"t2_{s}"] for s in range(LVS)], [[f"ct_{s}", f"x_{s}"] for s in range(LVS)]
        PRE_PE, PRE_ACT, PRE_DVE = 1, 3, 5
        GPS = Steps(g_pe, ["rows", "gram", "nat"] + sum(t1, []) + ["w", "v", "vt", "o", "n", "ds0", "ds1", "ds2", "ds3"], PRE_PE)
        GCS = Steps(g_act, ["dec", "nat"] + [x[0] for x in t1] + ["w", "v", "vt", "o", "n"], PRE_ACT)
        GDS = Steps(g_dve, ["dec", "kb", "low", "xinit"] + sum(t2, []) + ["smul", "vm0", "y", "vm1", "add0", "vm2", "add1", "vm3", "add2", "add3"], PRE_DVE)
        LEVELS = [(s, t) for s in range(LV) for t in range(4)]

        HEADS = [(ut[:, h], None, float(P), eps128) for h in range(GH)]
        HEADS += [(ut[:, GH + h], None, 1.0, eps1) for h in range(GH)]
        HEADS += [(kvq[:, k], G_K, 1.0 / P, eps1) for k in (4, 5, 8, 9)]
        HEADS += [(kvq[:, N_A + h], G_Q, 1.0, eps128) for h in range(QH)]
        GROUPS = [(mix[:, 0:16], 0, G_MIX), (mix[:, 0:4], 0, G_OA), (mix[:, 4:12], 4, G_OB), (hbuf[:, 0:16], 0, G_FFN)]
        GROUP_N = [16, 4, 8, 16]
        GROUP_0 = [0, 16, 20, 28]
        SPLIT_0 = [0, 16, 20, 32]
        ATT = [(h, i) for h in range(QH) for i in range(4)]

        def halves(x):
            return x[:, 0:256], x[:, 256:NT]

        def rows3(x):
            return x[:, 2:2 + TP], x[:, 2 + TP:ROW3].rearrange("p (b n) -> p b n", n=SEG3)[:, :, 2:SEG3]

        def smp(x):
            return x[:, TP:NT].rearrange("p (b t) -> p b t", t=TS)

        block = ctx.enter_context(nc.Block())

        @block.sync
        def _(e):
            def unit(u, src, n=UNIT):
                e.dma_start(at(RING + (u % SLOTS) * UNIT, n), src).then_inc(w_ready[u % SLOTS], 16)

            for dst, name in ((cst, "consts"), (gain, "gains"), (at(CW, 60), "conv_w"), (wsmall, "w_small"),
                              (gdn_in, "gdn_ab"), (hist_a, "hist_a"), (hist_g, "hist_g"),
                              (ptab[:], "page_table")):
                e.dma_start(dst, A[name]).then_inc(s_cst, 16)
            for q in range(4):
                e.dma_start(mix[:, 4 * q:4 * q + 4, :], A["x_t"][:, 4 * q:4 * q + 4, :]).then_inc(s_x, 16)
            def half_units(w, i, h0, first):
                for s in range(SLOTS):
                    if not first:
                        e.wait_ge(w_lo, SLOTS * i + (h0 + s - SLOTS + 1))
                    e.dma_start(raw[s], w[2 * i + s // 2][:, hw * (s % 2):hw * (s % 2 + 1)]).then_inc(w_ready[s], 16)

            half_units(A["w_proj"], 0, 0, True)
            with e.Fori(1, PROJ // 2) as i:
                half_units(A["w_proj"], i, 0, False)

            e.wait_ge(units, PROJ)
            e.dma_start(S_smp, A["state_gdn"]).then_inc(st_in, 16)
            e.wait_ge(gates_mm, 1)
            e.wait_ge(ya_out, 16)
            e.dma_start(mix[:, 0:4], ya_dram).then_inc(ya_in, 16)

            e.wait_ge(g_dve, GDS.end(1))
            e.wait_ge(g_pe, GPS.end(1))
            e.wait_ge(g_act, GCS.end(1))
            e.dma_start(O["gdn_sp"], W["S"]).then_inc(gdn_stored, 16)
            e.dma_start(O["gdn_ss"], S_smp).then_inc(gdn_stored, 16)
            e.wait_ge(tails, 2)
            e.dma_start(O["tail_a"], tail_a).then_inc(gdn_stored, 16)
            e.dma_start(O["tail_g"], tail_g).then_inc(gdn_stored, 16)
            e.wait_ge(s_cst, 16 * 8)
            e.wait_ge(gdn_stored, 64)
            e.dma_start(w2, A["w2c"]).then_inc(c_in, 16)
            e.dma_start(flip, A["flip"]).then_inc(c_in, 16)
            pages = [e.value_load(ptab[0:1, q:q + 1], min_val=0, max_val=NPOOL - 1) for q in range(16)]
            for q in range(16):
                b, j = q // 2, q % 2
                for k in range(2):
                    e.dma_start(crT[:, k, b, :, j * PAGE:(j + 1) * PAGE], A["cache_kt"][pages[q], :, k]).then_inc(c_in, 16)
            e.dma_start(seg_t[:, :, 16], A["pe_t"]).then_inc(c_in, 16)
            for u in range(8):
                if u >= SLOTS:
                    e.wait_ge(units, U_CMP + u - SLOTS + 1)
                unit(u, A["w1c"][u])

            for p in range(4):
                kind, bh = p // 2, p % 2
                if p == 0:
                    e.wait_ge(c_pe, 2)
                if p >= 2:
                    e.wait_ge(s_pe, 4 + 4 * (p - 1))
                for b in range(4):
                    for j in range(2):
                        q = 2 * (4 * bh + b) + j
                        kd = kbuf[bh][:, b, :, j * PAGE:(j + 1) * PAGE]
                        vd = vbuf[bh][:, b, j]
                        if kind == 0:
                            e.dma_start(kd, A["cache_kt"][pages[q], :, 2]).then_inc(kv_in[bh], 16)
                            e.dma_start(vd, A["cache_v"][pages[q]]).then_inc(kv_in[bh], 16)
                        else:
                            e.dma_start(kd, A["win_kt"][:, 4 * bh + b, :, j * PAGE:(j + 1) * PAGE]).then_inc(kv_in[bh], 16)
                            e.dma_start(vd, A["win_v"][:, 4 * bh + b, j]).then_inc(kv_in[bh], 16)

            e.wait_ge(s_dve, 16)
            e.wait_ge(s_pe, 20)
            e.wait_ge(a_ye, QH)
            half_units(A["w_o"], 0, H_OUT, True)
            with e.Fori(1, KC // 2) as i:
                half_units(A["w_o"], i, H_OUT, False)
            with e.Fori(0, FC) as i:
                half_units(A["w_up"], i, H_UP, False)
            for s in range(SLOTS):
                e.wait_ge(w_lo, H_END)
                if s >= 2:
                    e.wait_ge(units, U_DN)
                e.dma_start(at(RING + s * UNIT, DT * P), A["w_dn"][DN_ORDER[s]]).then_inc(w_ready[s], 16)
            with e.Fori(1, KC) as i:
                for s in range(SLOTS):
                    e.wait_ge(units, U_DN + SLOTS * i + s - SLOTS + 1)
                    e.dma_start(at(RING + s * UNIT, DT * P), A["w_dn"][SLOTS * i + DN_ORDER[s]]).then_inc(w_ready[s], 16)
            e.wait_ge(stored, 16 * 3)
            for q in range(2):
                e.wait_ge(y_out[q], 16 * (KC // 2))

        @block.tensor
        def _(e):
            def mm(out, lhsT, rhs, start=True, stop=True):
                return e.matmul(out, lhsT, rhs, start=start, stop=stop, skip_group_check=True)

            def tr(out, in_):
                n = in_.shape[0]
                return e.transpose(out, in_, ident[0:n, 0:n])

            def unit(i, h, banks):
                for half in range(2):
                    e.wait_ge(w_lo, SLOTS * i + (h + half + 1))
                    for k in range(HALF_K):
                        c = HALF_K * half + k
                        wh, wl = (w[half][:, P * k:P * k + P] for w in (whi, wlo))
                        for n, (w, x) in enumerate(((wh, xhi), (wh, xlo), (wl, xhi))):
                            start, stop = c == 0 and n == 0, c == KC - 1 and n == 2
                            a, b = halves(x[:, c])
                            mm(bank(banks, 256), w, a, start, stop)
                            last = mm(bank(banks + 1, NT - 256), w, b, start, stop)
                    last.then_inc(units if half else used, 1)

            def sum_squares(sq, first, last, banks):
                lo, hi = halves(sq)
                mm(bank(banks, 256), ones, lo, first, last)
                return mm(bank(banks + 1, NT - 256), ones, hi, first, last)

            def group_norm(g):
                for k in range(GROUP_N[g]):
                    e.wait_ge(n_sq, GROUP_0[g] + k + 1)
                    sum_squares(nrm_sq[k % 2], k == 0, k == GROUP_N[g] - 1, 4).then_inc(n_mm, 1)

            e.wait_ge(s_tab, 48)
            mm(bank(6, 320, QH), relb, onehot[:, 0:320])
            mm(bank(7, 320, QH), relb, onehot[:, 320:TAB]).then_inc(t_pe, 1)

            e.wait_ge(s_cst, 16 * 8)
            group_norm(0)

            e.wait_ge(n_lo, 16)
            unit(0, 0, 0)
            unit(0, 2, 2)
            with e.Fori(1, PROJ // 2) as i:
                for s in range(2):
                    e.wait_ge(proj_evac, 2 * i + s - 1)
                    unit(i, 2 * s, 2 * s)
            e.wait_ge(t_dve, 1)
            for t in range(5):
                n = P if t < 4 else NS
                for k in range(KC):
                    mm(bank(6, 32, n, 32 * t), xhi_f[:, k, P * t:P * t + n], wsmall[:, k], k == 0, False)
                    last = mm(bank(6, 32, n, 32 * t), xlo_f[:, k, P * t:P * t + n], wsmall[:, k], False, k == KC - 1)
            last.then_inc(gates_mm, 1)

            for t in range(len(HEADS)):
                e.wait_ge(nh_sq, t + 1)
                if t >= 2:
                    e.wait_ge(nh_rs, t - 1)
                else:
                    e.wait_ge(proj_evac, PROJ)
                sum_squares(hn_sq[t % 2], True, True, 2 * (t % 2)).then_inc(nh_mm, 1)

            e.wait_ge(g_dve, 3)
            mm(bank(7, 16, P, 0), tri, gdec[:, 0:16])
            mm(bank(7, 4, NS, 16), cst[0:NS, C_TRIB:C_TRIB + NS], gdec[0:NS, 16:20])
            mm(bank(7, 16, P, 32), ones, gdec[:, 0:16])
            mm(bank(7, 4, NS, 48), cst[0:NS, C_GRP:C_GRP + NS], gdec[0:NS, 16:20]).then_inc(g_pe, 1)

            def out(b, h, cols, parts=P):
                return bank(b, cols, parts, h * cols)

            def rows(t):
                n, b = (P, 4 * (t % 2)) if t < 4 else (NS, 0)
                for h in range(GH):
                    c = 4 * t + h
                    mm(out(b, h, n), gdec[0:n, c:c + 1].broadcast_to([n, P]), tri if t < 4 else cst[0:n, C_TRIB:C_TRIB + n])
                    last = mm(out(b + 1, h, n), sm[0:n, t, 28 + h:29 + h].broadcast_to([n, P]), ident[0:n, 0:n])
                return last

            def gram(t, kb):
                n, b = (P, 4 * (t % 2)) if t < 4 else (NS, 0)
                for h in range(GH):
                    kh = ut[:, GH + h, P * t:P * t + n]
                    mm(out(b + 2, h, n, n), kh, heads(kb, n)[:, h])
                    last = mm(out(b + 3, h, n, n), kh, ut[:, h, P * t:P * t + n])
                return last

            def nat(t, b):
                n = P if t < 4 else NS
                for h in range(GH):
                    tr(out(b, h, P, n), ut[:, GH + h, P * t:P * t + n])
                    last = tr(out(b + 1, h, P, n), ut[:, 2 * GH + h, P * t:P * t + n])
                return last

            e.wait_ge(g_dve, PRE_DVE)
            e.wait_ge(nh_mul, len(HEADS))
            for t in range(5):
                if t < 4:
                    if t >= 2:
                        e.wait_ge(r_low, t - 1)
                    rows(t).then_inc(r_rows, 1)
                if t >= 1:
                    e.wait_ge(r_kb, t)
                    gram(t - 1, KB[(t - 1) % 2]).then_inc(r_gram, 1)

            def first_product(m):
                s, t = LEVELS[m]
                e.wait_ge(l_ct, m + 1)
                if m == 0:
                    e.wait_ge(r_low, 4)
                if m >= 4:
                    e.wait_ge(l_x, m - 3)
                if m >= 2:
                    e.wait_ge(l_t1c, m - 1)
                for h in range(GH):
                    last = mm(out(m % 2, h, P), heads(CT[m % 2])[:, h], heads(of("X", t))[:, h])
                last.then_inc(l_t1p, 1)

            def second_product(m):
                s, t = LEVELS[m]
                e.wait_ge(l_t1c, m + 1)
                if m >= 3:
                    e.wait_ge(l_x, m - 2)
                b = 2 + 2 * (m % 3)
                first, xt = heads(T1[m % 2]), heads(of("XT", t))
                if s < LV - 1:
                    for h in range(GH):
                        mm(out(b, h, P), xt[:, h], first[:, h])
                for h in range(GH):
                    last = mm(out(b + 1, h, P), first[:, h], xt[:, h])
                last.then_inc(l_t2, 1)

            first_product(0)
            for m in range(len(LEVELS)):
                if m + 1 < len(LEVELS):
                    first_product(m + 1)
                second_product(m)

            def w_product(t):
                e.wait_ge(q_vk, t + 1)
                if t >= 1:
                    e.wait_ge(q_nw, t)
                for h in range(GH):
                    last = mm(out(3, h, P), heads(KBEG[t % 2])[:, h], heads(of("XT", t))[:, h])
                last.then_inc(q_w, 1)

            e.wait_ge(l_x, len(LEVELS))
            nat(0, 0).then_inc(q_nat, 1)
            w_product(0)
            for t in range(4):
                e.wait_ge(q_nw, t + 1)
                if t > 0:
                    e.wait_ge(q_s, t)
                for h in range(GH):
                    mm(out(4, h, P), heads(of("XT", t))[:, h], heads(VB[t % 2])[:, h], True, False)
                    last = mm(out(4, h, P), heads("nwT")[:, h], heads("S")[:, h], False, True)
                last.then_inc(q_v, 1)
                if t < 3:
                    e.wait_ge(q_vk, t + 1)
                    nat(t + 1, 0).then_inc(q_nat, 1)
                e.wait_ge(q_vn, t + 1)
                if t > 0:
                    e.wait_ge(q_oc, t)
                for h in range(GH):
                    mm(out(5, h, P), heads("S")[:, h], heads(of("qeg", t))[:, h], True, False)
                    mm(out(5, h, P), heads("vnew")[:, h], heads(of("qk", t))[:, h], False, True)
                for h in range(GH):
                    last = mm(out(6, h, P), heads(KD[t % 2])[:, h], heads("vnew")[:, h])
                last.then_inc(q_o, 1)
                if t < 3:
                    w_product(t + 1)
                e.wait_ge(q_oc, t + 1)
                if t > 0:
                    e.wait_ge(q_rs, t)
                mm(bank(7), ones, W["sq"]).then_inc(q_n, 1)

            n = NS
            e.wait_ge(q_y, 4)
            rows(4).then_inc(g_pe, 1)
            e.wait_ge(g_dve, GDS.after("kb"))
            gram(4, "kbT").then_inc(g_pe, 1)
            nat(4, 4).then_inc(g_pe, 1)
            for s in range(LVS):
                e.wait_ge(g_dve, GDS.after(f"ct_{s}"))
                for h in range(GH):
                    last = mm(out(0, h, n, n), heads("CT", n, n)[:, h], heads("X", n, n)[:, h])
                last.then_inc(g_pe, 1)
                e.wait_ge(g_act, GCS.after(f"t1_{s}"))
                for h in range(GH):
                    mm(out(1, h, n, n), heads("XT", n, n)[:, h], heads("T1", n, n)[:, h])
                for h in range(GH):
                    last = mm(out(2, h, n, n), heads("T1", n, n)[:, h], heads("XT", n, n)[:, h])
                last.then_inc(g_pe, 1)
            e.wait_ge(g_dve, GDS.after(f"x_{LVS - 1}"))
            e.wait_ge(g_act, GCS.after("nat"))
            for h in range(GH):
                last = mm(out(3, h, n), heads("kbeg", P, n)[:, h], heads("XT", n, n)[:, h])
            last.then_inc(g_pe, 1)
            e.wait_ge(g_act, GCS.after("w"))
            e.wait_ge(st_in, 16)
            for h in range(GH):
                mm(out(4, h, n), heads("vb", P, n)[:, h], heads("XT", n, n)[:, h], True, False)
                for b in range(NB):
                    last = mm(bank(4, TS, P, h * n + TS * b), S_smp[:, b, h], heads("nwT", n)[:, h, TS * b:TS * b + TS], False, b == NB - 1)
            last.then_inc(g_pe, 1)
            e.wait_ge(g_act, GCS.after("v"))
            for h in range(GH):
                last = tr(out(5, h, P, n), heads("T1", n)[:, h])
            last.then_inc(g_pe, 1)
            e.wait_ge(g_act, GCS.after("vt"))
            for h in range(GH):
                mm(out(6, h, n), heads("vnew", P, n)[:, h], heads("qk", n, n)[:, h], True, False)
                for b in range(NB):
                    last = mm(bank(6, TS, P, h * n + TS * b), S_smp[:, b, h], heads("qeg", n)[:, h, TS * b:TS * b + TS], False, b == NB - 1)
            last.then_inc(g_pe, 1)
            e.wait_ge(g_act, GCS.after("o"))
            mm(bank(7, GH * n), ones, W["sq"][:, 0:GH * n]).then_inc(g_pe, 1)
            for h in range(GH):
                e.wait_ge(g_dve, GDS.after(f"vm{h}"))
                if h >= 2:
                    e.wait_ge(g_dve, GDS.after(f"add{h - 2}"))
                for q in range(2):
                    last = mm(bank(2 * (h % 2) + q), heads("kd", P, n)[:, h], vm[h % 2][:, 512 * q:512 * q + 512])
                last.then_inc(g_pe, 1)

            e.wait_ge(g_dve, GDS.end(1))
            e.wait_ge(c_in, 16 * 35)
            for k in range(2):
                for hc in range(2):
                    bk = 2 * k + hc
                    for jh in range(2):
                        u = 4 * k + 2 * hc + jh
                        e.wait_ge(w_ready[u % SLOTS], 16 * (R_CMP + u // SLOTS + 1))
                        for jj in range(16):
                            j = 16 * jh + jj
                            w = slot[u % SLOTS][:, jj]
                            mm(bank(bk, G * NCP), w, kvq[:, 2 * k:2 * k + 2, j:j + CS * (NCP - 1) + 1:CS], j == 0, j == CB - 1)
                            last = mm(bank(bk, 17 * NCS, P, G * NCP), w, seg_t[:, k, :, j:j + CS * (NCS - 1) + 1:CS],
                                      False, j == CB - 1)
                        last.then_inc(units, 1)
                e.wait_ge(units, U_CMP + 4 * k + 4)
                e.sem_inc(c_pe, 1)
            e.wait_ge(c_act, 1)
            for hc in range(2):
                last = mm(bank(4, NCOL), w2[:, 0, hc], hid[:, 0, hc], hc == 0, hc == 1)
            last.then_inc(c_pe, 1)
            e.wait_ge(c_act, 3)
            mm(bank(5, NCOL), ones, csq).then_inc(c_pe, 1)
            for g in range(G):
                for hc in range(2):
                    mm(bank(6, P, NCP, P * g), hid[:, 1, hc, NCP * g:NCP * (g + 1)], w2[:, 1, hc], hc == 0, hc == 1)
            for q in range(16):
                for hc in range(2):
                    c = G * NCP + NCS * q
                    last = mm(bank(q // 4, P, NCS, P * (q % 4)), hid[:, 1, hc, c:c + NCS], w2[:, 1, hc], hc == 0, hc == 1)
            last.then_inc(c_pe, 1)

            e.wait_ge(c_act, 5)
            for kind in range(2):
                for g in range(G):
                    for j in range(4):
                        last = tr(bank(2 * kind + g, P, P, P * j), kvq[:, 6 + 4 * kind + g, P * j:P * j + P])
            last.then_inc(v_pe, 1)

            e.wait_ge(v_act, 1)
            e.wait_ge(bf_in, 16)
            for h in range(QH):
                last = mm(bank(h), flip[:, 0:P], bfull[:, h])
            last.then_inc(turned_pe, 1)
            e.wait_ge(turned, 1)
            e.wait_ge(bs_in, 16 * REP)
            for g in range(G):
                last = mm(bank(g, KEYS, 16), flip[0:16, P:P + 16], biasS[:, g])
            last.then_inc(turned_pe, 1)

            e.wait_ge(c_dve, 1)
            e.wait_ge(turned, 2)
            for i in range(4):
                n = 7 + 8 * i
                if i > 0:
                    e.wait_ge(ac_dve, 2 * i)
                for h in range(QH):
                    last = mm(bank(4, n, P, NCP * h), kvq[:, N_A + h, P * i:P * i + P], kcT[:, NCP * (h // REP):NCP * (h // REP) + n])
                last.then_inc(ac_pe, 1)
                e.wait_ge(ac_dve, 2 * i + 2)
                if i > 0:
                    e.wait_ge(ac_act, 2 * i)
                for h in range(QH):
                    last = tr(bank(5 + h // 4, P, n, P * (h % 4)), sC[:, h, 0:n])
                last.then_inc(ac_pe, 1)
            e.wait_ge(ac_act, 8)

            def score(s):
                h, i = ATT[s]
                if s >= 2:
                    e.wait_ge(a_m, s - 1)
                for kind in range(2):
                    last = mm(bank(4 + 2 * (s % 2) + kind, P * (i + 1)), kvq[:, N_A + h, P * i:P * i + P],
                              kvq[:, 4 + 4 * kind + h // REP, 0:P * (i + 1)])
                last.then_inc(a_s, 1)

            def turn(s):
                h, i = ATT[s]
                for kind in range(2):
                    e.wait_ge(a_p, 2 * s + kind + 1)
                    if s >= 1:
                        e.wait_ge(a_pt, 2 * s + kind - 1)
                    for j in range(i + 1):
                        last = tr(bank(2 + kind, P, P, P * j), pS[s % 3][:, kind, P * j:P * j + P])
                    last.then_inc(a_t, 1)

            def values(s):
                h, i = ATT[s]
                y = bank(h % 2, P, P, P * i)
                if i == 0 and h >= 2:
                    e.wait_ge(a_ye, h - 1)
                n = 7 + 8 * i
                mm(y, vcP[0:n, h // REP], PTc[0:n, h, P * i:P * i + P], True, False)
                for kind in range(2):
                    e.wait_ge(a_pt, 2 * s + kind + 1)
                    for j in range(i + 1):
                        last = mm(y, VN[:, kind, h // REP, j], pT[s % 2][:, kind, P * j:P * j + P], False, kind == 1 and j == i)
                last.then_inc(a_y, 1)

            for s in range(len(ATT) + 3):
                if s < len(ATT):
                    score(s)
                if 2 <= s < len(ATT) + 2:
                    turn(s - 2)
                if s >= 3:
                    values(s - 3)

            for kind in range(3):
                for h in range(QH):
                    last = mm(bank(6 + kind // 2, NS, P, 256 * (kind % 2) + NS * h),
                              sm[0:NS, 4, QH * kind + h:QH * kind + h + 1].broadcast_to([NS, P]), ident[0:NS, 0:NS])
            last.then_inc(s_pe, 1)
            e.wait_ge(k_new, 1)
            e.wait_ge(a_ye, QH)
            for q in range(16):
                last = mm(bank(0, NCS, 16, NCS * q), qs[:, q // G, 16 * (q % G):16 * (q % G) + 16],
                          kcT[:, G * NCP + NCS * q:G * NCP + NCS * (q + 1)])
            last.then_inc(s_pe, 1)
            e.wait_ge(s_dve, 2)
            for q in range(16):
                last = tr(bank(1, 16, NCS, 16 * q), s_S.rearrange("p q k -> p (q k)")[:, NCS * q:NCS * q + NCS])
            last.then_inc(s_pe, 1)
            e.wait_ge(s_act, 3)
            for q in range(16):
                last = mm(bank(2, 16, P, 16 * q), vcS[:, q], s_PT[0:NCS, 16 * q:16 * q + 16])
            last.then_inc(s_pe, 1)
            for p in range(4):
                kind, bh = p // 2, p % 2
                e.wait_ge(s_dve, 3 * p + 3)
                e.wait_ge(k_new, p + 2)
                e.wait_ge(kv_in[bh], 16 * 16 * (kind + 1))
                for q in range(8):
                    last = mm(bank(q, KEYS, 16), qs[:, 4 * bh + q // G, 16 * (q % G):16 * (q % G) + 16], kbuf[bh][:, q // G, q % G])
                last.then_inc(s_pe, 1)
                e.wait_ge(s_dve, 3 * p + 4)
                for q in range(8):
                    c = TP + TS * (4 * bh + q // G)
                    last = tr(bank(2 + q // 4, P, TS, P * (q % 4)), kvq[:, 6 + 4 * kind + q % G, c:c + TS])
                last.then_inc(s_pe, 1)
                e.wait_ge(s_dve, 3 * p + 5)
                for q in range(8):
                    for j in range(2):
                        tr(bank(0, 16, P, 32 * q + 16 * j), s_S[:, q, P * j:P * j + P])
                    last = tr(bank(1, 16, TS, 16 * q), s_S[:, q, PAST:KEYS])
                last.then_inc(s_pe, 1)
                e.wait_ge(s_act, 5 + 2 * p)
                for q in range(8):
                    for j in range(2):
                        mm(bank(4, 16, P, 16 * q), vbuf[bh][:, q // G, j, q % G], s_PT[:, 32 * q + 16 * j:32 * q + 16 * j + 16], j == 0, False)
                    last = mm(bank(4, 16, P, 16 * q), s_VN[:, q], s_PN[:, 16 * q:16 * q + 16], False, True)
                last.then_inc(s_pe, 1)

            e.wait_ge(s_dve, 16)
            group_norm(1)
            group_norm(2)

            e.wait_ge(n_lo, SPLIT_0[3])
            unit(0, H_OUT, 0)
            unit(0, H_OUT + 2, 2)
            with e.Fori(1, KC // 2) as i:
                for s in range(2):
                    e.wait_ge(h_add, 2 * i + s - 1)
                    unit(i, H_OUT + 2 * s, 2 * s)
            group_norm(3)

            e.wait_ge(n_lo, SPLIT_0[3] + 16)
            unit(0, H_UP, 0)
            unit(0, H_UP + 2, 2)
            with e.Fori(1, FC) as i:
                for s in range(2):
                    e.wait_ge(up_evac, 2 * i + s - 1)
                    unit(i, H_UP + 2 * s, 2 * s)

            def down_unit(banks, s):
                for k in range(DT):
                    c = DT * DN_ORDER[s] + k
                    lo, hi = halves(act_first[:, c] if c < SPILL else act[:, c - SPILL])
                    start, stop = s == 0 and k == 0, s == DU - 1 and k == DT - 1
                    mm(bank(banks, 256), slot[s][:, k], lo, start, stop)
                    last = mm(bank(banks + 1, NT - 256), slot[s][:, k], hi, start, stop)
                last.then_inc(units, 1)

            e.wait_ge(up_act, FC)
            e.wait_ge(up_evac, 2 * FC)
            def down(i, first):
                for d in range(2):
                    if not first:
                        e.wait_ge(dn_evac, 2 * i + d - 1)
                    for s in range(DU):
                        if first and d == 0 and s == 2:
                            e.wait_ge(act_in, 16)
                        e.wait_ge(w_ready[s], 32 * i + 16 * (R_DN + d + 1))
                        down_unit(2 * d, s)
            down(0, True)
            with e.Fori(1, KC // 2) as i:
                down(i, False)

        @block.scalar
        def _(e):
            n_chain = [0]

            def link(ins):
                n_chain[0] += 1
                ins.then_inc(a_chain, 1)
                e.wait_ge(a_chain, n_chain[0])

            def ln_exp():
                e.preload_act_table_set("natural_log_exp_and_others")

            def rstd(out, sums, scale, eps):
                link(e.activation(out, sums, ACT.Ln, bias=eps, scale=scale))
                return e.activation(out, out, ACT.Exp, scale=-0.5)

            def two_banks(b, n=NT):
                return bank(b, 256), bank(b + 1, NT - 256)

            def rstd_row(out, banks, scale, eps):
                lo, hi = halves(out)
                a, b = two_banks(banks)
                e.activation(lo, a, ACT.Ln, bias=eps, scale=scale)
                link(e.activation(hi, b, ACT.Ln, bias=eps, scale=scale))
                return e.activation(out, out, ACT.Exp, scale=-0.5)

            def group_norm(g):
                ln_exp()
                src = GROUPS[g][0]
                for k in range(GROUP_N[g]):
                    c = GROUP_0[g] + k
                    if k >= 2:
                        e.wait_ge(n_mm, c - 1)
                    e.activation(nrm_sq[k % 2], src[:, k], ACT.Square).then_inc(n_sq, 1)
                e.wait_ge(n_mm, GROUP_0[g] + GROUP_N[g])
                if g > 0:
                    e.wait_ge(n_mul, SPLIT_0[g])
                rstd_row(rs1, 4, 1.0 / (GROUP_N[g] * P), eps1).then_inc(n_rs, 1)
                for k in range(GROUP_N[g]):
                    e.wait_ge(n_mul, SPLIT_0[g] + k + 1)
                    e.activation(xhi[:, GROUPS[g][1] + k], tn[k % 4], ACT.Copy).then_inc(n_hi, 1)

            def split(i, h, extra=0, first=False):
                e.wait_ge(w_ready[h % SLOTS], 16 * i + 16 * (h // SLOTS + 1 + extra))
                if not first:
                    u = 2 * i + h // 2
                    e.wait_ge(units if h % 2 else used, u + 8 if h % 2 and extra else u)
                e.activation(whi[h % 2], raw[h % SLOTS], ACT.Copy).then_inc(w_hi, 1)

            e.dma_start(relb, A["rel_bias"]).then_inc(s_tab, 16)
            e.dma_start(onehot, A["onehot"]).then_inc(s_tab, 16)
            e.dma_start(negt, A["neg"]).then_inc(s_tab, 16)
            e.wait_ge(t_dve, 1)
            e.dma_start(table_dram, tabs).then_inc(t_out, 16)
            e.dma_start(O["win_old"], A["cache_win"]).then_inc(stored, 16)
            e.wait_ge(t_out, 16)
            for r in range(REP):
                src = bass.AP(table_dram.tensor, r * TAB + PAST - TS, [[1, TS], [REP * TAB, G], [1, KEYS]])
                e.dma_start(biasS[TS * r:TS * r + TS], src).then_inc(bs_in, 16)

            e.wait_ge(s_cst, 16 * 8)
            e.wait_ge(s_x, 64)
            split(0, 0, first=True)
            split(0, 1, first=True)
            group_norm(0)

            def copy_chunk(banks, dst, func=ACT.Copy):
                lo, hi = halves(dst)
                a, b = two_banks(banks)
                e.activation(lo, a, func)
                return e.activation(hi, b, func)

            for c in range(N_A):
                split(0, 2 * c + 2)
                split(0, 2 * c + 3)
                e.wait_ge(units, c + 1)
                copy_chunk(2 * (c % 2), abuf[:, c]).then_inc(proj_evac, 1)
            with e.Fori(0, N_KVQ // 2) as i:
                for s in range(2):
                    split(i, 2 * N_A + 2 * s + 2)
                    split(i, 2 * N_A + 2 * s + 3)
                    e.wait_ge(units, 2 * i + s + N_A + 1)
                    lo, hi = halves(at(KVQ, N_KVQ * NT).rearrange("p (k t) -> p k t", k=N_KVQ)[:, 2 * i + s])
                    e.activation(lo, bank(2 * s, 256), ACT.Copy)
                    e.activation(hi, bank(2 * s + 1, NT - 256), ACT.Copy).then_inc(proj_evac, 1)
            e.wait_ge(a_free, 1)
            for c in range(N_A):
                split(0, 2 * (N_A + N_KVQ + c) + 2)
                split(0, 2 * (N_A + N_KVQ + c) + 3)
                e.wait_ge(units, N_A + N_KVQ + c + 1)
                a, b = two_banks(2 * (c % 2))
                e.activation(gbuf[:, c, 3:3 + 256], a, ACT.Copy)
                e.activation(gbuf[:, c, 3 + 256:3 + TP], b[:, 0:256], ACT.Copy)
                e.activation(gbuf[:, c, 3 + TP:ROW4].rearrange("p (b n) -> p b n", n=SEG4)[:, :, 3:SEG4],
                             b[:, 256:NT - 256].rearrange("p (b t) -> p b t", t=TS), ACT.Copy).then_inc(proj_evac, 1)
            e.wait_ge(ya_out, 16)
            for c in range(GH):
                if c + 1 < GH:
                    split(0, 2 * (PROJ - GH + c) + 2)
                    split(0, 2 * (PROJ - GH + c) + 3)
                e.wait_ge(units, PROJ - GH + c + 1)
                copy_chunk(2 * (c % 2), zbuf[:, c], ACT.Silu).then_inc(proj_evac, 1)

            def silu_rows(i, s):
                e.wait_ge(gconv_dve, 8 * i + 4 * s + 4)
                c = ut[:, 2 * i + s]
                e.activation(c[:, 0:TP], cacc[s][:, 0:TP], ACT.Silu)
                e.activation(smp(c), at(XN + N_A * NT + s * ROW4 + TP + 3, NB * SEG4).rearrange("p (b n) -> p b n", n=SEG4)[:, :, 0:TS],
                             ACT.Silu).then_inc(gconv_act, 1)
            with e.Fori(0, N_A // 2) as i:
                silu_rows(i, 0)
                silu_rows(i, 1)

            def head_square(t):
                if t >= 2:
                    e.wait_ge(nh_mm, t - 1)
                e.activation(hn_sq[t % 2], HEADS[t][0], ACT.Square).then_inc(nh_sq, 1)
            e.wait_ge(gconv_act, N_A)
            e.wait_ge(proj_evac, PROJ)
            e.wait_ge(tails, 2)
            ln_exp()
            head_square(0)
            for t in range(len(HEADS)):
                if t + 1 < len(HEADS):
                    head_square(t + 1)
                e.wait_ge(nh_mm, t + 1)
                if t >= 2:
                    e.wait_ge(nh_mul, t - 1)
                rstd_row(hn_rs[t % 2], 2 * (t % 2), HEADS[t][2], HEADS[t][3]).then_inc(nh_rs, 1)
            e.wait_ge(nh_mul, len(HEADS))
            e.dma_start(O["kv_t"], kvq[:, 0:N_A]).then_inc(stored, 16)

            e.wait_ge(g_dve, 1)
            e.activation(sm[:, :, 0:24], sm[:, :, 0:24], ACT.Sigmoid)
            link(e.activation(sm[:, :, 28:32], sm[:, :, 28:32], ACT.Sigmoid))
            e.sem_inc(g_act, 1)
            ln_exp()
            e.wait_ge(g_dve, 2)
            link(e.activation(soft2, soft2, ACT.Exp))
            e.activation(soft2, soft2, ACT.Ln, bias=one)
            e.activation(gdn_in[:, 0:4], gdn_in[:, 0:4], ACT.Exp).then_inc(g_act, 1)
            e.wait_ge(g_dve, 4)
            e.activation(egc, gc, ACT.Exp)
            e.activation(ekd, ekd, ACT.Exp).then_inc(g_act, 1)

            for t in range(4):
                e.wait_ge(r_dec, t + 1)
                e.activation(W[DEC[t % 2]], W[DEC[t % 2]], ACT.Exp)
                e.activation(W[EG[t % 2]], bank(4 * (t % 2)), ACT.Exp).then_inc(r_exp, 1)
            for m in range(len(LEVELS)):
                e.wait_ge(l_t1p, m + 1)
                if m >= 2:
                    e.wait_ge(l_t2, m - 1)
                e.activation(W[T1[m % 2]], bank(m % 2), ACT.Copy).then_inc(l_t1c, 1)
            def w_negated(t):
                e.wait_ge(q_w, t + 1)
                if t >= 1:
                    e.wait_ge(q_v, t)
                e.activation(W["nwT"], bank(3), ACT.Copy, scale=-1.0).then_inc(q_nw, 1)

            w_negated(0)
            for t in range(4):
                e.wait_ge(q_v, t + 1)
                if t > 0:
                    e.wait_ge(q_o, t)
                e.activation(W["vnew"], bank(4), ACT.Copy).then_inc(q_vn, 1)
                e.wait_ge(q_o, t + 1)
                if t > 0:
                    e.wait_ge(q_y, t)
                    e.wait_ge(q_n, t)
                e.activation(W["oT"], bank(5), ACT.Copy)
                e.activation(W["sq"], bank(5), ACT.Square).then_inc(q_oc, 1)
                if t < 3:
                    w_negated(t + 1)
                e.wait_ge(q_n, t + 1)
                rstd(W["rs"], bank(7), 1.0 / P, eps1).then_inc(q_rs, 1)

            n, w = NS, GH * NS
            e.wait_ge(g_dve, GDS.after("dec"))
            e.activation(W["decT"][0:n, 0:w], W["decT"][0:n, 0:w], ACT.Exp)
            e.activation(W["eg"][:, 0:w], bank(0, w), ACT.Exp).then_inc(g_act, 1)
            e.wait_ge(g_pe, GPS.after("nat"))
            for h in range(GH):
                c = 16 + h
                e.activation(heads("vb", P, n)[:, h], bank(5, P, n, P * h), ACT.Copy, scale=sm[0:n, 4, 28 + h:29 + h])
                e.activation(heads("kbeg", P, n)[:, h], bank(4, P, n, P * h), ACT.Copy, scale=beg[0:n, c:c + 1])
                last = e.activation(heads("kd", P, n)[:, h], bank(4, P, n, P * h), ACT.Copy, scale=ekd[0:n, c:c + 1])
            last.then_inc(g_act, 1)
            for s in range(LVS):
                e.wait_ge(g_pe, GPS.after(f"t1_{s}"))
                e.activation(W["T1"][0:n, 0:w], bank(0, w, n), ACT.Copy).then_inc(g_act, 1)
            e.wait_ge(g_pe, GPS.after("w"))
            e.activation(W["nwT"][:, 0:w], bank(3, w), ACT.Copy, scale=-1.0).then_inc(g_act, 1)
            e.wait_ge(g_pe, GPS.after("v"))
            e.activation(W["T1"][:, 0:w], bank(4, w), ACT.Copy).then_inc(g_act, 1)
            e.wait_ge(g_pe, GPS.after("vt"))
            e.activation(W["vnew"][0:n], bank(5, 512, n), ACT.Copy).then_inc(g_act, 1)
            e.wait_ge(g_pe, GPS.after("o"))
            e.activation(W["oT"][:, 0:w], bank(6, w), ACT.Copy)
            e.activation(W["sq"][:, 0:w], bank(6, w), ACT.Square).then_inc(g_act, 1)
            e.wait_ge(g_pe, GPS.after("n"))
            rstd(W["rs"][:, 0:w], bank(7, w), 1.0 / P, eps1).then_inc(g_act, 1)

            for k in range(2):
                e.wait_ge(c_pe, k + 1)
                for hc in range(2):
                    link(e.activation(pebs[:, 2 * k + hc:2 * k + hc + 1], bank(2 * k + hc, 1, P, NCOL), ACT.Copy))
                    last = e.activation(hid[:, k, hc], bank(2 * k + hc, NCOL), ACT.Gelu_apprx_tanh, bias=pebs[:, 2 * k + hc:2 * k + hc + 1])
                last.then_inc(c_act, 1)
            ln_exp()
            e.wait_ge(c_pe, 3)
            e.activation(kcT, bank(4, NCOL), ACT.Copy)
            e.activation(csq, bank(4, NCOL), ACT.Square).then_inc(c_act, 1)
            e.wait_ge(c_pe, 4)
            rstd(crs, bank(5, NCOL), 1.0 / P, eps1).then_inc(c_act, 1)
            e.wait_ge(c_pe, 5)
            for g in range(G):
                e.activation(vcP[:, g], bank(6, P, NCP, P * g), ACT.Copy)
            e.activation(vcS.rearrange("p q d -> p (q d)"), ps[0:NCS, 0:2048], ACT.Copy).then_inc(c_act, 1)

            e.wait_ge(c_dve, 1)
            e.wait_ge(c_act, 5)
            e.wait_ge(gdn_stored, 64)
            src = bass.AP(table_dram.tensor, 0, [[1, P], [TAB, QH], [1, 512]])
            e.dma_start(bfull, src).then_inc(bf_in, 16)
            e.wait_ge(v_pe, 1)
            for b in range(4):
                last = e.activation(VN[:, b // 2, b % 2].rearrange("p j d -> p (j d)"), bank(b), ACT.Copy)
            last.then_inc(v_act, 1)
            e.wait_ge(turned_pe, 1)
            for h in range(QH):
                last = e.activation(bfull[:, h], bank(h), ACT.Copy)
            last.then_inc(turned, 1)
            e.wait_ge(turned_pe, 2)
            for g in range(G):
                last = e.activation(biasS[:, g], bank(g, KEYS, 16), ACT.Copy)
            last.then_inc(turned, 1)

            for i in range(4):
                n = 7 + 8 * i
                e.wait_ge(ac_dve, 2 * i + 1)
                e.activation(sC[:, :, 0:n], sC[:, :, 0:n], ACT.Exp).then_inc(ac_act, 1)
                e.wait_ge(ac_pe, 2 * i + 2)
                for q in range(2):
                    last = e.activation(PTc[0:n, 4 * q:4 * q + 4, P * i:P * i + P],
                                        bank(5 + q, 512, n).rearrange("p (h t) -> p h t", h=4), ACT.Copy)
                last.then_inc(ac_act, 1)

            def exps(s):
                h, i = ATT[s]
                e.wait_ge(a_m, s + 1)
                for kind in range(2):
                    x, c = pS[s % 3][:, kind, 0:P * (i + 1)], 2 * (s % 2) + kind
                    last = e.activation(x, x, ACT.Exp, bias=mx[:, c:c + 1], accum_out=zz[:, c:c + 1])
                last.then_inc(a_e, 1)

            def copies(s):
                h, i = ATT[s]
                n = P * (i + 1)
                if s >= 2:
                    e.wait_ge(a_y, s - 1)
                for kind in range(2):
                    e.wait_ge(a_t, 2 * s + kind + 1)
                    e.activation(pT[s % 2][:, kind, 0:n], bank(2 + kind, n), ACT.Copy).then_inc(a_pt, 1)

            def head_out(h):
                e.wait_ge(a_y, 4 * h + 4)
                e.activation(mix[:, 4 + h, 0:TP], bank(h % 2), ACT.Copy).then_inc(a_ye, 1)

            for s in range(len(ATT) + 2):
                if s < len(ATT):
                    exps(s)
                if s >= 2:
                    copies(s - 2)
                if s >= 7 and s % 4 == 3:
                    head_out((s - 7) // 4)
            head_out(QH - 1)

            e.wait_ge(s_pe, 1)
            for kind in range(3):
                link(e.activation(grow[:, kind].rearrange("p (b h t) -> p b h t", b=NB, h=QH),
                                  bank(6 + kind // 2, 256, P, 256 * (kind % 2)).rearrange("p (h b t) -> p b h t", h=QH, b=NB), ACT.Copy))
            e.sem_inc(s_act, 1)
            sC2 = s_S.rearrange("p q k -> p (q k)")[:, 0:16 * NCS]
            e.wait_ge(s_dve, 1)
            e.activation(sC2, sC2, ACT.Exp).then_inc(s_act, 1)
            e.wait_ge(s_pe, 3)
            e.activation(s_PT[0:NCS, 0:256], bank(1, 256, NCS), ACT.Copy).then_inc(s_act, 1)
            for p in range(4):
                e.wait_ge(s_dve, 3 * p + 4)
                e.activation(s_S, s_S, ACT.Exp).then_inc(s_act, 1)
                e.wait_ge(s_pe, 4 * p + 7)
                e.activation(s_PT, bank(0, 256), ACT.Copy)
                e.activation(s_PN, bank(1, P, TS), ACT.Copy)
                e.activation(s_VN.rearrange("p q d -> p (q d)"), ps[0:TS, 1024:2048], ACT.Copy).then_inc(s_act, 1)

            e.wait_ge(ya_in, 16)
            group_norm(1)
            group_norm(2)

            for c in range(4):
                e.wait_ge(n_mul, SPLIT_0[3] - 3 + c)
                e.activation(xhi[:, 12 + c], tn[c], ACT.Copy).then_inc(n_hi, 1)
            for c in range(2):
                e.dma_start(xin[c], A["x_t"][:, c]).then_inc(x_in[c], 16)
            for dst, name in ((hist, "hist_f"), (fw, "ffn_w")):
                e.dma_start(dst, A[name]).then_inc(f_in, 16)
            for h in range(SLOTS):
                split(0, H_OUT + h, R_OUT - R_CMP)
            with e.Fori(1, KC // 2) as i:
                for c in range(2):
                    split(i, H_OUT + 2 * c, R_OUT - R_CMP)
                    split(i, H_OUT + 2 * c + 1, R_OUT - R_CMP)
                    e.wait_ge(h_add, 2 * i + c - 1)
                    e.dma_start(xin[c], A["x_t"][:, 2 * i + c]).then_inc(x_in[c], 16)
            split(0, H_UP, R_OUT - R_CMP)
            split(0, H_UP + 1, R_OUT - R_CMP)
            e.wait_ge(h_add, KC)
            e.dma_start(h_dram, hbuf).then_inc(h_out, 16)
            group_norm(3)

            e.wait_ge(n_lo, SPLIT_0[3] + 16)
            def up(i, first, last=False):
                for q in range(SLOTS):
                    u = SLOTS * i + q
                    if not (last and q == SLOTS - 1):
                        split(2 * i, H_UP + 2 * q + 2, R_OUT - R_CMP)
                        split(2 * i, H_UP + 2 * q + 3, R_OUT - R_CMP)
                    e.wait_ge(units, u + (U_UP + 1))
                    if not first:
                        e.wait_ge(up_conv, 3 * u - 9)
                        e.wait_ge(up_tail, u - 3)
                    prompt, sample = rows3(fx[q])
                    a, b = two_banks(2 * (q % 2))
                    e.activation(prompt[:, 0:256], a, ACT.Copy)
                    e.activation(prompt[:, 256:TP], b[:, 0:256], ACT.Copy)
                    e.activation(sample, b[:, 256:NT - 256].rearrange("p (b t) -> p b t", t=TS), ACT.Copy).then_inc(up_evac, 1)
                    if q % 2:
                        e.wait_ge(up_conv, 3 * u)
                        e.activation(facc[q - 1], facc[q - 1], ACT.Silu).then_inc(up_silu, 1)
            up(0, True)
            with e.Fori(1, FC // 2 - 1) as i:
                up(i, False)
            up(FC // 2 - 1, False, True)
            e.wait_ge(units, U_DN)
            for q in range(2):
                e.wait_ge(act_out[q], 16 * (SPILL // 2))
            e.dma_start(act_first, act_dram).then_inc(act_in, 16)
            e.wait_ge(up_tail, 2 * FC)
            e.dma_start(O["tail_f"], tail).then_inc(stored, 16)

            e.wait_ge(h_out, 16)
            e.wait_ge(up_act, FC)
            for c in range(2):
                e.dma_start(hin[c], h_dram[:, c]).then_inc(h_in[c], 16)
            with e.Fori(0, KC // 2 - 1) as i:
                for c in range(2):
                    e.wait_ge(dn_evac, 2 * i + c + 1)
                    e.dma_start(O["y_t"][:, 2 * i + c], yout[c]).then_inc(y_out[c], 16)
                    e.dma_start(hin[c], h_dram[:, 2 * i + c + 2]).then_inc(h_in[c], 16)
            for c in range(2):
                e.wait_ge(dn_evac, KC - 1 + c)
                e.dma_start(O["y_t"][:, KC - 2 + c], yout[c]).then_inc(y_out[c], 16)

        @block.vector
        def _(e):
            n_chain = [0]

            def link(ins):
                n_chain[0] += 1
                ins.then_inc(d_chain, 1)
                e.wait_ge(d_chain, n_chain[0])

            def group_norm(g):
                src, c0, col = GROUPS[g]
                e.wait_ge(n_rs, g + 1)
                for k in range(GROUP_N[g] + 1):
                    if k < GROUP_N[g]:
                        e.scalar_tensor_tensor(out=tn[k % 4], in0=src[:, k], scalar=gain[:, col + k:col + k + 1], in1=rs1,
                                               op0=ALU.mult, op1=ALU.mult).then_inc(n_mul, 1)
                    if k >= 1:
                        e.wait_ge(n_hi, SPLIT_0[g] + k)
                        e.tensor_tensor(xlo[:, c0 + k - 1], tn[(k - 1) % 4], xhi_f[:, c0 + k - 1], ALU.subtract).then_inc(n_lo, 1)

            def split(i, h):
                e.wait_ge(w_hi, SLOTS * i + (h + 1))
                e.tensor_tensor(wlo[h % 2], raw[h % SLOTS], whi_f[h % 2], ALU.subtract).then_inc(w_lo, 1)

            e.memset(xa[:, 0:2], 0.0)
            e.memset(gc, 0.0)
            e.memset(gl, 0.0)
            link(e.memset(sm.rearrange("p c n -> p (c n)"), 0.0))
            e.wait_ge(t_pe, 1)
            e.wait_ge(s_tab, 48)
            e.tensor_tensor(tabs[:, 0:320], bank(6, 320, QH), negt[:, 0:320], ALU.add)
            e.tensor_tensor(tabs[:, 320:TAB], bank(7, 320, QH), negt[:, 320:TAB], ALU.add).then_inc(t_dve, 1)

            e.wait_ge(s_cst, 16 * 8)
            e.wait_ge(s_x, 64)
            split(0, 0)
            split(0, 1)
            group_norm(0)

            e.wait_ge(n_mul, 16)
            up_, us_ = rows3(xa)
            for j in range(4):
                for h in range(6):
                    split(0, 6 * j + 2 + h)
                e.wait_ge(proj_evac, 3 * j + 3)
                cc, hh, bb = abuf[:, 3 * j], abuf[:, 3 * j + 1], abuf[:, 3 * j + 2]
                e.tensor_copy(xa[:, 2 + TP:ROW3].rearrange("p (b n) -> p b n", n=SEG3)[:, :, 0:2], hist_a[:, j])
                e.tensor_tensor(up_, cc[:, 0:TP], hh[:, 0:TP], ALU.mult)
                link(e.tensor_tensor(us_, smp(cc), smp(hh), ALU.mult))
                e.tensor_copy(tail_a[:, j, 0:2], xa[:, TP:TP + 2])
                e.tensor_copy(tail_a[:, j, 2:18].rearrange("p (b k) -> p b k", k=2), us_[:, :, 2:4])
                link(e.tensor_scalar(acc_a, xa[:, 0:ROW3 - 2], aw[:, j, 0:1], None, ALU.mult))
                for k in (1, 2):
                    link(e.scalar_tensor_tensor(out=acc_a, in0=xa[:, k:ROW3 - 2 + k], scalar=aw[:, j, k:k + 1], in1=acc_a,
                                                op0=ALU.mult, op1=ALU.add))
                e.tensor_tensor(zbuf[:, j, 0:TP], acc_a[:, 0:TP], bb[:, 0:TP], ALU.mult)
                link(e.tensor_tensor(smp(zbuf[:, j]), at(BF + 512 + ROW3 + 2 + TP, NB * SEG3).rearrange("p (b n) -> p b n", n=SEG3)[:, :, 0:TS],
                                     smp(bb), ALU.mult))
            e.sem_inc(a_free, 1)
            e.sem_inc(tails, 1)
            split(0, 2 * N_A + 2)
            split(0, 2 * N_A + 3)
            with e.Fori((N_A + 2) // 2, PROJ // 2) as i:
                for h in range(SLOTS):
                    split(i, h)

            e.wait_ge(gconv_in, 1)
            e.wait_ge(proj_evac, PROJ - GH)
            e.wait_ge(units, PROJ)
            e.wait_ge(gates_mm, 1)
            def gconv(i, s, first):
                if not first:
                    e.wait_ge(gconv_act, 2 * i + s - 1)
                g = gbuf[:, 2 * i + s]
                e.tensor_scalar(cacc[s], g[:, 0:ROW4 - 3], gw[:, 2 * i + s, 0:1], None, ALU.mult).then_inc(gconv_dve, 1)
                for k in (1, 2, 3):
                    e.wait_ge(gconv_dve, 8 * i + 4 * s + k)
                    e.scalar_tensor_tensor(out=cacc[s], in0=g[:, k:ROW4 - 3 + k], scalar=gw[:, 2 * i + s, k:k + 1], in1=cacc[s],
                                           op0=ALU.mult, op1=ALU.add).then_inc(gconv_dve, 1)
            gconv(0, 0, True)
            gconv(0, 1, True)
            with e.Fori(1, N_A // 2) as i:
                gconv(i, 0, False)
                gconv(i, 1, False)

            for t, (rows, col, _, _) in enumerate(HEADS):
                e.wait_ge(nh_rs, t + 1)
                if col is None:
                    e.tensor_tensor(rows, rows, hn_rs[t % 2], ALU.mult).then_inc(nh_mul, 1)
                else:
                    e.scalar_tensor_tensor(out=rows, in0=rows, scalar=gain[:, col:col + 1], in1=hn_rs[t % 2],
                                           op0=ALU.mult, op1=ALU.mult).then_inc(nh_mul, 1)

            e.wait_ge(gates_mm, 1)
            e.tensor_copy(sm[:, 0:4, :], bank(6, 128).rearrange("p (c n) -> p c n", n=32))
            link(e.tensor_copy(sm[0:NS, 4, :], bank(6, 32, NS, 128)))
            e.sem_inc(g_dve, 1)
            s5 = soft.rearrange("p (c h) -> p c h", h=GH)
            link(e.tensor_tensor(s5, sm[:, :, 24:28], gdn_in[:, 4:8].unsqueeze(1).broadcast_to([P, 5, GH]), ALU.add))
            e.scalar_tensor_tensor(out=soft2, in0=soft, scalar=-1.0, in1=soft, op0=ALU.mult, op1=ALU.min).then_inc(g_dve, 1)
            e.wait_ge(g_act, 2)
            link(e.scalar_tensor_tensor(out=soft, in0=soft, scalar=0.0, in1=soft2, op0=ALU.max, op1=ALU.add))
            e.scalar_tensor_tensor(out=gdec.rearrange("p (c h) -> p c h", h=GH), in0=s5, scalar=-1.0,
                                   in1=gdn_in[:, 0:4].unsqueeze(1).broadcast_to([P, 5, GH]), op0=ALU.mult, op1=ALU.mult).then_inc(g_dve, 1)
            e.wait_ge(g_pe, 1)
            e.tensor_copy(gc[:, 0:16], bank(7, 16))
            e.tensor_copy(gc[0:NS, 16:20], bank(7, 4, NS, 16))
            e.tensor_copy(gl[:, 0:16], bank(7, 16, P, 32))
            link(e.tensor_copy(gl[0:NS, 16:20], bank(7, 4, NS, 48)))
            e.tensor_tensor(ekd, gl, gc, ALU.subtract).then_inc(g_dve, 1)
            e.wait_ge(g_act, 3)
            link(e.memset(W["S"], 0.0))
            e.tensor_tensor(beg.rearrange("p (c h) -> p c h", h=GH), egc.rearrange("p (c h) -> p c h", h=GH), sm[:, :, 28:32],
                            ALU.mult).then_inc(g_dve, 1)

            def b3(i, n, parts=P):
                return bank(i, GH * n, parts).rearrange("p (h i) -> p h i", h=GH)

            def decay(t, n, b, dst):
                for h in range(GH):
                    last = e.tensor_scalar(heads(dst, n, n)[:, h], bank(b, n, n, n * h), gc[0:n, 4 * t + h:4 * t + h + 1], 0.0,
                                           ALU.subtract, ALU.min)
                return last

            def decayed(t, n, b, dec, eg):
                mtri = (tri if t < 4 else cst[0:n, C_TRIB:C_TRIB + n]).unsqueeze(1).broadcast_to([n, GH, n])
                idb = ident[0:n, 0:n].unsqueeze(1).broadcast_to([n, GH, n])
                qk = heads(of("qk", t), n, n)
                e.tensor_tensor(heads(of("qeg", t), n), ut[:, 0:GH, P * t:P * t + n], heads(eg, n), ALU.mult)
                link(e.tensor_tensor(qk, b3(b + 3, n, n), heads(dec, n, n), ALU.mult))
                e.scalar_tensor_tensor(out=heads(of("nl", t), n, n), in0=b3(b + 2, n, n), scalar=-1.0, in1=heads(dec, n, n),
                                       op0=ALU.mult, op1=ALU.mult)
                e.tensor_tensor(qk, qk, mtri, ALU.mult)
                e.tensor_copy(heads(of("X", t), n, n), idb)
                return e.tensor_copy(heads(of("XT", t), n, n), idb)

            def level_mask(s, n):
                return cst[0:n, C_LEV + P * s:C_LEV + P * s + n].unsqueeze(1).broadcast_to([n, GH, n])

            for t in range(5):
                if t < 4:
                    e.wait_ge(r_rows, t + 1)
                    if t >= 2:
                        e.wait_ge(r_low, t - 1)
                        e.wait_ge(r_gram, t - 1)
                    decay(t, P, 4 * (t % 2), DEC[t % 2]).then_inc(r_dec, 1)
                    e.tensor_tensor(heads(KB[t % 2]), ut[:, GH:2 * GH, P * t:P * t + P], b3(4 * (t % 2) + 1, P), ALU.mult).then_inc(r_kb, 1)
                if t >= 1:
                    u = t - 1
                    e.wait_ge(r_exp, u + 1)
                    e.wait_ge(r_gram, u + 1)
                    e.tensor_copy(egl[:, 4 * u:4 * u + 4], heads(EG[u % 2])[:, :, P - 1])
                    decayed(u, P, 4 * (u % 2), DEC[u % 2], EG[u % 2]).then_inc(r_low, 1)

            def masked(m):
                s, t = LEVELS[m]
                if m >= 2:
                    e.wait_ge(l_t1p, m - 1)
                e.tensor_tensor(heads(CT[m % 2]), heads(of("nl", t)), level_mask(s, P), ALU.mult).then_inc(l_ct, 1)

            e.wait_ge(r_low, 4)
            masked(0)
            for m in range(len(LEVELS)):
                s, t = LEVELS[m]
                if m + 1 < len(LEVELS):
                    masked(m + 1)
                e.wait_ge(l_t2, m + 1)
                if m >= 4:
                    e.wait_ge(l_x, m - 3)
                b = 512 * (2 + 2 * (m % 3))
                x, y = (XX[t], ps[:, b:b + 1024]) if s < LV - 1 else (W[of("XT", t)], ps[:, b + 512:b + 1024])
                e.tensor_tensor(x, x, y, ALU.add).then_inc(l_x, 1)

            def scaled(t):
                e.wait_ge(q_nat, t + 1)
                if t >= 2:
                    e.wait_ge(q_o, t - 1)
                e.tensor_tensor(heads(KBEG[t % 2]), b3(0, P), beg[:, 4 * t:4 * t + 4].unsqueeze(2).broadcast_to([P, GH, P]), ALU.mult)
                e.tensor_tensor(heads(KD[t % 2]), b3(0, P), ekd[:, 4 * t:4 * t + 4].unsqueeze(2).broadcast_to([P, GH, P]), ALU.mult)
                e.tensor_tensor(heads(VB[t % 2]), b3(1, P), sm[:, t, 28:32].unsqueeze(2).broadcast_to([P, GH, P]), ALU.mult).then_inc(q_vk, 1)

            def y_c(t, n):
                w = GH * n
                link(e.scalar_tensor_tensor(out=W["oT"][:, 0:w], in0=W["oT"][:, 0:w], scalar=gain[:, G_GDN:G_GDN + 1], in1=W["rs"][:, 0:w],
                                            op0=ALU.mult, op1=ALU.mult))
                return e.tensor_tensor(mix[:, 12:16, P * t:P * t + n], heads("oT", n), zbuf[:, :, P * t:P * t + n], ALU.mult)

            scaled(0)
            for t in range(4):
                if t < 3:
                    scaled(t + 1)
                e.wait_ge(q_o, t + 1)
                if t > 0:
                    e.wait_ge(q_s, t)
                for h in range(GH):
                    last = e.scalar_tensor_tensor(out=heads("S")[:, h], in0=heads("S")[:, h], scalar=egl[:, 4 * t + h:4 * t + h + 1],
                                                  in1=bank(6, P, P, P * h), op0=ALU.mult, op1=ALU.add)
                last.then_inc(q_s, 1)
                e.wait_ge(q_rs, t + 1)
                y_c(t, P).then_inc(q_y, 1)

            n, w = NS, GH * NS
            e.wait_ge(g_pe, GPS.after("rows"))
            e.wait_ge(q_y, 4)
            decay(4, n, 0, "decT").then_inc(g_dve, 1)
            e.tensor_tensor(heads("kbT", n), ut[:, GH:2 * GH, TP:NT], b3(1, n), ALU.mult).then_inc(g_dve, 1)
            e.wait_ge(g_act, GCS.after("dec"))
            e.wait_ge(g_pe, GPS.after("gram"))
            link(decayed(4, n, 0, "decT", "eg"))
            e.sem_inc(g_dve, 2)
            for s in range(LVS):
                link(e.tensor_tensor(heads("CT", n, n), heads("nl", n, n), level_mask(s, n), ALU.mult))
                e.sem_inc(g_dve, 1)
                e.wait_ge(g_pe, GPS.after(f"t2_{s}"))
                e.tensor_tensor(heads("X", n, n), heads("X", n, n), b3(1, n, n), ALU.add)
                link(e.tensor_tensor(heads("XT", n, n), heads("XT", n, n), b3(2, n, n), ALU.add))
                e.sem_inc(g_dve, 1)
            e.wait_ge(g_pe, GPS.after("o"))

            def vm_(h):
                e.tensor_tensor(vm[h % 2].rearrange("p (b d) -> p b d", b=NB),
                                heads("vnew", P, n)[:, h].unsqueeze(1).broadcast_to([n, NB, P]),
                                cst[0:n, C_BM:C_BM + NB].unsqueeze(2).broadcast_to([n, NB, P]), ALU.mult).then_inc(g_dve, 1)

            def add_(h):
                e.wait_ge(g_pe, GPS.after(f"ds{h}"))
                b = 2 * (h % 2)
                e.tensor_tensor(S_smp[:, :, h], S_smp[:, :, h],
                                ps[:, 512 * b:512 * b + 1024].rearrange("p (b d) -> p b d", b=NB), ALU.add).then_inc(g_dve, 1)

            last_decay = W["eg"][:, 0:w].rearrange("p (h b t) -> p b h t", h=GH, t=TS)[:, :, :, TS - 1].unsqueeze(3).broadcast_to([P, NB, GH, P])
            link(e.tensor_tensor(S_smp, S_smp, last_decay, ALU.mult))
            e.sem_inc(g_dve, 1)
            vm_(0)
            e.wait_ge(g_act, GCS.after("n"))
            y_c(4, n).then_inc(g_dve, 1)
            vm_(1)
            add_(0)
            vm_(2)
            add_(1)
            vm_(3)
            add_(2)
            add_(3)

            e.wait_ge(c_act, 4)
            e.scalar_tensor_tensor(out=kcT, in0=kcT, scalar=gain[:, G_K:G_K + 1], in1=crs, op0=ALU.mult, op1=ALU.mult).then_inc(c_dve, 1)

            e.wait_ge(turned, 2)
            e.wait_ge(g_act, GCS.end(1))
            for i in range(4):
                n = 7 + 8 * i
                x0 = CB - 1 + 384 - P * i
                s = sC[:, :, 0:n]
                e.wait_ge(ac_pe, 2 * i + 1)
                if i > 0:
                    e.wait_ge(ac_pe, 2 * i)
                link(e.tensor_tensor(s, bank(4, QH * NCP).rearrange("p (h c) -> p h c", h=QH)[:, :, 0:n],
                                     bfull[:, :, x0:x0 + CS * (n - 1) + 1:CS], ALU.add))
                link(e.tensor_reduce(mx[:, 0:QH], s, AX, ALU.max))
                e.tensor_tensor(s, s, mx[:, 0:QH].unsqueeze(2).broadcast_to([P, QH, n]), ALU.subtract).then_inc(ac_dve, 1)
                e.wait_ge(ac_act, 2 * i + 1)
                if i == 0:
                    link(e.tensor_tensor(s, s, cst[:, C_VAL:C_VAL + n].unsqueeze(1).broadcast_to([P, QH, n]), ALU.mult))
                link(e.tensor_reduce(zz[:, 0:QH], s, AX, ALU.add))
                link(e.tensor_scalar(zz[:, 0:QH], zz[:, 0:QH], 1.0, None, ALU.max))
                link(e.reciprocal(rz[:, 0:QH], zz[:, 0:QH]))
                link(e.tensor_tensor(rz[:, 0:QH], rz[:, 0:QH], sm[:, i, 0:QH], ALU.mult))
                e.tensor_tensor(s, s, rz[:, 0:QH].unsqueeze(2).broadcast_to([P, QH, n]), ALU.mult).then_inc(ac_dve, 1)

            def scores(s):
                h, i = ATT[s]
                n, c = P * (i + 1), 2 * (s % 2)
                x = pS[s % 3][:, :, 0:n]
                e.wait_ge(a_s, s + 1)
                if s >= 3:
                    e.wait_ge(a_t, 2 * (s - 2))
                b = 512 * (4 + 2 * (s % 2))
                link(e.tensor_tensor(x, ps[:, b:b + 1024].rearrange("p (k t) -> p k t", k=2)[:, :, 0:n],
                                     bfull[:, h, 384 - P * i:512].unsqueeze(1).broadcast_to([P, 2, n]), ALU.add))
                e.tensor_reduce(mx[:, c:c + 2], x, AX, ALU.max, negate=True).then_inc(a_m, 1)

            def scale(s):
                h, i = ATT[s]
                n, c = P * (i + 1), 2 * (s % 2)
                e.wait_ge(a_e, s + 1)
                link(e.reciprocal(rz[:, c:c + 2], zz[:, c:c + 2]))
                link(e.tensor_tensor(rz[:, c:c + 2], rz[:, c:c + 2], sm[:, i, QH + h:QH + h + QH + 1:QH], ALU.mult))
                for kind in range(2):
                    x = pS[s % 3][:, kind, 0:n]
                    e.tensor_scalar(x, x, rz[:, c + kind:c + kind + 1], None, ALU.mult).then_inc(a_p, 1)

            e.wait_ge(ac_pe, 8)
            for s in range(len(ATT) + 1):
                if s < len(ATT):
                    scores(s)
                if s >= 1:
                    scale(s - 1)

            for h in range(QH):
                last = e.tensor_copy(qs[:, :, TS * h:TS * h + TS], smp(kvq[:, N_A + h]))
            link(last)
            e.sem_inc(k_new, 1)

            def softmax(s, q, n, step):
                link(e.tensor_reduce(mx[0:16, 0:q], s, AX, ALU.max))
                e.tensor_tensor(s, s, mx[0:16, 0:q].unsqueeze(2).broadcast_to([16, q, n]), ALU.subtract).then_inc(s_dve, 1)
                e.wait_ge(s_act, step)
                link(e.tensor_reduce(zz[0:16, 0:q], s, AX, ALU.add))
                link(e.reciprocal(rz[0:16, 0:q], zz[0:16, 0:q]))
                e.tensor_tensor(s, s, rz[0:16, 0:q].unsqueeze(2).broadcast_to([16, q, n]), ALU.mult).then_inc(s_dve, 1)

            e.wait_ge(s_pe, 2)
            sC2 = s_S.rearrange("p q k -> p (q k)")[:, 0:16 * NCS].rearrange("p (q c) -> p q c", c=NCS)
            for g in range(G):
                last = e.tensor_tensor(sC2[:, g::G], bank(0, 16 * NCS, 16).rearrange("p (q c) -> p q c", c=NCS)[:, g::G],
                                       biasS[:, g, CB - 1:CB - 1 + CS * (NCS - 1) + 1:CS].unsqueeze(1).broadcast_to([16, NB, NCS]), ALU.add)
            link(last)
            softmax(sC2, 16, NCS, 2)
            e.wait_ge(s_pe, 4)
            e.tensor_tensor(ys, bank(2, 256), grow[:, 0], ALU.mult).then_inc(s_dve, 1)
            for p in range(4):
                kind, bh = p // 2, p % 2
                for g in range(G):
                    last = e.tensor_copy(kbuf[bh][:, :, g, PAST:KEYS],
                                         smp(kvq[:, 4 + 4 * kind + g])[:, 4 * bh:4 * bh + 4])
                last.then_inc(k_new, 1)
                e.wait_ge(s_pe, 4 * p + 5)
                for g in range(G):
                    last = e.tensor_tensor(s_S[:, g::G], ps[0:16, :].rearrange("p (q n) -> p q n", n=512)[:, g::G, 0:KEYS],
                                           biasS[:, g].unsqueeze(1).broadcast_to([16, 4, KEYS]), ALU.add)
                link(last)
                softmax(s_S, 8, KEYS, 2 * p + 4)
                e.wait_ge(s_pe, 4 * p + 8)
                c = P * bh
                link(e.tensor_tensor(ytmp[:, 0:P], bank(4, P), grow[:, kind + 1, c:c + P], ALU.mult))
                link(e.tensor_tensor(ys[:, c:c + P], ys[:, c:c + P], ytmp[:, 0:P], ALU.add))
                e.sem_inc(s_dve, 1)
            for h in range(QH):
                last = e.tensor_copy(smp(mix[:, 4 + h]), ys.rearrange("p (b n) -> p b n", b=NB)[:, :, TS * h:TS * h + TS])
            e.wait_ge(a_ye, QH)
            last.then_inc(s_dve, 1)

            e.wait_ge(ya_in, 16)
            group_norm(1)
            group_norm(2)
            e.wait_ge(n_lo, SPLIT_0[3] - 4)
            for c in range(4):
                e.tensor_copy(tn[c], mix[:, 12 + c]).then_inc(n_mul, 1)
            for c in range(4):
                e.wait_ge(n_hi, SPLIT_0[3] - 3 + c)
                e.tensor_tensor(xlo[:, 12 + c], tn[c], xhi_f[:, 12 + c], ALU.subtract).then_inc(n_lo, 1)
            split(0, H_OUT)
            split(0, H_OUT + 1)

            def h_sum(i, c):
                e.wait_ge(units, 2 * i + (U_OUT + c + 1))
                e.wait_ge(x_in[c], 16 * i + 16)
                for (d, x, b) in zip(halves(hbuf[:, 2 * i + c]), halves(xin[c]), (bank(2 * c, 256), bank(2 * c + 1, NT - 256))):
                    last = e.tensor_tensor(d, b, x, ALU.add)
                last.then_inc(h_add, 1)
            with e.Fori(0, KC // 2) as i:
                for c in range(2):
                    split(i, H_OUT + 2 * c + 2)
                    split(i, H_OUT + 2 * c + 3)
                    h_sum(i, c)
            e.wait_ge(h_add, KC)
            group_norm(3)

            e.wait_ge(n_lo, SPLIT_0[3] + 16)
            e.wait_ge(f_in, 32)
            e.wait_ge(h_out, 16)
            def ffn(i, first=False, last=False, spilled=False):
                for q in range(SLOTS):
                    u = SLOTS * i + q
                    if not (last and q == SLOTS - 1):
                        split(2 * i, H_UP + 2 * q + 2)
                        split(2 * i, H_UP + 2 * q + 3)
                    e.wait_ge(up_evac, u + 1)
                    e.wait_ge(up_hist, u + 1)
                    x = fx[q]
                    e.tensor_scalar(facc[q], x[:, 0:ROW3 - 2], fw[:, u, 0:1], None, ALU.mult).then_inc(up_conv, 1)
                    for k in (1, 2):
                        e.wait_ge(up_conv, 3 * u + k)
                        e.scalar_tensor_tensor(out=facc[q], in0=x[:, k:ROW3 - 2 + k], scalar=fw[:, u, k:k + 1], in1=facc[q],
                                               op0=ALU.mult, op1=ALU.add).then_inc(up_conv, 1)
                    if q % 2:
                        j = 2 * i + q // 2
                        e.wait_ge(up_silu, j + 1)
                        e.wait_ge(up_conv, 3 * u + 3)
                        if spilled and not first:
                            e.wait_ge(act_out[q // 2], 16 * i)
                        out = spill[q // 2] if spilled else act[:, j - SPILL]
                        e.tensor_tensor(out[:, 0:TP], facc[q - 1][:, 0:TP], facc[q][:, 0:TP], ALU.mult)
                        e.tensor_tensor(smp(out), seg(q - 1), seg(q), ALU.mult).then_inc(up_act, 1)

            def seg(q):
                return arena[:, FACC + (ROW3 - 2) * q + 2 + TP:FACC + (ROW3 - 2) * q + 2 + TP + NB * SEG3].rearrange("p (b n) -> p b n", n=SEG3)[:, :, 0:TS]

            ffn(0, first=True, spilled=True)
            with e.Fori(1, SPILL // 2) as i:
                ffn(i, spilled=True)
            with e.Fori(SPILL // 2, FC // 2 - 1) as i:
                ffn(i)
            ffn(FC // 2 - 1, last=True)

            e.wait_ge(up_act, FC)
            def y_sum(i, c, first):
                e.wait_ge(units, DU * (2 * i + c) + (U_DN + DU))
                e.wait_ge(h_in[c], 16 * i + 16)
                if not first:
                    e.wait_ge(y_out[c], 16 * i)
                for (d, x, b) in zip(halves(yout[c]), halves(hin[c]), (bank(2 * c, 256), bank(2 * c + 1, NT - 256))):
                    last = e.tensor_tensor(d, b, x, ALU.add)
                last.then_inc(dn_evac, 1)
            y_sum(0, 0, True)
            y_sum(0, 1, True)
            with e.Fori(1, KC // 2) as i:
                y_sum(i, 0, False)
                y_sum(i, 1, False)

        @block.gpsimd
        def _(e):
            e.wait_ge(s_cst, 16 * 8)
            e.wait_ge(a_free, 1)
            e.memset(gbuf[:, :, 0:3], 0.0)
            e.tensor_copy(gbuf[:, :, 3 + TP:ROW4].rearrange("p c (b n) -> p c b n", n=SEG4)[:, :, :, 0:3], hist_g).then_inc(p_chain, 1)
            e.wait_ge(p_chain, 1)
            e.sem_inc(gconv_in, 1)
            e.dma_start(ya_dram, zbuf).then_inc(ya_out, 16)
            e.wait_ge(proj_evac, PROJ - GH)
            e.tensor_copy(tail_g[:, :, 0:3], gbuf[:, :, TP:TP + 3])
            e.tensor_copy(tail_g[:, :, 3:27].rearrange("p c (b k) -> p c b k", k=3),
                          gbuf[:, :, 3 + TP:ROW4].rearrange("p c (b n) -> p c b n", n=SEG4)[:, :, :, 4:SEG4]).then_inc(p_chain, 1)
            e.wait_ge(p_chain, 2)
            e.sem_inc(tails, 1)

            e.wait_ge(n_lo, SPLIT_0[3] + 16)
            e.wait_ge(f_in, 32)
            for q in range(SLOTS):
                e.memset(fx[q][:, 0:2], 0.0)
            def rows(i, first=False, spilled=False):
                for q in range(SLOTS):
                    u = SLOTS * i + q
                    if not first:
                        e.wait_ge(up_conv, 3 * u - 9)
                    segs = fx[q][:, 2 + TP:ROW3].rearrange("p (b n) -> p b n", n=SEG3)
                    e.tensor_copy(segs[:, :, 0:2], hist[:, u]).then_inc(up_hist, 1)
                for q in range(SLOTS):
                    u = SLOTS * i + q
                    segs = fx[q][:, 2 + TP:ROW3].rearrange("p (b n) -> p b n", n=SEG3)
                    e.wait_ge(up_evac, u + 1)
                    e.tensor_copy(tail[:, u, 0:2], fx[q][:, TP:TP + 2])
                    e.tensor_copy(tail[:, u, 2:18].rearrange("p (b k) -> p b k", k=2), segs[:, :, 4:SEG3]).then_inc(up_tail, 1)
                if spilled:
                    for q in range(2):
                        e.wait_ge(up_act, 2 * i + q + 1)
                        e.dma_start(act_dram[:, 2 * i + q], spill[q]).then_inc(act_out[q], 16)
            rows(0, first=True, spilled=True)
            with e.Fori(1, SPILL // 2) as i:
                rows(i, spilled=True)
            with e.Fori(SPILL // 2, FC // 2) as i:
                rows(i)


_OUTS = {
    "y_t": (P, KC, NT), "kv_t": (P, N_A, NT), "win_old": (NB, PAST, 2 * G * P), "tail_a": (P, 4, 18), "tail_g": (P, N_A, 27),
    "gdn_sp": (P, GH * P), "gdn_ss": (P, NB, GH, P), "tail_f": (P, 2 * FC, 18),
}


def _cols(w, n):
    k = w.shape[0] // P
    return np.ascontiguousarray(w.reshape(k, P, n, P).transpose(2, 1, 0, 3).reshape(n, P, k * P))


def _feat(a, lead):
    x = a.reshape(*a.shape[:-1], -1, P)
    return np.ascontiguousarray(np.moveaxis(np.moveaxis(x, -1, 0), -1, 1))


def lay_out(x):
    x = {k: np.asarray(v) for k, v in x.items()}
    w = x["w_in"][0]
    o = np.cumsum([0, 512, 512, 512, 1024, 1536, 24, 1536, 4, 4, 512])
    part = [w[:, o[i]:o[i + 1]] for i in range(10)]
    a_b, a_c, a_h, nq, nkv, gate, qkv, ga, gb, gz = part
    abc = np.stack([p.reshape(DM, 4, P) for p in (a_c, a_h, a_b)], axis=2).reshape(DM, 12 * P)
    consts, onehot, neg = shape_constants()
    toks = np.concatenate([x["x_prompt"][0], x["x_sample"].reshape(NS, DM)], axis=0)
    d = {}
    d["x_t"] = np.ascontiguousarray(toks.T.reshape(KC, P, NT).transpose(1, 0, 2))
    d["consts"], d["onehot"], d["neg"] = consts, onehot, neg
    flip = np.zeros((P, P + 16), np.float32)
    flip[:, :P] = np.eye(P)[::-1]
    flip[:16, P:] = np.kron(np.eye(REP), np.eye(TS)[::-1])
    d["flip"] = flip
    d["w_proj"] = _cols(np.concatenate([abc, nkv, nq, qkv, gz], axis=1), PROJ)
    small = np.concatenate([gate, ga, gb], axis=1)
    d["w_small"] = np.ascontiguousarray(small.reshape(KC, P, 32).transpose(1, 0, 2))
    vec = [x[n][0].reshape(-1, P).T for n in ("norm_mix_g", "norm_ffn_g", "out_norm_a", "out_norm_b", "q_norm_g", "k_norm_g", "gdn_norm_g")]
    d["gains"] = np.ascontiguousarray(np.concatenate(vec, axis=1))
    d["conv_w"] = np.concatenate([_feat(x["conv_a_w"][0], 1).reshape(P, 12), _feat(x["gdn_conv_w"][0], 1).reshape(P, 48)], axis=1)
    d["ffn_w"] = _inter(_feat(x["ffn_conv_w"][0], 1))
    d["hist_a"] = _feat(x["state_conv_a"][0], 2)
    d["hist_g"] = _feat(x["state_gdn_conv"][0], 2)
    d["hist_f"] = _inter(_feat(x["state_ffn_conv"][0], 2))
    d["gdn_ab"] = np.ascontiguousarray(np.broadcast_to(np.concatenate([x["gdn_a_log"][0], x["gdn_dt_bias"][0]])[None], (P, 8)))
    d["pe_t"] = np.zeros((P, 2, PAST), np.float32)
    d["pe_t"][:, :, :CB] = x["cmp_pe"][0].transpose(2, 0, 1)
    d["page_table"] = np.ascontiguousarray(x["page_table"].reshape(1, 16))
    d["rel_bias"] = x["rel_bias"]
    d["state_gdn"] = np.ascontiguousarray(x["state_gdn"][0].transpose(2, 0, 1, 3))
    kv = x["cache_kv"][0]
    d["cache_kt"] = np.ascontiguousarray(kv[:, :, 0:3].transpose(0, 4, 2, 3, 1))
    d["cache_v"] = np.ascontiguousarray(kv[:, :, 3])
    cw = x["cache_win"][0]
    d["win_kt"] = np.ascontiguousarray(cw[:, :, 0].transpose(3, 0, 2, 1))
    d["win_v"] = np.ascontiguousarray(cw[:, :, 1].reshape(NB, 2, PAGE, G, P).transpose(2, 0, 1, 3, 4))
    d["cache_win"] = cw.reshape(NB, PAST, 2 * G * P)
    w1 = x["cmp_w1"][0].reshape(2, 2, 16, P, 2, P)
    d["w1c"] = np.ascontiguousarray(w1.transpose(0, 4, 1, 3, 2, 5).reshape(8, P, UNIT))
    d["w2c"] = np.ascontiguousarray(x["cmp_w2"][0].reshape(2, 2, P, P).transpose(2, 0, 1, 3).reshape(P, 512))
    d["w_o"] = _cols(x["w_out"][0], KC)
    up = x["ffn_up"][0].reshape(DM, 2, FC, P).transpose(0, 2, 1, 3).reshape(DM, 2 * DFF)
    d["w_up"] = _cols(up, 2 * FC)
    d["w_dn"] = np.ascontiguousarray(_cols(x["ffn_down"][0], KC).reshape(KC, P, DU, DT * P).transpose(0, 2, 1, 3).reshape(KC * DU, P, DT * P))
    return d


def _inter(a):
    return np.ascontiguousarray(a.reshape(P, 2, FC, *a.shape[2:]).swapaxes(1, 2).reshape(P, 2 * FC, *a.shape[2:]))


def take_back(r):
    def feats(a):
        return np.ascontiguousarray(a.transpose(2, 1, 0)).reshape(a.shape[2], -1)

    def tails(a, k):
        f = feats(a)
        return f[:k][None, None], f[k:].reshape(1, NB, k, -1)

    y = feats(r["y_t"])
    kv = feats(r["kv_t"]).reshape(NT, 3, 2, G, P)
    rows, win = kv[:, 0:2].reshape(NT, 4, G, P), kv[:, 2]
    old = r["win_old"].reshape(NB, PAST, 2, G, P)
    win_s = np.concatenate([old, win[TP:].reshape(NB, TS, 2, G, P)], axis=1)
    ca, gv = tails(r["tail_a"], 2), tails(r["tail_g"], 3)
    tf = r["tail_f"].reshape(P, FC, 2, 18).transpose(0, 2, 1, 3).reshape(P, 2 * FC, 18)
    ff = tails(tf, 2)
    sp = r["gdn_sp"].reshape(P, GH, P).transpose(1, 0, 2)[None, None]
    ss = r["gdn_ss"].transpose(1, 2, 0, 3)[None]
    c = np.ascontiguousarray
    return (c(y[:TP][None]), c(y[TP:].reshape(NB, TS, DM)), c(rows[:TP][None, None]), c(rows[TP:].reshape(1, NB, TS, 4, G, P)),
            c(win[:TP][None, None]), c(win_s[None]), c(ca[0]), c(ca[1]), c(gv[0]), c(gv[1]), c(sp), c(ss), c(ff[0]), c(ff[1]))


def kernel(**inputs):
    import concourse.bacc as bacc
    from concourse.bass_utils import run_bass_kernel_spmd

    nc = bacc.Bacc("TRN2", target_bir_lowering=False, num_devices=1)
    arrays, ins, outs = {}, {}, {}
    for name, a in lay_out(inputs).items():
        arrays[f"in_{name}"] = a
        ins[name] = nc.dram_tensor(f"in_{name}", a.shape, mybir.dt.from_np(a.dtype), kind="ExternalInput").ap()
    for name, shape in _OUTS.items():
        outs[name] = nc.dram_tensor(f"out_{name}", shape, F32, kind="ExternalOutput").ap()
    build(nc, ins, outs)
    r = run_bass_kernel_spmd(nc, [arrays], core_ids=[0])
    return take_back({name: r.results[0][f"out_{name}"] for name in _OUTS})
```

```python
import math
from contextlib import ExitStack

import numpy as np
import concourse.bass as bass
from concourse import mybir

F32 = mybir.dt.float32
F32R = mybir.dt.float32r
I32 = mybir.dt.int32
ALU = mybir.AluOpType
ACT = mybir.ActivationFunctionType
AX = mybir.AxisListType.X

P = 128
DM = 2048
KC = DM // P
TP, NB, TS = 512, 8, 4
NS = NB * TS
NT = TP + NS
QH, G, REP = 8, 2, 4
GH = 4
PAST, PAGE = 256, 128
KEYS = PAST + TS
CB, CS = 32, 16
NCP, NCS = (TP - CB) // CS + 1, (KEYS - CB) // CS + 1
DFF = 5632
FC = DFF // P
NPOOL = 20
EPS = 1e-6
NEG = -1e30
SLOTS = 4
UNIT = KC * P
PARTS = 4
FQ = FC // PARTS
DH = (6, FQ - 6)
N_A, N_KVQ, N_GZ = 12, 20, 16
PROJ = N_A + N_KVQ + N_GZ
U_CMP = PROJ
U_OUT = U_CMP + 8
U_UP = U_OUT + KC
U_PART = 2 * FQ + KC
HALF_K = KC // 2
H_OUT = 2 * PROJ
H_UP = H_OUT + 2 * KC
R_CMP = 2 * PROJ // SLOTS
R_OUT = R_CMP + 8 // SLOTS
ROW3, SEG3 = 2 + TP + NB * (2 + TS), 2 + TS
ROW4, SEG4 = 3 + TP + NB * (3 + TS), 3 + TS
TAB = 640

C_ONE, C_ID, C_TRI, C_SU = 0, 128, 256, 384
C_LEV = 512
C_GRP, C_TRIB, C_SUB = C_LEV + 7 * 128, C_LEV + 7 * 128 + 32, C_LEV + 7 * 128 + 64
C_BM = C_SUB + 32
C_VAL = C_BM + 8
C_EPS = C_VAL + 7
NCONST = C_EPS + 3
G_MIX, G_FFN, G_OA, G_OB, G_Q, G_K, G_GDN = 0, 16, 32, 36, 44, 45, 46


def shape_constants():
    c = np.zeros((P, NCONST), np.float32)
    row, col = np.arange(P)[:, None], np.arange(P)[None, :]
    c[:, C_ONE:C_ONE + P] = 1
    c[:, C_ID:C_ID + P] = row == col
    c[:, C_TRI:C_TRI + P] = row <= col
    c[:, C_SU:C_SU + P] = row < col
    for s in range(7):
        same, split = row >> (s + 1) == col >> (s + 1), row >> s != col >> s
        c[:, C_LEV + s * P:C_LEV + (s + 1) * P] = same & split & (row < col)
    r, q = row[:NS], col[:, :NS]
    c[:NS, C_GRP:C_GRP + NS] = r // TS == q // TS
    c[:NS, C_TRIB:C_TRIB + NS] = (r // TS == q // TS) & (r <= q)
    c[:NS, C_SUB:C_SUB + NS] = (r // TS == q // TS) & (r < q)
    c[:NS, C_BM:C_BM + NB] = r // TS == np.arange(NB)[None, :]
    c[:, C_VAL:C_VAL + 7] = row >= CB - 1 + CS * np.arange(7)[None, :]
    c[:, C_EPS:C_EPS + 3] = [EPS, P * EPS, 1.0]
    dist = TP - 1 - np.arange(TAB)
    n = np.maximum(dist, 0)
    nf = np.maximum(n, 1).astype(np.float32)
    far = 16 + (np.log(nf / np.float32(16)) / np.float32(math.log(64)) * np.float32(16)).astype(np.int32)
    bucket = np.where(n < 16, n, np.minimum(far, 31))
    onehot = ((np.arange(32)[:, None] == bucket[None, :]) & (dist >= 0)[None, :]).astype(np.float32)
    neg = np.broadcast_to(np.where(dist >= 0, 0.0, NEG).astype(np.float32), (QH, TAB))
    return c, onehot, np.ascontiguousarray(neg)


class Steps:

    def __init__(self, sem, names, base=0):
        self.sem, self.names, self.base = sem, names, base

    def after(self, name, rnd=0):
        return self.base + rnd * len(self.names) + self.names.index(name) + 1

    def end(self, rounds):
        return self.base + rounds * len(self.names)


def build(nc, A, O):
    ctx = ExitStack()
    with ctx:
        XN = 0
        MIX = XN + KC * NT
        KVQ = MIX + KC * NT
        GA = KVQ + N_KVQ * NT
        Z = GA + N_A * ROW4
        BF = -(-(Z + GH * NT) // 8) * 8
        RING = BF + QH * 512
        CST = RING + SLOTS * UNIT
        GAIN = CST + NCONST
        CW = GAIN + 47
        SMALL = CW + 12 + 48

        words = 53156
        TN = KVQ + 28 * NT
        hw = HALF_K * P
        with nc.sbuf_tensor("x_hi", [P, KC * NT], F32R) as xhi_t, nc.sbuf_tensor("x_lo", [P, KC * NT], F32R) as xlo_t, \
                nc.sbuf_tensor("gap0", [P, TN - 2 * KC * NT], F32), nc.sbuf_tensor("x_whole", [P, 4 * NT], F32) as tn_t, \
                nc.sbuf_tensor("gap1", [P, RING - TN - 4 * NT], F32), nc.sbuf_tensor("w_whole", [P, 4 * hw], F32) as raw_t, \
                nc.sbuf_tensor("w_hi", [P, 2 * hw], F32R) as whi_t, nc.sbuf_tensor("w_lo", [P, 2 * hw], F32R) as wlo_t:
            pass
        AH = KVQ + KC * NT
        with nc.sbuf_tensor("gap3", [P, AH], F32), nc.sbuf_tensor("act_hi", [P, FQ * NT], F32R) as ahi_t, \
                nc.sbuf_tensor("act_lo", [P, FQ * NT], F32R) as alo_t, nc.sbuf_tensor("act_whole", [P, NT], F32) as aw_t:
            pass
        arena = ctx.enter_context(nc.sbuf_tensor("arena", [P, words], F32))
        ptab = ctx.enter_context(nc.sbuf_tensor("ptab", [1, 16], I32))
        ps = ctx.enter_context(nc.psum_tensor("ps", [P, 8 * 512], F32))
        table_dram = nc.dram_tensor("bias_table", (QH, TAB), F32, kind="Internal").ap()
        ya_dram = nc.dram_tensor("y_a_spill", (P, 4, NT), F32, kind="Internal").ap()

        def sem(name):
            return ctx.enter_context(nc.semaphore(name))

        def at(off, n, parts=P):
            assert off + n <= words
            return arena[0:parts, off:off + n]

        def bank(i, n=512, parts=P, off=0):
            return ps[0:parts, i * 512 + off:i * 512 + off + n]

        mix = at(MIX, KC * NT).rearrange("p (k t) -> p k t", k=KC)
        kvq = at(KVQ, N_KVQ * NT).rearrange("p (k t) -> p k t", k=N_KVQ)
        abuf = at(GA, N_A * NT).rearrange("p (k t) -> p k t", k=N_A)
        gbuf = at(GA, N_A * ROW4).rearrange("p (k t) -> p k t", k=N_A)
        zbuf = at(Z, GH * NT).rearrange("p (k t) -> p k t", k=GH)
        slot = [at(RING + s * UNIT, UNIT).rearrange("p (k n) -> p k n", n=P) for s in range(SLOTS)]
        xhi, xlo = (t[:].rearrange("p (k t) -> p k t", k=KC) for t in (xhi_t, xlo_t))
        raw = [raw_t[:, s * hw:(s + 1) * hw] for s in range(4)]
        whi, wlo = ([t[:, s * hw:(s + 1) * hw] for s in range(2)] for t in (whi_t, wlo_t))
        whi_f = [w.bitcast(F32) for w in whi]
        xhi_f, xlo_f = xhi.bitcast(F32), xlo.bitcast(F32)
        cst = at(CST, NCONST)
        gain = at(GAIN, 47)
        aw = at(CW, 12).rearrange("p (c k) -> p c k", k=3)
        gw = at(CW + 12, 48).rearrange("p (c k) -> p c k", k=4)
        ones, ident, tri = cst[:, C_ONE:C_ONE + P], cst[:, C_ID:C_ID + P], cst[:, C_TRI:C_TRI + P]
        eps1, eps128, one = (cst[:, C_EPS + i:C_EPS + i + 1] for i in range(3))

        pos = [SMALL]

        def small(n, parts=P):
            pos[0] += n
            return at(pos[0] - n, n, parts)

        sm = small(160).rearrange("p (c n) -> p c n", c=5)
        gdn_in = small(8)
        soft = small(20)
        soft2 = small(20)
        gdec = small(20)
        gc = small(20)
        gl = small(20)
        egc, ekd, beg = small(20), small(20), small(20)
        egl = small(16)
        biasS = small(G * KEYS, 16).rearrange("p (g k) -> p g k", g=G)
        kcT = small(2 * NCP + 16 * NCS)
        vcP = small(G * P, NCP).rearrange("p (g d) -> p g d", g=G)
        pebs = small(4)
        mx, zz, rz = small(16), small(16), small(16)
        assert pos[0] <= words, pos[0]

        xa = at(BF + 512, ROW3)
        acc_a = at(BF + 512 + ROW3, ROW3 - 2)
        o = BF + 512 + 2 * ROW3 - 2
        hist_a = at(o, 64).rearrange("p (c b k) -> p c b k", c=4, b=NB)
        hist_g = at(o + 64, 288).rearrange("p (c b k) -> p c b k", c=N_A, b=NB)
        tail_a = at(o + 352, 72).rearrange("p (c n) -> p c n", c=4)
        tail_g = at(o + 424, 324).rearrange("p (c n) -> p c n", c=N_A)
        assert o + 748 <= BF + 2384
        nrm_sq = [at(Z, NT), at(Z + NT, NT)]
        rs1 = at(Z + 2 * NT, NT)

        ut = gbuf[:, :, 0:NT]
        cacc = [at(BF + 2384, ROW4 - 3), at(BF + 2384 + ROW4, ROW4 - 3)]
        names = ["decT", "kbT", "eg", "qeg", "nl", "qk", "X", "XT", "CT", "T1", "vb", "kbeg", "kd"]
        W = {n: at(XN + 512 * i, 512) for i, n in enumerate(names)}
        for i, n in enumerate(["nwT", "vnew", "S", "oT", "sq", "rs"]):
            W[n] = at(RING + 512 * i, 512)
        free = [MIX + 4 * NT + 512 * i for i in range(8)] + [XN + 512 * (len(names) + i) for i in range(4)]
        free += [BF + 2384 + 512 * i for i in range(3)] + [RING + 7168 + 512 * i for i in range(2)]
        tile_names = [f"{n}{t}" for t in (1, 2, 3) for n in ("X", "XT")]
        tile_names += [f"{n}{t}" for n in ("nl", "qk", "qeg") for t in (1, 2, 3)] + ["CT_odd", "T1_odd"]
        W.update({n: at(a, 512) for n, a in zip(tile_names, free, strict=True)})
        XX = [at(XN + 512 * names.index("X"), 1024)] + [at(free[2 * i], 1024) for i in range(3)]

        def of(n, t):
            return f"{n}{t}" if 0 < t < 4 else n

        CT, T1 = ("CT", "CT_odd"), ("T1", "T1_odd")
        DEC, KB, EG = ("decT", "kbeg"), ("kbT", "vb"), ("eg", "kd")
        VB, KBEG, KD = ("vb", "CT"), ("kbeg", "CT_odd"), ("kd", "T1")
        S_smp = at(RING + 3072, 4096).rearrange("p (b h e) -> p b h e", b=NB, h=GH)
        vm = [at(RING + 7168, 1024, NS), at(XN, 1024, NS)]
        hn_sq, hn_rs = ([[at(a + NT * (2 * n + i), NT) for i in range(2)] for a in (Z, XN)] for n in range(2))
        relb, onehot = at(KVQ, QH, 32), at(KVQ + 8, TAB, 32)
        negt, tabs = at(KVQ + 8 + TAB, TAB, QH), at(KVQ + 8 + 2 * TAB, TAB, QH)

        def heads(w, n=P, parts=P):
            return W[w][0:parts, 0:GH * n].rearrange("p (h i) -> p h i", h=GH)

        segs_t = [at(a, 17 * PAST).rearrange("p (s t) -> p s t", s=17) for a in (MIX + 4 * NT, XN)]
        crT = [x[:, 0:16].rearrange("p (b g) t -> p b g t", b=NB) for x in segs_t]
        flip = at(GA + 6144, P + 16)
        w2 = at(GA, 512).rearrange("p (k c d) -> p k c d", k=2, c=2)
        NCOL = G * NCP + 16 * NCS
        hid = at(GA + 512, 4 * NCOL).rearrange("p (k c n) -> p k c n", k=2, c=2)
        csq, crs = at(GA + 2048, NCOL), at(GA + 2560, NCOL)
        vcS = at(Z, 2048, NCS).rearrange("p (q d) -> p q d", d=P)

        bfull = at(BF, QH * 512).rearrange("p (h x) -> p h x", h=QH)
        PTc = at(GA, 4096, NCP).rearrange("p (h t) -> p h t", h=QH)
        VN = at(GA + 4096, 2048).rearrange("p (k g j d) -> p k g j d", k=2, g=G, j=4)
        sC = at(RING, QH * NCP).rearrange("p (h c) -> p h c", h=QH)
        pS = [at(RING + 1024 * i, 1024).rearrange("p (k t) -> p k t", k=2) for i in range(3)]
        pT = [at(RING + 3072 + 1024 * i, 1024).rearrange("p (k t) -> p k t", k=2) for i in range(2)]
        o = RING + 3072
        s_S = at(o, 8 * KEYS, 16).rearrange("p (q k) -> p q k", k=KEYS)
        s_PT = at(o + 2080, 256)
        s_PN = at(o + 2336, 128, TS)
        s_VN = at(o + 2464, 1024, TS).rearrange("p (q d) -> p q d", d=P)
        grow = at(o + 3488, 768).rearrange("p (k n) -> p k n", k=3)
        ys = at(o + 4256, 256)
        qs = at(o + 4512, 256).rearrange("p (b n) -> p b n", b=NB)
        ytmp = at(o + 4768, 256)
        assert 3072 + 4768 + 256 <= SLOTS * UNIT
        kbuf = [at(XN + i * 4128, 2080).rearrange("p (b g k) -> p b g k", b=4, g=G) for i in range(2)]
        vbuf = [at(XN + i * 4128 + 2080, 2048).rearrange("p (b j g d) -> p b j g d", b=4, j=2, g=G) for i in range(2)]

        hbuf = at(KVQ, KC * NT).rearrange("p (k t) -> p k t", k=KC)
        xin = [at(Z + i * NT, NT) for i in range(2)]
        ahi, alo = (t[:].rearrange("p (k t) -> p k t", k=FQ) for t in (ahi_t, alo_t))
        ahi_f = ahi.bitcast(F32)
        aw_ = aw_t[:]
        FX = AH + (2 * FQ + 1) * NT
        fx = [at(FX + ROW3 * i, ROW3) for i in range(2)]
        FACC = FX + 2 * ROW3
        facc = [at(FACC + (ROW3 - 2) * i, ROW3 - 2) for i in range(2)]
        o = FACC + 2 * (ROW3 - 2)
        fw = at(o, 6 * FC).rearrange("p (u k) -> p u k", u=2 * FC)
        assert o + 6 * FC <= RING
        hist = at(CST, 2 * FC * 16).rearrange("p (u b k) -> p u b k", u=2 * FC, b=NB)
        tail = at(CST + 2 * FC * 16, 2 * FC * 18).rearrange("p (u n) -> p u n", u=2 * FC)
        tn = [tn_t[:, NT * i:NT * (i + 1)] for i in range(4)]

        s_x = [sem(f"x_loaded{q}") for q in range(4)]
        s_cst, s_tab = sem("constants_loaded"), sem("table_inputs_loaded")
        w_ready = [sem(f"weights_in_slot{s}") for s in range(SLOTS)]
        units = sem("units_multiplied")
        w_hi, w_lo = sem("weights_high_part"), sem("weights_low_part")
        used = sem("first_halves_multiplied")
        proj_evac = sem("proj_evacuated")
        n_sq, n_mm, n_rs, n_mul = (sem(n) for n in ("norm_squared", "norm_summed", "norm_rstd", "norm_scaled"))
        n_hi, n_lo = sem("x_high_part"), sem("x_low_part")
        ya_out, ya_in = sem("y_a_stored"), sem("y_a_reloaded")
        act_hi, act_lo = sem("act_high_part"), sem("act_low_part")
        gw_in, gw_hi, gw_lo = sem("gates_weights_loaded"), sem("gates_weights_high_part"), sem("gates_weights_low_part")
        gates_mm, a_free = sem("gates_summed"), sem("conv_a_buffer_read")
        gconv_in, gconv_dve, gconv_act = sem("gdn_conv_rows_set"), sem("gdn_conv_tap"), sem("gdn_conv_silu")
        tails = sem("conv_tails_copied")
        nh_sq, nh_mm, nh_rs, nh_mul = (sem(n) for n in ("hnorm_squared", "hnorm_summed", "hnorm_rstd", "hnorm_scaled"))
        g_pe, g_act, g_dve = sem("gdn_pe"), sem("gdn_act"), sem("gdn_dve")
        r_rows, r_dec, r_kb, r_exp, r_gram, r_low = (sem(n) for n in (
            "decay_rows", "decay_exponents", "beta_k", "decay_exp", "grams", "grams_decayed"))
        l_ct, l_t1p, l_t1c, l_t2, l_x = (sem(n) for n in (
            "level_masked", "level_first_product", "level_first_copied", "level_second_product", "level_added"))
        q_nat, q_vk, q_w, q_nw, q_v, q_vn, q_o, q_s, q_oc, q_n, q_rs, q_y = (sem(n) for n in (
            "kv_token_major", "kv_scaled", "w_product", "w_negated", "v_new_product", "v_new_copied",
            "o_product", "state_updated", "o_copied", "o_squares_summed", "o_rstd", "y_c_done"))
        st_in, gdn_stored = sem("states_loaded"), sem("gdn_states_stored")
        cv_in = sem("cache_values_loaded")
        c_in, c_pe, c_act, c_dve = sem("cache_loaded"), sem("cmp_pe"), sem("cmp_act"), sem("cmp_dve")
        t_pe, t_dve, t_out, bs_in, bf_in = sem("table_summed"), sem("table_ready"), sem("table_stored"), sem("sample_bias_loaded"), sem("bias_loaded")
        turned_pe, turned = sem("bias_turned"), sem("bias_turned_copied")
        v_pe, v_act = sem("values_transposed"), sem("values_copied")
        ac_pe, ac_act, ac_dve = sem("acmp_pe"), sem("acmp_act"), sem("acmp_dve")
        a_s, a_m, a_e, a_p, a_t, a_pt, a_y, a_ye = (sem(n) for n in (
            "scores_ready", "max_ready", "exp_ready", "probs_ready", "probs_transposed", "probsT_copied",
            "head_summed", "head_evacuated"))
        kv_in, k_new = [sem("kv_loaded0"), sem("kv_loaded1")], sem("new_keys_copied")
        s_pe, s_act, s_dve = sem("smp_pe"), sem("smp_act"), sem("smp_dve")
        x_in, h_add = [sem("x_reloaded0"), sem("x_reloaded1")], sem("h_added")
        f_in = sem("ffn_small_loaded")
        up_evac, up_hist, up_tail, up_conv, up_silu, up_act = (sem(n) for n in (
            "up_evacuated", "up_history", "up_tail", "up_conv", "up_silu", "up_gated"))
        y_add, y_out = sem("y_added"), sem("y_stored")
        stored = sem("outputs_stored")
        d_chain, a_chain, p_chain = sem("dve_done"), sem("act_done"), sem("pool_done")

        LV, LVS = 7, 2
        t1, t2 = [[f"t1_{s}", f"t2_{s}"] for s in range(LVS)], [[f"ct_{s}", f"x_{s}"] for s in range(LVS)]
        PRE_PE, PRE_ACT, PRE_DVE = 1, 3, 5
        GPS = Steps(g_pe, ["rows", "gram", "nat"] + sum(t1, []) + ["w", "v", "vt", "o", "n", "ds0", "ds1", "ds2", "ds3"], PRE_PE)
        GCS = Steps(g_act, ["dec", "nat"] + [x[0] for x in t1] + ["w", "v", "vt", "o", "n"], PRE_ACT)
        GDS = Steps(g_dve, ["dec", "kb", "low", "xinit"] + sum(t2, []) + ["smul", "vm0", "y", "vm1", "add0", "vm2", "add1", "vm3", "add2", "add3"], PRE_DVE)
        LEVELS = [(s, t) for s in range(LV) for t in range(4)]

        HEADS = [(kvq[:, k], G_K, 1.0 / P, eps1) for k in (4, 5, 8, 9)]
        HEADS += [(kvq[:, N_A + h], G_Q, 1.0, eps128) for h in range(QH)]
        HEADS += [(ut[:, h], None, float(P), eps128) for h in range(GH)]
        HEADS += [(ut[:, GH + h], None, 1.0, eps1) for h in range(GH)]
        NKQ = 4 + QH
        GROUPS = [(mix[:, 0:16], 0, G_MIX), (mix[:, 0:4], 0, G_OA), (mix[:, 4:12], 4, G_OB), (hbuf[:, 0:16], 0, G_FFN)]
        GROUP_N = [16, 4, 8, 16]
        GROUP_0 = [0, 16, 20, 28]
        SPLIT_0 = [0, 16, 20, 32]
        ATT = [(h, i) for h in range(QH) for i in range(4)]

        def halves(x):
            return x[:, 0:256], x[:, 256:NT]

        def rows3(x):
            return x[:, 2:2 + TP], x[:, 2 + TP:ROW3].rearrange("p (b n) -> p b n", n=SEG3)[:, :, 2:SEG3]

        def smp(x):
            return x[:, TP:NT].rearrange("p (b t) -> p b t", t=TS)

        block = ctx.enter_context(nc.Block())

        @block.sync
        def _(e):
            def unit(u, src, n=UNIT):
                e.dma_start(at(RING + (u % SLOTS) * UNIT, n), src).then_inc(w_ready[u % SLOTS], 16)

            for dst, name in ((cst, "consts"), (gain, "gains"), (at(CW, 60), "conv_w"),
                              (gdn_in, "gdn_ab"), (hist_a, "hist_a"), (hist_g, "hist_g"),
                              (ptab[:], "page_table")):
                e.dma_start(dst, A[name]).then_inc(s_cst, 16)
            for q in range(4):
                e.dma_start(mix[:, 4 * q:4 * q + 4, :], A["x_t"][:, 4 * q:4 * q + 4, :]).then_inc(s_x[q], 16)
            def half_units(w, i, h0, first, u0=0, tiles=(HALF_K, HALF_K)):
                for s in range(SLOTS):
                    if not first:
                        e.wait_ge(w_lo, SLOTS * i + (h0 + s - SLOTS + 1))
                    n, c = P * tiles[s % 2], P * tiles[0] * (s % 2)
                    e.dma_start(raw[s][:, 0:n], w[2 * i + (u0 + s // 2)][:, c:c + n]).then_inc(w_ready[s], 16)

            half_units(A["w_proj"], 0, 0, True)
            with e.Fori(1, PROJ // 2) as i:
                half_units(A["w_proj"], i, 0, False)

            e.wait_ge(w_lo, 2 * PROJ - SLOTS + 1)
            e.dma_start(raw[0][:, 0:32 * KC], A["w_small"]).then_inc(gw_in, 16)

            e.wait_ge(units, PROJ)
            e.wait_ge(gates_mm, 1)
            e.dma_start(S_smp, A["state_gdn"]).then_inc(st_in, 16)
            e.wait_ge(ya_out, 16)
            e.dma_start(mix[:, 0:4], ya_dram).then_inc(ya_in, 16)

            e.wait_ge(q_y, 4)
            e.wait_ge(s_cst, 16 * 7)
            pages = [e.value_load(ptab[0:1, q:q + 1], min_val=0, max_val=NPOOL - 1) for q in range(16)]
            e.dma_start(segs_t[0][:, 16], A["pe_t"][:, 0]).then_inc(c_in, 16)

            def cached_rows(k, loaded):
                for q in range(16):
                    e.dma_start(crT[k][:, q // 2, :, q % 2 * PAGE:(q % 2 + 1) * PAGE], A["cache_kt"][pages[q], :, k]).then_inc(loaded, 16)

            cached_rows(0, c_in)
            e.wait_ge(g_dve, GDS.end(1))
            e.wait_ge(g_pe, GPS.end(1))
            e.wait_ge(g_act, GCS.end(1))
            e.dma_start(O["gdn_sp"], W["S"]).then_inc(gdn_stored, 16)
            e.dma_start(O["gdn_ss"], S_smp).then_inc(gdn_stored, 16)
            e.wait_ge(tails, 1 + N_A)
            e.dma_start(O["tail_a"], tail_a).then_inc(gdn_stored, 16)
            e.dma_start(O["tail_g"], tail_g).then_inc(gdn_stored, 16)
            e.wait_ge(gdn_stored, 64)
            e.dma_start(w2, A["w2c"]).then_inc(c_in, 16)
            for u in range(8):
                if u >= SLOTS:
                    e.wait_ge(units, U_CMP + u - SLOTS + 1)
                unit(u, A["w1c"][u])
                if u == 1:
                    e.dma_start(segs_t[1][:, 16], A["pe_t"][:, 1]).then_inc(cv_in, 16)
                    cached_rows(1, cv_in)
            e.dma_start(flip, A["flip"]).then_inc(cv_in, 16)

            for p in range(4):
                kind, bh = p // 2, p % 2
                if p == 0:
                    e.wait_ge(c_pe, 2)
                if p >= 2:
                    e.wait_ge(s_pe, 4 + 4 * (p - 1))
                for b in range(4):
                    for j in range(2):
                        q = 2 * (4 * bh + b) + j
                        kd = kbuf[bh][:, b, :, j * PAGE:(j + 1) * PAGE]
                        vd = vbuf[bh][:, b, j]
                        if kind == 0:
                            e.dma_start(kd, A["cache_kt"][pages[q], :, 2]).then_inc(kv_in[bh], 16)
                            e.dma_start(vd, A["cache_v"][pages[q]]).then_inc(kv_in[bh], 16)
                        else:
                            e.dma_start(kd, A["win_kt"][:, 4 * bh + b, :, j * PAGE:(j + 1) * PAGE]).then_inc(kv_in[bh], 16)
                            e.dma_start(vd, A["win_v"][:, 4 * bh + b, j]).then_inc(kv_in[bh], 16)

            e.wait_ge(s_dve, 16)
            e.wait_ge(s_pe, 20)
            e.wait_ge(a_ye, QH)
            half_units(A["w_o"], 0, H_OUT, True)
            with e.Fori(1, KC // 2) as i:
                half_units(A["w_o"], i, H_OUT, False)
            for part in range(PARTS):
                h0 = H_UP + 2 * U_PART * part
                with e.Fori(0, FQ) as i:
                    half_units(A["w_up"], i, h0, False, 2 * FQ * part)
                with e.Fori(0, KC // 2) as i:
                    half_units(A["w_dn"], i, h0 + 4 * FQ, False, KC * part, DH)
            e.wait_ge(up_tail, 2 * FC)
            e.dma_start(O["tail_f"], tail).then_inc(stored, 16)
            with e.Fori(0, KC) as i:
                e.wait_ge(y_add, i + (KC * (PARTS - 1) + 1))
                e.dma_start(O["y_t"][:, i], hbuf[:, i]).then_inc(y_out, 16)
            e.wait_ge(stored, 16 * 3)
            e.wait_ge(y_out, 16 * KC)

        @block.tensor
        def _(e):
            def mm(out, lhsT, rhs, start=True, stop=True):
                return e.matmul(out, lhsT, rhs, start=start, stop=stop, skip_group_check=True)

            def tr(out, in_):
                n = in_.shape[0]
                return e.transpose(out, in_, ident[0:n, 0:n])

            def unit(i, h, banks, xs=(xhi, xlo), tiles=(HALF_K, HALF_K), last_chunk=None, split0=None):
                for half in range(2):
                    e.wait_ge(w_lo, SLOTS * i + (h + half + 1))
                    for k in range(tiles[half]):
                        c = tiles[0] * half + k
                        if last_chunk and c == sum(tiles) - 1:
                            e.wait_ge(act_lo, last_chunk)
                        if split0 is not None:
                            e.wait_ge(n_lo, split0 + c + 1)
                        wh, wl = (w[half][:, P * k:P * k + P] for w in (whi, wlo))
                        for n, (w, x) in enumerate(((wh, xs[0]), (wh, xs[1]), (wl, xs[0]))):
                            start, stop = c == 0 and n == 0, c == sum(tiles) - 1 and n == 2
                            a, b = halves(x[:, c])
                            mm(bank(banks, 256), w, a, start, stop)
                            last = mm(bank(banks + 1, NT - 256), w, b, start, stop)
                    last.then_inc(units if half else used, 1)

            def sum_squares(sq, first, last, banks):
                lo, hi = halves(sq)
                mm(bank(banks, 256), ones, lo, first, last)
                return mm(bank(banks + 1, NT - 256), ones, hi, first, last)

            def group_norm(g):
                for k in range(GROUP_N[g]):
                    e.wait_ge(n_sq, GROUP_0[g] + k + 1)
                    sum_squares(nrm_sq[k % 2], k == 0, k == GROUP_N[g] - 1, 4).then_inc(n_mm, 1)

            e.wait_ge(s_tab, 48)
            mm(bank(6, 320, QH), relb, onehot[:, 0:320])
            mm(bank(7, 320, QH), relb, onehot[:, 320:TAB]).then_inc(t_pe, 1)

            e.wait_ge(s_cst, 16 * 7)
            group_norm(0)

            unit(0, 0, 0, split0=0)
            unit(0, 2, 2)
            def proj_units(i, sums=(), reused=()):
                for s in range(2):
                    e.wait_ge(proj_evac, 2 * i + s - 1)
                    unit(i, 2 * s, 2 * s)
                    if s in sums:
                        t = 2 * i + (s - 1 - N_A - N_KVQ)
                        e.wait_ge(nh_sq, t + 1)
                        if s in reused:
                            e.wait_ge(nh_rs, t - 1)
                        odd = (s - 1) % 2
                        sum_squares(hn_sq[0][odd], True, True, 4 + 2 * odd).then_inc(nh_mm, 1)

            c = (N_A + N_KVQ) // 2
            with e.Fori(1, c) as i:
                proj_units(i)
            e.wait_ge(t_dve, 1)
            proj_units(c, (1,))
            proj_units(c + 1, (0, 1), (1,))
            with e.Fori(c + 2, c + N_A // 2) as i:
                proj_units(i, (0, 1), (0, 1))
            proj_units(c + N_A // 2, (0,), (0,))
            proj_units(c + N_A // 2 + 1)
            e.wait_ge(nh_rs, NKQ)
            e.wait_ge(gw_lo, 1)
            for t in range(5):
                for k in range(KC):
                    c = slice(32 * k, 32 * k + 32)
                    hi, lo = (x[:, k, P * t:min(P * t + P, NT)] for x in (xhi, xlo))
                    passes = [(hi, whi[0][:, c]), (lo, whi[0][:, c]), (hi, wlo[0][:, c])]
                    if t == 4:
                        passes = [(x[:, k, TP:NT], raw[0][:, c]) for x in (xhi_f, xlo_f)]
                    for q, (x, w) in enumerate(passes):
                        last = mm(bank(6, 32, P if t < 4 else NS, 32 * t), x, w, k + q == 0, k == KC - 1 and q == len(passes) - 1)
            last.then_inc(gates_mm, 1)

            for t in range(NKQ, len(HEADS)):
                e.wait_ge(nh_sq, t + 1)
                if t >= NKQ + 2:
                    e.wait_ge(nh_rs, t - 1)
                else:
                    e.wait_ge(proj_evac, PROJ)
                sum_squares(hn_sq[1][t % 2], True, True, 2 * (t % 2)).then_inc(nh_mm, 1)

            e.wait_ge(g_dve, 3)
            mm(bank(7, 16, P, 0), tri, gdec[:, 0:16])
            mm(bank(7, 4, NS, 16), cst[0:NS, C_TRIB:C_TRIB + NS], gdec[0:NS, 16:20])
            mm(bank(7, 16, P, 32), ones, gdec[:, 0:16])
            mm(bank(7, 4, NS, 48), cst[0:NS, C_GRP:C_GRP + NS], gdec[0:NS, 16:20]).then_inc(g_pe, 1)

            def out(b, h, cols, parts=P):
                return bank(b, cols, parts, h * cols)

            def rows(t):
                n, b = (P, 4 * (t % 2)) if t < 4 else (NS, 0)
                for h in range(GH):
                    c = 4 * t + h
                    mm(out(b, h, n), gdec[0:n, c:c + 1].broadcast_to([n, P]), tri if t < 4 else cst[0:n, C_TRIB:C_TRIB + n])
                    last = mm(out(b + 1, h, n), sm[0:n, t, 28 + h:29 + h].broadcast_to([n, P]), ident[0:n, 0:n])
                return last

            def gram(t, kb):
                n, b = (P, 4 * (t % 2)) if t < 4 else (NS, 0)
                for h in range(GH):
                    kh = ut[:, GH + h, P * t:P * t + n]
                    mm(out(b + 2, h, n, n), kh, heads(kb, n)[:, h])
                    last = mm(out(b + 3, h, n, n), kh, ut[:, h, P * t:P * t + n])
                return last

            def nat(t, b):
                n = P if t < 4 else NS
                for h in range(GH):
                    tr(out(b, h, P, n), ut[:, GH + h, P * t:P * t + n])
                    last = tr(out(b + 1, h, P, n), ut[:, 2 * GH + h, P * t:P * t + n])
                return last

            e.wait_ge(g_dve, PRE_DVE)
            e.wait_ge(nh_mul, len(HEADS))
            for t in range(5):
                if t < 4:
                    if t >= 2:
                        e.wait_ge(r_low, t - 1)
                    rows(t).then_inc(r_rows, 1)
                if t >= 1:
                    e.wait_ge(r_kb, t)
                    gram(t - 1, KB[(t - 1) % 2]).then_inc(r_gram, 1)

            def first_product(m):
                s, t = LEVELS[m]
                e.wait_ge(l_ct, m + 1)
                if m == 0:
                    e.wait_ge(r_low, 4)
                if m >= 4:
                    e.wait_ge(l_x, m - 3)
                if m >= 2:
                    e.wait_ge(l_t1c, m - 1)
                for h in range(GH):
                    last = mm(out(m % 2, h, P), heads(CT[m % 2])[:, h], heads(of("X", t))[:, h])
                last.then_inc(l_t1p, 1)

            def second_product(m):
                s, t = LEVELS[m]
                e.wait_ge(l_t1c, m + 1)
                if m >= 3:
                    e.wait_ge(l_x, m - 2)
                b = 2 + 2 * (m % 3)
                first, xt = heads(T1[m % 2]), heads(of("XT", t))
                if s < LV - 1:
                    for h in range(GH):
                        mm(out(b, h, P), xt[:, h], first[:, h])
                for h in range(GH):
                    last = mm(out(b + 1, h, P), first[:, h], xt[:, h])
                last.then_inc(l_t2, 1)

            first_product(0)
            for m in range(len(LEVELS)):
                if m + 1 < len(LEVELS):
                    first_product(m + 1)
                second_product(m)

            def w_product(t):
                e.wait_ge(q_vk, t + 1)
                if t >= 1:
                    e.wait_ge(q_nw, t)
                for h in range(GH):
                    last = mm(out(3, h, P), heads(KBEG[t % 2])[:, h], heads(of("XT", t))[:, h])
                last.then_inc(q_w, 1)

            e.wait_ge(l_x, len(LEVELS))
            nat(0, 0).then_inc(q_nat, 1)
            w_product(0)
            for t in range(4):
                e.wait_ge(q_nw, t + 1)
                if t > 0:
                    e.wait_ge(q_s, t)
                for h in range(GH):
                    mm(out(4, h, P), heads(of("XT", t))[:, h], heads(VB[t % 2])[:, h], True, False)
                    last = mm(out(4, h, P), heads("nwT")[:, h], heads("S")[:, h], False, True)
                last.then_inc(q_v, 1)
                if t < 3:
                    e.wait_ge(q_vk, t + 1)
                    nat(t + 1, 0).then_inc(q_nat, 1)
                e.wait_ge(q_vn, t + 1)
                if t > 0:
                    e.wait_ge(q_oc, t)
                for h in range(GH):
                    mm(out(5, h, P), heads("S")[:, h], heads(of("qeg", t))[:, h], True, False)
                    mm(out(5, h, P), heads("vnew")[:, h], heads(of("qk", t))[:, h], False, True)
                for h in range(GH):
                    last = mm(out(6, h, P), heads(KD[t % 2])[:, h], heads("vnew")[:, h])
                last.then_inc(q_o, 1)
                if t < 3:
                    w_product(t + 1)
                e.wait_ge(q_oc, t + 1)
                if t > 0:
                    e.wait_ge(q_rs, t)
                mm(bank(7), ones, W["sq"]).then_inc(q_n, 1)

            n = NS
            e.wait_ge(q_y, 4)
            rows(4).then_inc(g_pe, 1)
            e.wait_ge(g_dve, GDS.after("kb"))
            gram(4, "kbT").then_inc(g_pe, 1)
            nat(4, 4).then_inc(g_pe, 1)
            for s in range(LVS):
                e.wait_ge(g_dve, GDS.after(f"ct_{s}"))
                for h in range(GH):
                    last = mm(out(0, h, n, n), heads("CT", n, n)[:, h], heads("X", n, n)[:, h])
                last.then_inc(g_pe, 1)
                e.wait_ge(g_act, GCS.after(f"t1_{s}"))
                for h in range(GH):
                    mm(out(1, h, n, n), heads("XT", n, n)[:, h], heads("T1", n, n)[:, h])
                for h in range(GH):
                    last = mm(out(2, h, n, n), heads("T1", n, n)[:, h], heads("XT", n, n)[:, h])
                last.then_inc(g_pe, 1)
            e.wait_ge(g_dve, GDS.after(f"x_{LVS - 1}"))
            e.wait_ge(g_act, GCS.after("nat"))
            for h in range(GH):
                last = mm(out(3, h, n), heads("kbeg", P, n)[:, h], heads("XT", n, n)[:, h])
            last.then_inc(g_pe, 1)
            e.wait_ge(g_act, GCS.after("w"))
            e.wait_ge(st_in, 16)
            for h in range(GH):
                mm(out(4, h, n), heads("vb", P, n)[:, h], heads("XT", n, n)[:, h], True, False)
                for b in range(NB):
                    last = mm(bank(4, TS, P, h * n + TS * b), S_smp[:, b, h], heads("nwT", n)[:, h, TS * b:TS * b + TS], False, b == NB - 1)
            last.then_inc(g_pe, 1)
            e.wait_ge(g_act, GCS.after("v"))
            for h in range(GH):
                last = tr(out(5, h, P, n), heads("T1", n)[:, h])
            last.then_inc(g_pe, 1)
            e.wait_ge(g_act, GCS.after("vt"))
            for h in range(GH):
                mm(out(6, h, n), heads("vnew", P, n)[:, h], heads("qk", n, n)[:, h], True, False)
                for b in range(NB):
                    last = mm(bank(6, TS, P, h * n + TS * b), S_smp[:, b, h], heads("qeg", n)[:, h, TS * b:TS * b + TS], False, b == NB - 1)
            last.then_inc(g_pe, 1)
            e.wait_ge(g_act, GCS.after("o"))
            mm(bank(7, GH * n), ones, W["sq"][:, 0:GH * n]).then_inc(g_pe, 1)
            for h in range(GH):
                e.wait_ge(g_dve, GDS.after(f"vm{h}"))
                if h >= 2:
                    e.wait_ge(g_dve, GDS.after(f"add{h - 2}"))
                for q in range(2):
                    last = mm(bank(2 * (h % 2) + q), heads("kd", P, n)[:, h], vm[h % 2][:, 512 * q:512 * q + 512])
                last.then_inc(g_pe, 1)

            e.wait_ge(g_dve, GDS.end(1))
            for k in range(2):
                e.wait_ge((c_in, cv_in)[k], 16 * (18, 17)[k])
                for hc in range(2):
                    bk = 2 * k + hc
                    for jh in range(2):
                        u = 4 * k + 2 * hc + jh
                        e.wait_ge(w_ready[u % SLOTS], 16 * (R_CMP + u // SLOTS + 1))
                        for jj in range(16):
                            j = 16 * jh + jj
                            w = slot[u % SLOTS][:, jj]
                            mm(bank(bk, G * NCP), w, kvq[:, 2 * k:2 * k + 2, j:j + CS * (NCP - 1) + 1:CS], j == 0, j == CB - 1)
                            last = mm(bank(bk, 17 * NCS, P, G * NCP), w, segs_t[k][:, :, j:j + CS * (NCS - 1) + 1:CS],
                                      False, j == CB - 1)
                        last.then_inc(units, 1)
                e.wait_ge(units, U_CMP + 4 * k + 4)
                e.sem_inc(c_pe, 1)
            e.wait_ge(c_act, 1)
            for hc in range(2):
                last = mm(bank(4, NCOL), w2[:, 0, hc], hid[:, 0, hc], hc == 0, hc == 1)
            last.then_inc(c_pe, 1)
            e.wait_ge(c_act, 3)
            mm(bank(5, NCOL), ones, csq).then_inc(c_pe, 1)
            for g in range(G):
                for hc in range(2):
                    mm(bank(6, P, NCP, P * g), hid[:, 1, hc, NCP * g:NCP * (g + 1)], w2[:, 1, hc], hc == 0, hc == 1)
            for q in range(16):
                for hc in range(2):
                    c = G * NCP + NCS * q
                    last = mm(bank(q // 4, P, NCS, P * (q % 4)), hid[:, 1, hc, c:c + NCS], w2[:, 1, hc], hc == 0, hc == 1)
            last.then_inc(c_pe, 1)

            e.wait_ge(c_act, 5)
            for kind in range(2):
                for g in range(G):
                    for j in range(4):
                        last = tr(bank(2 * kind + g, P, P, P * j), kvq[:, 6 + 4 * kind + g, P * j:P * j + P])
            last.then_inc(v_pe, 1)

            e.wait_ge(v_act, 1)
            e.wait_ge(bf_in, 16)
            e.wait_ge(cv_in, 16 * 18)
            for h in range(QH):
                last = mm(bank(h), flip[:, 0:P], bfull[:, h])
            last.then_inc(turned_pe, 1)
            e.wait_ge(turned, 1)
            e.wait_ge(bs_in, 16 * REP)
            for g in range(G):
                last = mm(bank(g, KEYS, 16), flip[0:16, P:P + 16], biasS[:, g])
            last.then_inc(turned_pe, 1)

            e.wait_ge(c_dve, 1)
            e.wait_ge(turned, 2)
            for i in range(4):
                n = 7 + 8 * i
                if i > 0:
                    e.wait_ge(ac_dve, 2 * i)
                for h in range(QH):
                    last = mm(bank(4, n, P, NCP * h), kvq[:, N_A + h, P * i:P * i + P], kcT[:, NCP * (h // REP):NCP * (h // REP) + n])
                last.then_inc(ac_pe, 1)
                e.wait_ge(ac_dve, 2 * i + 2)
                if i > 0:
                    e.wait_ge(ac_act, 2 * i)
                for h in range(QH):
                    last = tr(bank(5 + h // 4, P, n, P * (h % 4)), sC[:, h, 0:n])
                last.then_inc(ac_pe, 1)
            e.wait_ge(ac_act, 8)

            def score(s):
                h, i = ATT[s]
                if s >= 2:
                    e.wait_ge(a_m, s - 1)
                for kind in range(2):
                    last = mm(bank(4 + 2 * (s % 2) + kind, P * (i + 1)), kvq[:, N_A + h, P * i:P * i + P],
                              kvq[:, 4 + 4 * kind + h // REP, 0:P * (i + 1)])
                last.then_inc(a_s, 1)

            def turn(s):
                h, i = ATT[s]
                for kind in range(2):
                    e.wait_ge(a_p, 2 * s + kind + 1)
                    if s >= 1:
                        e.wait_ge(a_pt, 2 * s + kind - 1)
                    for j in range(i + 1):
                        last = tr(bank(2 + kind, P, P, P * j), pS[s % 3][:, kind, P * j:P * j + P])
                    last.then_inc(a_t, 1)

            def values(s):
                h, i = ATT[s]
                y = bank(h % 2, P, P, P * i)
                if i == 0 and h >= 2:
                    e.wait_ge(a_ye, h - 1)
                n = 7 + 8 * i
                mm(y, vcP[0:n, h // REP], PTc[0:n, h, P * i:P * i + P], True, False)
                for kind in range(2):
                    e.wait_ge(a_pt, 2 * s + kind + 1)
                    for j in range(i + 1):
                        last = mm(y, VN[:, kind, h // REP, j], pT[s % 2][:, kind, P * j:P * j + P], False, kind == 1 and j == i)
                last.then_inc(a_y, 1)

            for s in range(len(ATT) + 3):
                if s < len(ATT):
                    score(s)
                if 2 <= s < len(ATT) + 2:
                    turn(s - 2)
                if s >= 3:
                    values(s - 3)

            for kind in range(3):
                for h in range(QH):
                    last = mm(bank(6 + kind // 2, NS, P, 256 * (kind % 2) + NS * h),
                              sm[0:NS, 4, QH * kind + h:QH * kind + h + 1].broadcast_to([NS, P]), ident[0:NS, 0:NS])
            last.then_inc(s_pe, 1)
            e.wait_ge(k_new, 1)
            e.wait_ge(a_ye, QH)
            for q in range(16):
                last = mm(bank(0, NCS, 16, NCS * q), qs[:, q // G, 16 * (q % G):16 * (q % G) + 16],
                          kcT[:, G * NCP + NCS * q:G * NCP + NCS * (q + 1)])
            last.then_inc(s_pe, 1)
            e.wait_ge(s_dve, 2)
            for q in range(16):
                last = tr(bank(1, 16, NCS, 16 * q), s_S.rearrange("p q k -> p (q k)")[:, NCS * q:NCS * q + NCS])
            last.then_inc(s_pe, 1)
            e.wait_ge(s_act, 3)
            for q in range(16):
                last = mm(bank(2, 16, P, 16 * q), vcS[:, q], s_PT[0:NCS, 16 * q:16 * q + 16])
            last.then_inc(s_pe, 1)
            for p in range(4):
                kind, bh = p // 2, p % 2
                e.wait_ge(s_dve, 3 * p + 3)
                e.wait_ge(k_new, p + 2)
                e.wait_ge(kv_in[bh], 16 * 16 * (kind + 1))
                for q in range(8):
                    last = mm(bank(q, KEYS, 16), qs[:, 4 * bh + q // G, 16 * (q % G):16 * (q % G) + 16], kbuf[bh][:, q // G, q % G])
                last.then_inc(s_pe, 1)
                e.wait_ge(s_dve, 3 * p + 4)
                for q in range(8):
                    c = TP + TS * (4 * bh + q // G)
                    last = tr(bank(2 + q // 4, P, TS, P * (q % 4)), kvq[:, 6 + 4 * kind + q % G, c:c + TS])
                last.then_inc(s_pe, 1)
                e.wait_ge(s_dve, 3 * p + 5)
                for q in range(8):
                    for j in range(2):
                        tr(bank(0, 16, P, 32 * q + 16 * j), s_S[:, q, P * j:P * j + P])
                    last = tr(bank(1, 16, TS, 16 * q), s_S[:, q, PAST:KEYS])
                last.then_inc(s_pe, 1)
                e.wait_ge(s_act, 5 + 2 * p)
                for q in range(8):
                    for j in range(2):
                        mm(bank(4, 16, P, 16 * q), vbuf[bh][:, q // G, j, q % G], s_PT[:, 32 * q + 16 * j:32 * q + 16 * j + 16], j == 0, False)
                    last = mm(bank(4, 16, P, 16 * q), s_VN[:, q], s_PN[:, 16 * q:16 * q + 16], False, True)
                last.then_inc(s_pe, 1)

            e.wait_ge(s_dve, 16)
            group_norm(1)
            group_norm(2)

            unit(0, H_OUT, 0, split0=SPLIT_0[1])
            unit(0, H_OUT + 2, 2)
            with e.Fori(1, KC // 2) as i:
                for s in range(2):
                    e.wait_ge(h_add, 2 * i + s - 1)
                    unit(i, H_OUT + 2 * s, 2 * s)
            group_norm(3)

            for part in range(PARTS):
                h0 = H_UP + 2 * U_PART * part
                for q in range(2):
                    if part > 0:
                        e.wait_ge(y_add, KC * part - 1 + q)
                    unit(0, h0 + 2 * q, 2 * q, split0=SPLIT_0[3] if part + q == 0 else None)
                with e.Fori(1, FQ) as i:
                    for q in range(2):
                        e.wait_ge(up_evac, 2 * i + (2 * FQ * part + q - 1))
                        unit(i, h0 + 2 * q, 2 * q)
                h0 += 4 * FQ
                for d in range(2):
                    e.wait_ge(up_evac, 2 * FQ * (part + 1) - 1 + d)
                    if d == 0:
                        e.wait_ge(act_lo, FQ * (part + 1) - 1)
                    unit(0, h0 + 2 * d, 2 * d, (ahi, alo), DH, FQ * (part + 1))
                with e.Fori(1, KC // 2) as i:
                    for d in range(2):
                        e.wait_ge(y_add, 2 * i + (KC * part + d - 1))
                        unit(i, h0 + 2 * d, 2 * d, (ahi, alo), DH)

        @block.scalar
        def _(e):
            n_chain = [0]

            def link(ins):
                n_chain[0] += 1
                ins.then_inc(a_chain, 1)
                e.wait_ge(a_chain, n_chain[0])

            def ln_exp():
                e.preload_act_table_set("natural_log_exp_and_others")

            def rstd(out, sums, scale, eps):
                link(e.activation(out, sums, ACT.Ln, bias=eps, scale=scale))
                return e.activation(out, out, ACT.Exp, scale=-0.5)

            def two_banks(b, n=NT):
                return bank(b, 256), bank(b + 1, NT - 256)

            def rstd_row(out, banks, scale, eps):
                lo, hi = halves(out)
                a, b = two_banks(banks)
                e.activation(lo, a, ACT.Ln, bias=eps, scale=scale)
                link(e.activation(hi, b, ACT.Ln, bias=eps, scale=scale))
                return e.activation(out, out, ACT.Exp, scale=-0.5)

            def group_norm(g):
                ln_exp()
                src = GROUPS[g][0]
                for k in range(GROUP_N[g]):
                    c = GROUP_0[g] + k
                    if k >= 2:
                        e.wait_ge(n_mm, c - 1)
                    if g == 0 and k % 4 == 0:
                        e.wait_ge(s_x[k // 4], 16)
                    e.activation(nrm_sq[k % 2], src[:, k], ACT.Square).then_inc(n_sq, 1)
                e.wait_ge(n_mm, GROUP_0[g] + GROUP_N[g])
                if g > 0:
                    e.wait_ge(n_mul, SPLIT_0[g])
                rstd_row(rs1, 4, 1.0 / (GROUP_N[g] * P), eps1).then_inc(n_rs, 1)
                if g == 0:
                    split(0, 0, first=True)
                    split(0, 1, first=True)
                for k in range(GROUP_N[g]):
                    e.wait_ge(n_mul, SPLIT_0[g] + k + 1)
                    e.activation(xhi[:, GROUPS[g][1] + k], tn[k % 4], ACT.Copy).then_inc(n_hi, 1)

            def split(i, h, extra=0, first=False, n=hw):
                e.wait_ge(w_ready[h % SLOTS], 16 * i + 16 * (h // SLOTS + 1 + extra))
                if not first:
                    u = 2 * i + h // 2
                    e.wait_ge(units if h % 2 else used, u + 8 if h % 2 and extra else u)
                e.activation(whi[h % 2][:, 0:n], raw[h % SLOTS][:, 0:n], ACT.Copy).then_inc(w_hi, 1)

            e.dma_start(relb, A["rel_bias"]).then_inc(s_tab, 16)
            e.dma_start(onehot, A["onehot"]).then_inc(s_tab, 16)
            e.dma_start(negt, A["neg"]).then_inc(s_tab, 16)
            e.wait_ge(t_dve, 1)
            e.dma_start(table_dram, tabs).then_inc(t_out, 16)
            e.dma_start(O["win_old"], A["cache_win"]).then_inc(stored, 16)
            e.wait_ge(t_out, 16)
            for r in range(REP):
                src = bass.AP(table_dram.tensor, r * TAB + PAST - TS, [[1, TS], [REP * TAB, G], [1, KEYS]])
                e.dma_start(biasS[TS * r:TS * r + TS], src).then_inc(bs_in, 16)

            e.wait_ge(s_cst, 16 * 7)
            group_norm(0)

            def copy_chunk(banks, dst, func=ACT.Copy):
                lo, hi = halves(dst)
                a, b = two_banks(banks)
                e.activation(lo, a, func)
                return e.activation(hi, b, func)

            for c in range(N_A):
                split(0, 2 * c + 2)
                split(0, 2 * c + 3)
                e.wait_ge(units, c + 1)
                copy_chunk(2 * (c % 2), abuf[:, c]).then_inc(proj_evac, 1)
            with e.Fori(0, N_KVQ // 2) as i:
                for s in range(2):
                    split(i, 2 * N_A + 2 * s + 2)
                    split(i, 2 * N_A + 2 * s + 3)
                    e.wait_ge(units, 2 * i + s + N_A + 1)
                    lo, hi = halves(at(KVQ, N_KVQ * NT).rearrange("p (k t) -> p k t", k=N_KVQ)[:, 2 * i + s])
                    e.activation(lo, bank(2 * s, 256), ACT.Copy)
                    e.activation(hi, bank(2 * s + 1, NT - 256), ACT.Copy).then_inc(proj_evac, 1)
            def silu_rows(c):
                e.wait_ge(gconv_dve, 4 * c + 4)
                e.wait_ge(tails, 1 + c + 1)
                e.activation(ut[:, c, 0:TP], cacc[c % 2][:, 0:TP], ACT.Silu)
                e.activation(smp(ut[:, c]), at(BF + 2384 + c % 2 * ROW4 + TP + 3, NB * SEG4).rearrange("p (b n) -> p b n", n=SEG4)[:, :, 0:TS],
                             ACT.Silu).then_inc(gconv_act, 1)

            def head_square(t):
                if t >= 2:
                    e.wait_ge(nh_mm, t - 1)
                e.activation(hn_sq[t >= NKQ][t % 2], HEADS[t][0], ACT.Square).then_inc(nh_sq, 1)

            def head_rstd(t):
                e.wait_ge(nh_mm, t + 1)
                if t >= 2:
                    e.wait_ge(nh_mul, t - 1)
                rstd_row(hn_rs[t >= NKQ][t % 2], (4 if t < NKQ else 0) + 2 * (t % 2), HEADS[t][2], HEADS[t][3]).then_inc(nh_rs, 1)

            e.wait_ge(a_free, 1)
            e.wait_ge(ya_out, 16)
            for c in range(N_A):
                split(0, 2 * (N_A + N_KVQ + c) + 2)
                split(0, 2 * (N_A + N_KVQ + c) + 3)
                e.wait_ge(units, N_A + N_KVQ + c + 1)
                a, b = two_banks(2 * (c % 2))
                e.activation(gbuf[:, c, 3:3 + 256], a, ACT.Copy)
                e.activation(gbuf[:, c, 3 + 256:3 + TP], b[:, 0:256], ACT.Copy)
                e.activation(gbuf[:, c, 3 + TP:ROW4].rearrange("p (b n) -> p b n", n=SEG4)[:, :, 3:SEG4],
                             b[:, 256:NT - 256].rearrange("p (b t) -> p b t", t=TS), ACT.Copy).then_inc(proj_evac, 1)
                ln_exp()
                if c > 0:
                    head_rstd(c - 1)
                head_square(c)
                if c > 0:
                    silu_rows(c - 1)
            silu_rows(N_A - 1)
            for c in range(GH):
                if c + 1 < GH:
                    split(0, 2 * (PROJ - GH + c) + 2)
                    split(0, 2 * (PROJ - GH + c) + 3)
                else:
                    e.wait_ge(gw_in, 16)
                    e.wait_ge(used, PROJ)
                    e.activation(whi[0][:, 0:32 * KC], raw[0][:, 0:32 * KC], ACT.Copy).then_inc(gw_hi, 1)
                e.wait_ge(units, PROJ - GH + c + 1)
                if c == 0:
                    ln_exp()
                    head_rstd(NKQ - 1)
                    e.wait_ge(nh_mul, NKQ)
                copy_chunk(2 * (c % 2), zbuf[:, c], ACT.Silu).then_inc(proj_evac, 1)

            e.wait_ge(gconv_act, N_A)
            e.wait_ge(proj_evac, PROJ)
            e.wait_ge(gates_mm, 1)
            ln_exp()
            head_square(NKQ)
            for t in range(NKQ, len(HEADS)):
                if t + 1 < len(HEADS):
                    head_square(t + 1)
                head_rstd(t)
            e.wait_ge(nh_mul, len(HEADS))
            e.dma_start(O["kv_t"], kvq[:, 0:N_A]).then_inc(stored, 16)

            e.wait_ge(g_dve, 1)
            e.activation(sm[:, :, 0:24], sm[:, :, 0:24], ACT.Sigmoid)
            link(e.activation(sm[:, :, 28:32], sm[:, :, 28:32], ACT.Sigmoid))
            e.sem_inc(g_act, 1)
            ln_exp()
            e.wait_ge(g_dve, 2)
            link(e.activation(soft2, soft2, ACT.Exp))
            e.activation(soft2, soft2, ACT.Ln, bias=one)
            e.activation(gdn_in[:, 0:4], gdn_in[:, 0:4], ACT.Exp).then_inc(g_act, 1)
            e.wait_ge(g_dve, 4)
            e.activation(egc, gc, ACT.Exp)
            e.activation(ekd, ekd, ACT.Exp).then_inc(g_act, 1)

            for t in range(4):
                e.wait_ge(r_dec, t + 1)
                e.activation(W[DEC[t % 2]], W[DEC[t % 2]], ACT.Exp)
                e.activation(W[EG[t % 2]], bank(4 * (t % 2)), ACT.Exp).then_inc(r_exp, 1)
            for m in range(len(LEVELS)):
                e.wait_ge(l_t1p, m + 1)
                if m >= 2:
                    e.wait_ge(l_t2, m - 1)
                e.activation(W[T1[m % 2]], bank(m % 2), ACT.Copy).then_inc(l_t1c, 1)
            def w_negated(t):
                e.wait_ge(q_w, t + 1)
                if t >= 1:
                    e.wait_ge(q_v, t)
                e.activation(W["nwT"], bank(3), ACT.Copy, scale=-1.0).then_inc(q_nw, 1)

            w_negated(0)
            for t in range(4):
                e.wait_ge(q_v, t + 1)
                if t > 0:
                    e.wait_ge(q_o, t)
                e.activation(W["vnew"], bank(4), ACT.Copy).then_inc(q_vn, 1)
                e.wait_ge(q_o, t + 1)
                if t > 0:
                    e.wait_ge(q_y, t)
                    e.wait_ge(q_n, t)
                e.activation(W["oT"], bank(5), ACT.Copy)
                e.activation(W["sq"], bank(5), ACT.Square).then_inc(q_oc, 1)
                if t < 3:
                    w_negated(t + 1)
                e.wait_ge(q_n, t + 1)
                rstd(W["rs"], bank(7), 1.0 / P, eps1).then_inc(q_rs, 1)

            n, w = NS, GH * NS
            e.wait_ge(g_dve, GDS.after("dec"))
            e.activation(W["decT"][0:n, 0:w], W["decT"][0:n, 0:w], ACT.Exp)
            e.activation(W["eg"][:, 0:w], bank(0, w), ACT.Exp).then_inc(g_act, 1)
            e.wait_ge(g_pe, GPS.after("nat"))
            for h in range(GH):
                c = 16 + h
                e.activation(heads("vb", P, n)[:, h], bank(5, P, n, P * h), ACT.Copy, scale=sm[0:n, 4, 28 + h:29 + h])
                e.activation(heads("kbeg", P, n)[:, h], bank(4, P, n, P * h), ACT.Copy, scale=beg[0:n, c:c + 1])
                last = e.activation(heads("kd", P, n)[:, h], bank(4, P, n, P * h), ACT.Copy, scale=ekd[0:n, c:c + 1])
            last.then_inc(g_act, 1)
            for s in range(LVS):
                e.wait_ge(g_pe, GPS.after(f"t1_{s}"))
                e.activation(W["T1"][0:n, 0:w], bank(0, w, n), ACT.Copy).then_inc(g_act, 1)
            e.wait_ge(g_pe, GPS.after("w"))
            e.activation(W["nwT"][:, 0:w], bank(3, w), ACT.Copy, scale=-1.0).then_inc(g_act, 1)
            e.wait_ge(g_pe, GPS.after("v"))
            e.activation(W["T1"][:, 0:w], bank(4, w), ACT.Copy).then_inc(g_act, 1)
            e.wait_ge(g_pe, GPS.after("vt"))
            e.activation(W["vnew"][0:n], bank(5, 512, n), ACT.Copy).then_inc(g_act, 1)
            e.wait_ge(g_pe, GPS.after("o"))
            e.activation(W["oT"][:, 0:w], bank(6, w), ACT.Copy)
            e.activation(W["sq"][:, 0:w], bank(6, w), ACT.Square).then_inc(g_act, 1)
            e.wait_ge(g_pe, GPS.after("n"))
            rstd(W["rs"][:, 0:w], bank(7, w), 1.0 / P, eps1).then_inc(g_act, 1)

            e.wait_ge(units, U_CMP + 1)
            e.wait_ge(gdn_stored, 64)
            src = bass.AP(table_dram.tensor, 0, [[1, P], [TAB, QH], [1, 512]])
            e.dma_start(bfull, src).then_inc(bf_in, 16)

            for k in range(2):
                e.wait_ge(c_pe, k + 1)
                for hc in range(2):
                    link(e.activation(pebs[:, 2 * k + hc:2 * k + hc + 1], bank(2 * k + hc, 1, P, NCOL), ACT.Copy))
                    last = e.activation(hid[:, k, hc], bank(2 * k + hc, NCOL), ACT.Gelu_apprx_tanh, bias=pebs[:, 2 * k + hc:2 * k + hc + 1])
                last.then_inc(c_act, 1)
            ln_exp()
            e.wait_ge(c_pe, 3)
            e.activation(kcT, bank(4, NCOL), ACT.Copy)
            e.activation(csq, bank(4, NCOL), ACT.Square).then_inc(c_act, 1)
            e.wait_ge(c_pe, 4)
            rstd(crs, bank(5, NCOL), 1.0 / P, eps1).then_inc(c_act, 1)
            e.wait_ge(c_pe, 5)
            for g in range(G):
                e.activation(vcP[:, g], bank(6, P, NCP, P * g), ACT.Copy)
            e.activation(vcS.rearrange("p q d -> p (q d)"), ps[0:NCS, 0:2048], ACT.Copy).then_inc(c_act, 1)

            e.wait_ge(c_act, 5)
            e.wait_ge(v_pe, 1)
            for b in range(4):
                last = e.activation(VN[:, b // 2, b % 2].rearrange("p j d -> p (j d)"), bank(b), ACT.Copy)
            last.then_inc(v_act, 1)
            e.wait_ge(turned_pe, 1)
            for h in range(QH):
                last = e.activation(bfull[:, h], bank(h), ACT.Copy)
            last.then_inc(turned, 1)
            e.wait_ge(turned_pe, 2)
            for g in range(G):
                last = e.activation(biasS[:, g], bank(g, KEYS, 16), ACT.Copy)
            last.then_inc(turned, 1)

            for i in range(4):
                n = 7 + 8 * i
                e.wait_ge(ac_dve, 2 * i + 1)
                e.activation(sC[:, :, 0:n], sC[:, :, 0:n], ACT.Exp).then_inc(ac_act, 1)
                e.wait_ge(ac_pe, 2 * i + 2)
                for q in range(2):
                    last = e.activation(PTc[0:n, 4 * q:4 * q + 4, P * i:P * i + P],
                                        bank(5 + q, 512, n).rearrange("p (h t) -> p h t", h=4), ACT.Copy)
                last.then_inc(ac_act, 1)

            def exps(s):
                h, i = ATT[s]
                e.wait_ge(a_m, s + 1)
                for kind in range(2):
                    x, c = pS[s % 3][:, kind, 0:P * (i + 1)], 2 * (s % 2) + kind
                    last = e.activation(x, x, ACT.Exp, bias=mx[:, c:c + 1], accum_out=zz[:, c:c + 1])
                last.then_inc(a_e, 1)

            def copies(s):
                h, i = ATT[s]
                n = P * (i + 1)
                if s >= 2:
                    e.wait_ge(a_y, s - 1)
                for kind in range(2):
                    e.wait_ge(a_t, 2 * s + kind + 1)
                    e.activation(pT[s % 2][:, kind, 0:n], bank(2 + kind, n), ACT.Copy).then_inc(a_pt, 1)

            def head_out(h):
                e.wait_ge(a_y, 4 * h + 4)
                e.activation(mix[:, 4 + h, 0:TP], bank(h % 2), ACT.Copy).then_inc(a_ye, 1)

            for s in range(len(ATT) + 2):
                if s < len(ATT):
                    exps(s)
                if s >= 2:
                    copies(s - 2)
                if s >= 7 and s % 4 == 3:
                    head_out((s - 7) // 4)
            head_out(QH - 1)

            e.wait_ge(s_pe, 1)
            for kind in range(3):
                link(e.activation(grow[:, kind].rearrange("p (b h t) -> p b h t", b=NB, h=QH),
                                  bank(6 + kind // 2, 256, P, 256 * (kind % 2)).rearrange("p (h b t) -> p b h t", h=QH, b=NB), ACT.Copy))
            e.sem_inc(s_act, 1)
            sC2 = s_S.rearrange("p q k -> p (q k)")[:, 0:16 * NCS]
            e.wait_ge(s_dve, 1)
            e.activation(sC2, sC2, ACT.Exp).then_inc(s_act, 1)
            e.wait_ge(s_pe, 3)
            e.activation(s_PT[0:NCS, 0:256], bank(1, 256, NCS), ACT.Copy).then_inc(s_act, 1)
            for p in range(4):
                e.wait_ge(s_dve, 3 * p + 4)
                e.activation(s_S, s_S, ACT.Exp).then_inc(s_act, 1)
                e.wait_ge(s_pe, 4 * p + 7)
                e.activation(s_PT, bank(0, 256), ACT.Copy)
                e.activation(s_PN, bank(1, P, TS), ACT.Copy)
                e.activation(s_VN.rearrange("p q d -> p (q d)"), ps[0:TS, 1024:2048], ACT.Copy).then_inc(s_act, 1)

            e.wait_ge(ya_in, 16)
            group_norm(1)
            group_norm(2)

            for c in range(4):
                e.wait_ge(n_mul, SPLIT_0[3] - 3 + c)
                e.activation(xhi[:, 12 + c], tn[c], ACT.Copy).then_inc(n_hi, 1)
            for c in range(2):
                e.dma_start(xin[c], A["x_t"][:, c]).then_inc(x_in[c], 16)
            for h in range(SLOTS):
                split(0, H_OUT + h, R_OUT - R_CMP)
            with e.Fori(1, KC // 2) as i:
                for c in range(2):
                    split(i, H_OUT + 2 * c, R_OUT - R_CMP)
                    split(i, H_OUT + 2 * c + 1, R_OUT - R_CMP)
                    e.wait_ge(h_add, 2 * i + c - 1)
                    e.dma_start(xin[c], A["x_t"][:, 2 * i + c]).then_inc(x_in[c], 16)
            split(0, H_UP, R_OUT - R_CMP)
            split(0, H_UP + 1, R_OUT - R_CMP)
            e.wait_ge(h_add, KC)
            group_norm(3)

            e.wait_ge(n_lo, SPLIT_0[3] + 16)
            for dst, name in ((hist, "hist_f"), (fw, "ffn_w")):
                e.dma_start(dst, A[name]).then_inc(f_in, 16)

            def split_unit(i, h, tiles=(HALF_K, HALF_K)):
                split(i, h, R_OUT - R_CMP, n=P * tiles[0])
                split(i, h + 1, R_OUT - R_CMP, n=P * tiles[1])

            def up(i, part, first, last):
                h0 = H_UP + 2 * U_PART * part
                for q in range(2):
                    split_unit(i, h0 + 2 * q + 2, DH if last and q else (HALF_K, HALF_K))
                    u = 2 * i + (2 * FQ * part + q)
                    e.wait_ge(units, 2 * i + (U_UP + U_PART * part + q + 1))
                    if not first:
                        e.wait_ge(up_conv, 3 * u - 3)
                        e.wait_ge(up_tail, u - 1)
                    prompt, sample = rows3(fx[q])
                    a, b = two_banks(2 * q)
                    e.activation(prompt[:, 0:256], a, ACT.Copy)
                    e.activation(prompt[:, 256:TP], b[:, 0:256], ACT.Copy)
                    e.activation(sample, b[:, 256:NT - 256].rearrange("p (b t) -> p b t", t=TS), ACT.Copy).then_inc(up_evac, 1)
                e.wait_ge(up_conv, 3 * u)
                e.activation(facc[0], facc[0], ACT.Silu).then_inc(up_silu, 1)
                e.wait_ge(up_act, i + (FQ * part + 1))
                e.activation(ahi[:, i], aw_, ACT.Copy).then_inc(act_hi, 1)

            for part in range(PARTS):
                up(0, part, part == 0, False)
                with e.Fori(1, FQ - 1) as i:
                    up(i, part, False, False)
                up(FQ - 1, part, False, True)
                h0 = H_UP + 2 * U_PART * part + 4 * FQ
                with e.Fori(0, KC // 2 - 1) as i:
                    split_unit(i, h0 + 2, DH)
                    split_unit(i, h0 + 4, DH)
                split_unit(KC // 2 - 1, h0 + 2, DH)
                if part < PARTS - 1:
                    split_unit(KC // 2 - 1, h0 + 4)

        @block.vector
        def _(e):
            n_chain = [0]

            def link(ins):
                n_chain[0] += 1
                ins.then_inc(d_chain, 1)
                e.wait_ge(d_chain, n_chain[0])

            def group_norm(g):
                src, c0, col = GROUPS[g]
                e.wait_ge(n_rs, g + 1)
                if g == 0:
                    split(0, 0)
                    split(0, 1)
                for k in range(GROUP_N[g] + 1):
                    if k < GROUP_N[g]:
                        e.scalar_tensor_tensor(out=tn[k % 4], in0=src[:, k], scalar=gain[:, col + k:col + k + 1], in1=rs1,
                                               op0=ALU.mult, op1=ALU.mult).then_inc(n_mul, 1)
                    if k >= 1:
                        e.wait_ge(n_hi, SPLIT_0[g] + k)
                        e.tensor_tensor(xlo[:, c0 + k - 1], tn[(k - 1) % 4], xhi_f[:, c0 + k - 1], ALU.subtract).then_inc(n_lo, 1)

            def split(i, h, n=hw):
                e.wait_ge(w_hi, SLOTS * i + (h + 1))
                e.tensor_tensor(wlo[h % 2][:, 0:n], raw[h % SLOTS][:, 0:n], whi_f[h % 2][:, 0:n], ALU.subtract).then_inc(w_lo, 1)

            e.memset(xa[:, 0:2], 0.0)
            e.memset(gc, 0.0)
            e.memset(gl, 0.0)
            link(e.memset(sm.rearrange("p c n -> p (c n)"), 0.0))
            e.wait_ge(t_pe, 1)
            e.wait_ge(s_tab, 48)
            e.tensor_tensor(tabs[:, 0:320], bank(6, 320, QH), negt[:, 0:320], ALU.add)
            e.tensor_tensor(tabs[:, 320:TAB], bank(7, 320, QH), negt[:, 320:TAB], ALU.add).then_inc(t_dve, 1)

            e.wait_ge(s_cst, 16 * 7)
            for q in range(4):
                e.wait_ge(s_x[q], 16)
            group_norm(0)

            e.wait_ge(n_mul, 16)
            up_, us_ = rows3(xa)
            for j in range(4):
                for h in range(6):
                    split(0, 6 * j + 2 + h)
                e.wait_ge(proj_evac, 3 * j + 3)
                cc, hh, bb = abuf[:, 3 * j], abuf[:, 3 * j + 1], abuf[:, 3 * j + 2]
                e.tensor_copy(xa[:, 2 + TP:ROW3].rearrange("p (b n) -> p b n", n=SEG3)[:, :, 0:2], hist_a[:, j])
                e.tensor_tensor(up_, cc[:, 0:TP], hh[:, 0:TP], ALU.mult)
                link(e.tensor_tensor(us_, smp(cc), smp(hh), ALU.mult))
                e.tensor_copy(tail_a[:, j, 0:2], xa[:, TP:TP + 2])
                e.tensor_copy(tail_a[:, j, 2:18].rearrange("p (b k) -> p b k", k=2), us_[:, :, 2:4])
                link(e.tensor_scalar(acc_a, xa[:, 0:ROW3 - 2], aw[:, j, 0:1], None, ALU.mult))
                for k in (1, 2):
                    link(e.scalar_tensor_tensor(out=acc_a, in0=xa[:, k:ROW3 - 2 + k], scalar=aw[:, j, k:k + 1], in1=acc_a,
                                                op0=ALU.mult, op1=ALU.add))
                e.tensor_tensor(zbuf[:, j, 0:TP], acc_a[:, 0:TP], bb[:, 0:TP], ALU.mult)
                link(e.tensor_tensor(smp(zbuf[:, j]), at(BF + 512 + ROW3 + 2 + TP, NB * SEG3).rearrange("p (b n) -> p b n", n=SEG3)[:, :, 0:TS],
                                     smp(bb), ALU.mult))
            e.sem_inc(a_free, 1)
            e.sem_inc(tails, 1)
            split(0, 2 * N_A + 2)
            split(0, 2 * N_A + 3)
            with e.Fori((N_A + 2) // 2, (N_A + N_KVQ) // 2) as i:
                for h in range(SLOTS):
                    split(i, h)
            split(0, 2 * (N_A + N_KVQ))
            split(0, 2 * (N_A + N_KVQ) + 1)

            def head_norm(t):
                rows, col = HEADS[t][0:2]
                rs = hn_rs[t >= NKQ][t % 2]
                e.wait_ge(nh_rs, t + 1)
                if col is None:
                    e.tensor_tensor(rows, rows, rs, ALU.mult).then_inc(nh_mul, 1)
                else:
                    e.scalar_tensor_tensor(out=rows, in0=rows, scalar=gain[:, col:col + 1], in1=rs,
                                           op0=ALU.mult, op1=ALU.mult).then_inc(nh_mul, 1)

            e.wait_ge(gconv_in, 1)
            for c in range(N_A):
                h = 2 * (N_A + N_KVQ + c + 1)
                split(0, h)
                split(0, h + 1)
                e.wait_ge(proj_evac, N_A + N_KVQ + c + 1)
                if c >= 2:
                    e.wait_ge(gconv_act, c - 1)
                acc, g = cacc[c % 2], gbuf[:, c]
                e.tensor_scalar(acc, g[:, 0:ROW4 - 3], gw[:, c, 0:1], None, ALU.mult).then_inc(gconv_dve, 1)
                for k in (1, 2, 3):
                    e.wait_ge(gconv_dve, 4 * c + k)
                    e.scalar_tensor_tensor(out=acc, in0=g[:, k:ROW4 - 3 + k], scalar=gw[:, c, k:k + 1], in1=acc,
                                           op0=ALU.mult, op1=ALU.add).then_inc(gconv_dve, 1)
                if c > 0:
                    head_norm(c - 1)
            for h in range(2 * (PROJ - GH) + 2, 2 * PROJ):
                split(0, h)
                if h == 2 * (PROJ - GH) + 3:
                    head_norm(NKQ - 1)
            e.wait_ge(gw_hi, 1)
            e.tensor_tensor(wlo[0][:, 0:32 * KC], raw[0][:, 0:32 * KC], whi_f[0][:, 0:32 * KC], ALU.subtract).then_inc(gw_lo, 1)

            for t in range(NKQ, len(HEADS)):
                head_norm(t)

            e.wait_ge(gates_mm, 1)
            e.tensor_copy(sm[:, 0:4, :], bank(6, 128).rearrange("p (c n) -> p c n", n=32))
            link(e.tensor_copy(sm[0:NS, 4, :], bank(6, 32, NS, 128)))
            e.sem_inc(g_dve, 1)
            s5 = soft.rearrange("p (c h) -> p c h", h=GH)
            link(e.tensor_tensor(s5, sm[:, :, 24:28], gdn_in[:, 4:8].unsqueeze(1).broadcast_to([P, 5, GH]), ALU.add))
            e.scalar_tensor_tensor(out=soft2, in0=soft, scalar=-1.0, in1=soft, op0=ALU.mult, op1=ALU.min).then_inc(g_dve, 1)
            e.wait_ge(g_act, 2)
            link(e.scalar_tensor_tensor(out=soft, in0=soft, scalar=0.0, in1=soft2, op0=ALU.max, op1=ALU.add))
            e.scalar_tensor_tensor(out=gdec.rearrange("p (c h) -> p c h", h=GH), in0=s5, scalar=-1.0,
                                   in1=gdn_in[:, 0:4].unsqueeze(1).broadcast_to([P, 5, GH]), op0=ALU.mult, op1=ALU.mult).then_inc(g_dve, 1)
            e.wait_ge(g_pe, 1)
            e.tensor_copy(gc[:, 0:16], bank(7, 16))
            e.tensor_copy(gc[0:NS, 16:20], bank(7, 4, NS, 16))
            e.tensor_copy(gl[:, 0:16], bank(7, 16, P, 32))
            link(e.tensor_copy(gl[0:NS, 16:20], bank(7, 4, NS, 48)))
            e.tensor_tensor(ekd, gl, gc, ALU.subtract).then_inc(g_dve, 1)
            e.wait_ge(g_act, 3)
            link(e.memset(W["S"], 0.0))
            e.tensor_tensor(beg.rearrange("p (c h) -> p c h", h=GH), egc.rearrange("p (c h) -> p c h", h=GH), sm[:, :, 28:32],
                            ALU.mult).then_inc(g_dve, 1)

            def b3(i, n, parts=P):
                return bank(i, GH * n, parts).rearrange("p (h i) -> p h i", h=GH)

            def decay(t, n, b, dst):
                for h in range(GH):
                    last = e.tensor_scalar(heads(dst, n, n)[:, h], bank(b, n, n, n * h), gc[0:n, 4 * t + h:4 * t + h + 1], 0.0,
                                           ALU.subtract, ALU.min)
                return last

            def decayed(t, n, b, dec, eg):
                mtri = (tri if t < 4 else cst[0:n, C_TRIB:C_TRIB + n]).unsqueeze(1).broadcast_to([n, GH, n])
                idb = ident[0:n, 0:n].unsqueeze(1).broadcast_to([n, GH, n])
                qk = heads(of("qk", t), n, n)
                e.tensor_tensor(heads(of("qeg", t), n), ut[:, 0:GH, P * t:P * t + n], heads(eg, n), ALU.mult)
                link(e.tensor_tensor(qk, b3(b + 3, n, n), heads(dec, n, n), ALU.mult))
                e.scalar_tensor_tensor(out=heads(of("nl", t), n, n), in0=b3(b + 2, n, n), scalar=-1.0, in1=heads(dec, n, n),
                                       op0=ALU.mult, op1=ALU.mult)
                e.tensor_tensor(qk, qk, mtri, ALU.mult)
                e.tensor_copy(heads(of("X", t), n, n), idb)
                return e.tensor_copy(heads(of("XT", t), n, n), idb)

            def level_mask(s, n):
                return cst[0:n, C_LEV + P * s:C_LEV + P * s + n].unsqueeze(1).broadcast_to([n, GH, n])

            for t in range(5):
                if t < 4:
                    e.wait_ge(r_rows, t + 1)
                    if t >= 2:
                        e.wait_ge(r_low, t - 1)
                        e.wait_ge(r_gram, t - 1)
                    decay(t, P, 4 * (t % 2), DEC[t % 2]).then_inc(r_dec, 1)
                    e.tensor_tensor(heads(KB[t % 2]), ut[:, GH:2 * GH, P * t:P * t + P], b3(4 * (t % 2) + 1, P), ALU.mult).then_inc(r_kb, 1)
                if t >= 1:
                    u = t - 1
                    e.wait_ge(r_exp, u + 1)
                    e.wait_ge(r_gram, u + 1)
                    e.tensor_copy(egl[:, 4 * u:4 * u + 4], heads(EG[u % 2])[:, :, P - 1])
                    decayed(u, P, 4 * (u % 2), DEC[u % 2], EG[u % 2]).then_inc(r_low, 1)

            def masked(m):
                s, t = LEVELS[m]
                if m >= 2:
                    e.wait_ge(l_t1p, m - 1)
                e.tensor_tensor(heads(CT[m % 2]), heads(of("nl", t)), level_mask(s, P), ALU.mult).then_inc(l_ct, 1)

            e.wait_ge(r_low, 4)
            masked(0)
            for m in range(len(LEVELS)):
                s, t = LEVELS[m]
                if m + 1 < len(LEVELS):
                    masked(m + 1)
                e.wait_ge(l_t2, m + 1)
                if m >= 4:
                    e.wait_ge(l_x, m - 3)
                b = 512 * (2 + 2 * (m % 3))
                x, y = (XX[t], ps[:, b:b + 1024]) if s < LV - 1 else (W[of("XT", t)], ps[:, b + 512:b + 1024])
                e.tensor_tensor(x, x, y, ALU.add).then_inc(l_x, 1)

            def scaled(t):
                e.wait_ge(q_nat, t + 1)
                if t >= 2:
                    e.wait_ge(q_o, t - 1)
                e.tensor_tensor(heads(KBEG[t % 2]), b3(0, P), beg[:, 4 * t:4 * t + 4].unsqueeze(2).broadcast_to([P, GH, P]), ALU.mult)
                e.tensor_tensor(heads(KD[t % 2]), b3(0, P), ekd[:, 4 * t:4 * t + 4].unsqueeze(2).broadcast_to([P, GH, P]), ALU.mult)
                e.tensor_tensor(heads(VB[t % 2]), b3(1, P), sm[:, t, 28:32].unsqueeze(2).broadcast_to([P, GH, P]), ALU.mult).then_inc(q_vk, 1)

            def y_c(t, n):
                w = GH * n
                link(e.scalar_tensor_tensor(out=W["oT"][:, 0:w], in0=W["oT"][:, 0:w], scalar=gain[:, G_GDN:G_GDN + 1], in1=W["rs"][:, 0:w],
                                            op0=ALU.mult, op1=ALU.mult))
                return e.tensor_tensor(mix[:, 12:16, P * t:P * t + n], heads("oT", n), zbuf[:, :, P * t:P * t + n], ALU.mult)

            scaled(0)
            for t in range(4):
                if t < 3:
                    scaled(t + 1)
                e.wait_ge(q_o, t + 1)
                if t > 0:
                    e.wait_ge(q_s, t)
                for h in range(GH):
                    last = e.scalar_tensor_tensor(out=heads("S")[:, h], in0=heads("S")[:, h], scalar=egl[:, 4 * t + h:4 * t + h + 1],
                                                  in1=bank(6, P, P, P * h), op0=ALU.mult, op1=ALU.add)
                last.then_inc(q_s, 1)
                e.wait_ge(q_rs, t + 1)
                y_c(t, P).then_inc(q_y, 1)

            n, w = NS, GH * NS
            e.wait_ge(g_pe, GPS.after("rows"))
            e.wait_ge(q_y, 4)
            decay(4, n, 0, "decT").then_inc(g_dve, 1)
            e.tensor_tensor(heads("kbT", n), ut[:, GH:2 * GH, TP:NT], b3(1, n), ALU.mult).then_inc(g_dve, 1)
            e.wait_ge(g_act, GCS.after("dec"))
            e.wait_ge(g_pe, GPS.after("gram"))
            link(decayed(4, n, 0, "decT", "eg"))
            e.sem_inc(g_dve, 2)
            for s in range(LVS):
                link(e.tensor_tensor(heads("CT", n, n), heads("nl", n, n), level_mask(s, n), ALU.mult))
                e.sem_inc(g_dve, 1)
                e.wait_ge(g_pe, GPS.after(f"t2_{s}"))
                e.tensor_tensor(heads("X", n, n), heads("X", n, n), b3(1, n, n), ALU.add)
                link(e.tensor_tensor(heads("XT", n, n), heads("XT", n, n), b3(2, n, n), ALU.add))
                e.sem_inc(g_dve, 1)
            e.wait_ge(g_pe, GPS.after("o"))

            def vm_(h):
                e.tensor_tensor(vm[h % 2].rearrange("p (b d) -> p b d", b=NB),
                                heads("vnew", P, n)[:, h].unsqueeze(1).broadcast_to([n, NB, P]),
                                cst[0:n, C_BM:C_BM + NB].unsqueeze(2).broadcast_to([n, NB, P]), ALU.mult).then_inc(g_dve, 1)

            def add_(h):
                e.wait_ge(g_pe, GPS.after(f"ds{h}"))
                b = 2 * (h % 2)
                e.tensor_tensor(S_smp[:, :, h], S_smp[:, :, h],
                                ps[:, 512 * b:512 * b + 1024].rearrange("p (b d) -> p b d", b=NB), ALU.add).then_inc(g_dve, 1)

            last_decay = W["eg"][:, 0:w].rearrange("p (h b t) -> p b h t", h=GH, t=TS)[:, :, :, TS - 1].unsqueeze(3).broadcast_to([P, NB, GH, P])
            link(e.tensor_tensor(S_smp, S_smp, last_decay, ALU.mult))
            e.sem_inc(g_dve, 1)
            vm_(0)
            e.wait_ge(g_act, GCS.after("n"))
            y_c(4, n).then_inc(g_dve, 1)
            vm_(1)
            add_(0)
            vm_(2)
            add_(1)
            vm_(3)
            add_(2)
            add_(3)

            e.wait_ge(c_act, 4)
            e.scalar_tensor_tensor(out=kcT, in0=kcT, scalar=gain[:, G_K:G_K + 1], in1=crs, op0=ALU.mult, op1=ALU.mult).then_inc(c_dve, 1)

            e.wait_ge(turned, 2)
            e.wait_ge(g_act, GCS.end(1))
            for i in range(4):
                n = 7 + 8 * i
                x0 = CB - 1 + 384 - P * i
                s = sC[:, :, 0:n]
                e.wait_ge(ac_pe, 2 * i + 1)
                if i > 0:
                    e.wait_ge(ac_pe, 2 * i)
                link(e.tensor_tensor(s, bank(4, QH * NCP).rearrange("p (h c) -> p h c", h=QH)[:, :, 0:n],
                                     bfull[:, :, x0:x0 + CS * (n - 1) + 1:CS], ALU.add))
                link(e.tensor_reduce(mx[:, 0:QH], s, AX, ALU.max))
                e.tensor_tensor(s, s, mx[:, 0:QH].unsqueeze(2).broadcast_to([P, QH, n]), ALU.subtract).then_inc(ac_dve, 1)
                e.wait_ge(ac_act, 2 * i + 1)
                if i == 0:
                    link(e.tensor_tensor(s, s, cst[:, C_VAL:C_VAL + n].unsqueeze(1).broadcast_to([P, QH, n]), ALU.mult))
                link(e.tensor_reduce(zz[:, 0:QH], s, AX, ALU.add))
                link(e.tensor_scalar(zz[:, 0:QH], zz[:, 0:QH], 1.0, None, ALU.max))
                link(e.reciprocal(rz[:, 0:QH], zz[:, 0:QH]))
                link(e.tensor_tensor(rz[:, 0:QH], rz[:, 0:QH], sm[:, i, 0:QH], ALU.mult))
                e.tensor_tensor(s, s, rz[:, 0:QH].unsqueeze(2).broadcast_to([P, QH, n]), ALU.mult).then_inc(ac_dve, 1)

            def scores(s):
                h, i = ATT[s]
                n, c = P * (i + 1), 2 * (s % 2)
                x = pS[s % 3][:, :, 0:n]
                e.wait_ge(a_s, s + 1)
                if s >= 3:
                    e.wait_ge(a_t, 2 * (s - 2))
                b = 512 * (4 + 2 * (s % 2))
                link(e.tensor_tensor(x, ps[:, b:b + 1024].rearrange("p (k t) -> p k t", k=2)[:, :, 0:n],
                                     bfull[:, h, 384 - P * i:512].unsqueeze(1).broadcast_to([P, 2, n]), ALU.add))
                e.tensor_reduce(mx[:, c:c + 2], x, AX, ALU.max, negate=True).then_inc(a_m, 1)

            def scale(s):
                h, i = ATT[s]
                n, c = P * (i + 1), 2 * (s % 2)
                e.wait_ge(a_e, s + 1)
                link(e.reciprocal(rz[:, c:c + 2], zz[:, c:c + 2]))
                link(e.tensor_tensor(rz[:, c:c + 2], rz[:, c:c + 2], sm[:, i, QH + h:QH + h + QH + 1:QH], ALU.mult))
                for kind in range(2):
                    x = pS[s % 3][:, kind, 0:n]
                    e.tensor_scalar(x, x, rz[:, c + kind:c + kind + 1], None, ALU.mult).then_inc(a_p, 1)

            e.wait_ge(ac_pe, 8)
            for s in range(len(ATT) + 1):
                if s < len(ATT):
                    scores(s)
                if s >= 1:
                    scale(s - 1)

            for h in range(QH):
                last = e.tensor_copy(qs[:, :, TS * h:TS * h + TS], smp(kvq[:, N_A + h]))
            link(last)
            e.sem_inc(k_new, 1)

            def softmax(s, q, n, step):
                link(e.tensor_reduce(mx[0:16, 0:q], s, AX, ALU.max))
                e.tensor_tensor(s, s, mx[0:16, 0:q].unsqueeze(2).broadcast_to([16, q, n]), ALU.subtract).then_inc(s_dve, 1)
                e.wait_ge(s_act, step)
                link(e.tensor_reduce(zz[0:16, 0:q], s, AX, ALU.add))
                link(e.reciprocal(rz[0:16, 0:q], zz[0:16, 0:q]))
                e.tensor_tensor(s, s, rz[0:16, 0:q].unsqueeze(2).broadcast_to([16, q, n]), ALU.mult).then_inc(s_dve, 1)

            e.wait_ge(s_pe, 2)
            sC2 = s_S.rearrange("p q k -> p (q k)")[:, 0:16 * NCS].rearrange("p (q c) -> p q c", c=NCS)
            for g in range(G):
                last = e.tensor_tensor(sC2[:, g::G], bank(0, 16 * NCS, 16).rearrange("p (q c) -> p q c", c=NCS)[:, g::G],
                                       biasS[:, g, CB - 1:CB - 1 + CS * (NCS - 1) + 1:CS].unsqueeze(1).broadcast_to([16, NB, NCS]), ALU.add)
            link(last)
            softmax(sC2, 16, NCS, 2)
            e.wait_ge(s_pe, 4)
            e.tensor_tensor(ys, bank(2, 256), grow[:, 0], ALU.mult).then_inc(s_dve, 1)
            for p in range(4):
                kind, bh = p // 2, p % 2
                for g in range(G):
                    last = e.tensor_copy(kbuf[bh][:, :, g, PAST:KEYS],
                                         smp(kvq[:, 4 + 4 * kind + g])[:, 4 * bh:4 * bh + 4])
                last.then_inc(k_new, 1)
                e.wait_ge(s_pe, 4 * p + 5)
                for g in range(G):
                    last = e.tensor_tensor(s_S[:, g::G], ps[0:16, :].rearrange("p (q n) -> p q n", n=512)[:, g::G, 0:KEYS],
                                           biasS[:, g].unsqueeze(1).broadcast_to([16, 4, KEYS]), ALU.add)
                link(last)
                softmax(s_S, 8, KEYS, 2 * p + 4)
                e.wait_ge(s_pe, 4 * p + 8)
                c = P * bh
                link(e.tensor_tensor(ytmp[:, 0:P], bank(4, P), grow[:, kind + 1, c:c + P], ALU.mult))
                link(e.tensor_tensor(ys[:, c:c + P], ys[:, c:c + P], ytmp[:, 0:P], ALU.add))
                e.sem_inc(s_dve, 1)
            for h in range(QH):
                last = e.tensor_copy(smp(mix[:, 4 + h]), ys.rearrange("p (b n) -> p b n", b=NB)[:, :, TS * h:TS * h + TS])
            e.wait_ge(a_ye, QH)
            last.then_inc(s_dve, 1)

            e.wait_ge(ya_in, 16)
            group_norm(1)
            group_norm(2)
            e.wait_ge(n_lo, SPLIT_0[3] - 4)
            for c in range(4):
                e.tensor_copy(tn[c], mix[:, 12 + c]).then_inc(n_mul, 1)
            for c in range(4):
                e.wait_ge(n_hi, SPLIT_0[3] - 3 + c)
                e.tensor_tensor(xlo[:, 12 + c], tn[c], xhi_f[:, 12 + c], ALU.subtract).then_inc(n_lo, 1)
            split(0, H_OUT)
            split(0, H_OUT + 1)

            def h_sum(i, c):
                e.wait_ge(units, 2 * i + (U_OUT + c + 1))
                e.wait_ge(x_in[c], 16 * i + 16)
                for (d, x, b) in zip(halves(hbuf[:, 2 * i + c]), halves(xin[c]), (bank(2 * c, 256), bank(2 * c + 1, NT - 256))):
                    last = e.tensor_tensor(d, b, x, ALU.add)
                last.then_inc(h_add, 1)
            with e.Fori(0, KC // 2) as i:
                for c in range(2):
                    split(i, H_OUT + 2 * c + 2)
                    split(i, H_OUT + 2 * c + 3)
                    h_sum(i, c)
            e.wait_ge(h_add, KC)
            group_norm(3)

            def split_unit(i, h, tiles=(HALF_K, HALF_K)):
                split(i, h, P * tiles[0])
                split(i, h + 1, P * tiles[1])

            def up(i, part, first, last):
                h0 = H_UP + 2 * U_PART * part
                j = i + FQ * part
                for q in range(2):
                    split_unit(i, h0 + 2 * q + 2, DH if last and q else (HALF_K, HALF_K))
                    u = 2 * i + (2 * FQ * part + q)
                    e.wait_ge(up_evac, u + 1)
                    e.wait_ge(up_hist, u + 1)
                    if not first:
                        e.wait_ge(up_act, j)
                    x = fx[q]
                    e.tensor_scalar(facc[q], x[:, 0:ROW3 - 2], fw[:, u, 0:1], None, ALU.mult).then_inc(up_conv, 1)
                    for k in (1, 2):
                        e.wait_ge(up_conv, 3 * u + k)
                        e.scalar_tensor_tensor(out=facc[q], in0=x[:, k:ROW3 - 2 + k], scalar=fw[:, u, k:k + 1], in1=facc[q],
                                               op0=ALU.mult, op1=ALU.add).then_inc(up_conv, 1)
                e.wait_ge(up_silu, j + 1)
                e.wait_ge(up_conv, 3 * u + 3)
                if not first:
                    e.wait_ge(act_lo, j)
                e.tensor_tensor(aw_[:, 0:TP], facc[0][:, 0:TP], facc[1][:, 0:TP], ALU.mult)
                e.tensor_tensor(smp(aw_), seg(0), seg(1), ALU.mult).then_inc(up_act, 1)
                e.wait_ge(act_hi, j + 1)
                e.tensor_tensor(alo[:, i], aw_, ahi_f[:, i], ALU.subtract).then_inc(act_lo, 1)

            def seg(q):
                return arena[:, FACC + (ROW3 - 2) * q + 2 + TP:FACC + (ROW3 - 2) * q + 2 + TP + NB * SEG3].rearrange("p (b n) -> p b n", n=SEG3)[:, :, 0:TS]

            def y_sum(i, part, d):
                e.wait_ge(units, 2 * i + (U_UP + U_PART * part + 2 * FQ + d + 1))
                for (y, b) in zip(halves(hbuf[:, 2 * i + d]), (bank(2 * d, 256), bank(2 * d + 1, NT - 256))):
                    last = e.tensor_tensor(y, b, y, ALU.add)
                last.then_inc(y_add, 1)

            e.wait_ge(f_in, 32)
            for part in range(PARTS):
                up(0, part, part == 0, False)
                with e.Fori(1, FQ - 1) as i:
                    up(i, part, False, False)
                up(FQ - 1, part, False, True)
                if part > 0:
                    e.wait_ge(y_add, KC * part)
                h0 = H_UP + 2 * U_PART * part + 4 * FQ
                with e.Fori(0, KC // 2 - 1) as i:
                    for d in range(2):
                        split_unit(i, h0 + 2 * d + 2, DH)
                        y_sum(i, part, d)
                split_unit(KC // 2 - 1, h0 + 2, DH)
                y_sum(KC // 2 - 1, part, 0)
                if part < PARTS - 1:
                    split_unit(KC // 2 - 1, h0 + 4)
                y_sum(KC // 2 - 1, part, 1)

        @block.gpsimd
        def _(e):
            e.wait_ge(s_cst, 16 * 7)
            e.wait_ge(a_free, 1)
            e.memset(gbuf[:, :, 0:3], 0.0)
            e.tensor_copy(gbuf[:, :, 3 + TP:ROW4].rearrange("p c (b n) -> p c b n", n=SEG4)[:, :, :, 0:3], hist_g).then_inc(p_chain, 1)
            e.wait_ge(p_chain, 1)
            e.sem_inc(gconv_in, 1)
            e.dma_start(ya_dram, zbuf).then_inc(ya_out, 16)
            for c in range(N_A):
                e.wait_ge(proj_evac, N_A + N_KVQ + c + 1)
                e.tensor_copy(tail_g[:, c, 0:3], gbuf[:, c, TP:TP + 3])
                e.tensor_copy(tail_g[:, c, 3:27].rearrange("p (b k) -> p b k", k=3),
                              gbuf[:, c, 3 + TP:ROW4].rearrange("p (b n) -> p b n", n=SEG4)[:, :, 4:SEG4]).then_inc(tails, 1)

            e.wait_ge(n_lo, SPLIT_0[3] + 16)
            e.wait_ge(f_in, 32)
            for q in range(2):
                e.memset(fx[q][:, 0:2], 0.0)

            def rows(i, first=False):
                for q in range(2):
                    u = 2 * i + q
                    if not first:
                        e.wait_ge(up_conv, 3 * u - 3)
                    segs = fx[q][:, 2 + TP:ROW3].rearrange("p (b n) -> p b n", n=SEG3)
                    e.tensor_copy(segs[:, :, 0:2], hist[:, u]).then_inc(up_hist, 1)
                for q in range(2):
                    u = 2 * i + q
                    segs = fx[q][:, 2 + TP:ROW3].rearrange("p (b n) -> p b n", n=SEG3)
                    e.wait_ge(up_evac, u + 1)
                    e.tensor_copy(tail[:, u, 0:2], fx[q][:, TP:TP + 2])
                    e.tensor_copy(tail[:, u, 2:18].rearrange("p (b k) -> p b k", k=2), segs[:, :, 4:SEG3]).then_inc(up_tail, 1)

            rows(0, first=True)
            with e.Fori(1, FC) as i:
                rows(i)


_OUTS = {
    "y_t": (P, KC, NT), "kv_t": (P, N_A, NT), "win_old": (NB, PAST, 2 * G * P), "tail_a": (P, 4, 18), "tail_g": (P, N_A, 27),
    "gdn_sp": (P, GH * P), "gdn_ss": (P, NB, GH, P), "tail_f": (P, 2 * FC, 18),
}


def _cols(w, n):
    k = w.shape[0] // P
    return np.ascontiguousarray(w.reshape(k, P, n, P).transpose(2, 1, 0, 3).reshape(n, P, k * P))


def _feat(a, lead):
    x = a.reshape(*a.shape[:-1], -1, P)
    return np.ascontiguousarray(np.moveaxis(np.moveaxis(x, -1, 0), -1, 1))


def lay_out(x):
    x = {k: np.asarray(v) for k, v in x.items()}
    w = x["w_in"][0]
    o = np.cumsum([0, 512, 512, 512, 1024, 1536, 24, 1536, 4, 4, 512])
    part = [w[:, o[i]:o[i + 1]] for i in range(10)]
    a_b, a_c, a_h, nq, nkv, gate, qkv, ga, gb, gz = part
    abc = np.stack([p.reshape(DM, 4, P) for p in (a_c, a_h, a_b)], axis=2).reshape(DM, 12 * P)
    consts, onehot, neg = shape_constants()
    toks = np.concatenate([x["x_prompt"][0], x["x_sample"].reshape(NS, DM)], axis=0)
    d = {}
    d["x_t"] = np.ascontiguousarray(toks.T.reshape(KC, P, NT).transpose(1, 0, 2))
    d["consts"], d["onehot"], d["neg"] = consts, onehot, neg
    flip = np.zeros((P, P + 16), np.float32)
    flip[:, :P] = np.eye(P)[::-1]
    flip[:16, P:] = np.kron(np.eye(REP), np.eye(TS)[::-1])
    d["flip"] = flip
    d["w_proj"] = _cols(np.concatenate([abc, nkv, nq, qkv, gz], axis=1), PROJ)
    small = np.concatenate([gate, ga, gb], axis=1)
    d["w_small"] = np.ascontiguousarray(small.reshape(KC, P, 32).transpose(1, 0, 2))
    vec = [x[n][0].reshape(-1, P).T for n in ("norm_mix_g", "norm_ffn_g", "out_norm_a", "out_norm_b", "q_norm_g", "k_norm_g", "gdn_norm_g")]
    d["gains"] = np.ascontiguousarray(np.concatenate(vec, axis=1))
    d["conv_w"] = np.concatenate([_feat(x["conv_a_w"][0], 1).reshape(P, 12), _feat(x["gdn_conv_w"][0], 1).reshape(P, 48)], axis=1)
    d["ffn_w"] = _inter(_feat(x["ffn_conv_w"][0], 1))
    d["hist_a"] = _feat(x["state_conv_a"][0], 2)
    d["hist_g"] = _feat(x["state_gdn_conv"][0], 2)
    d["hist_f"] = _inter(_feat(x["state_ffn_conv"][0], 2))
    d["gdn_ab"] = np.ascontiguousarray(np.broadcast_to(np.concatenate([x["gdn_a_log"][0], x["gdn_dt_bias"][0]])[None], (P, 8)))
    d["pe_t"] = np.zeros((P, 2, PAST), np.float32)
    d["pe_t"][:, :, :CB] = x["cmp_pe"][0].transpose(2, 0, 1)
    d["page_table"] = np.ascontiguousarray(x["page_table"].reshape(1, 16))
    d["rel_bias"] = x["rel_bias"]
    d["state_gdn"] = np.ascontiguousarray(x["state_gdn"][0].transpose(2, 0, 1, 3))
    kv = x["cache_kv"][0]
    d["cache_kt"] = np.ascontiguousarray(kv[:, :, 0:3].transpose(0, 4, 2, 3, 1))
    d["cache_v"] = np.ascontiguousarray(kv[:, :, 3])
    cw = x["cache_win"][0]
    d["win_kt"] = np.ascontiguousarray(cw[:, :, 0].transpose(3, 0, 2, 1))
    d["win_v"] = np.ascontiguousarray(cw[:, :, 1].reshape(NB, 2, PAGE, G, P).transpose(2, 0, 1, 3, 4))
    d["cache_win"] = cw.reshape(NB, PAST, 2 * G * P)
    w1 = x["cmp_w1"][0].reshape(2, 2, 16, P, 2, P)
    d["w1c"] = np.ascontiguousarray(w1.transpose(0, 4, 1, 3, 2, 5).reshape(8, P, UNIT))
    d["w2c"] = np.ascontiguousarray(x["cmp_w2"][0].reshape(2, 2, P, P).transpose(2, 0, 1, 3).reshape(P, 512))
    d["w_o"] = _cols(x["w_out"][0], KC)
    up = x["ffn_up"][0].reshape(DM, 2, FC, P).transpose(0, 2, 1, 3).reshape(DM, 2 * DFF)
    d["w_up"] = _cols(up, 2 * FC)
    d["w_dn"] = np.ascontiguousarray(_cols(x["ffn_down"][0], KC).reshape(KC, P, PARTS, FQ * P).transpose(2, 0, 1, 3).reshape(PARTS * KC, P, FQ * P))
    return d


def _inter(a):
    return np.ascontiguousarray(a.reshape(P, 2, FC, *a.shape[2:]).swapaxes(1, 2).reshape(P, 2 * FC, *a.shape[2:]))


def take_back(r):
    def feats(a):
        return np.ascontiguousarray(a.transpose(2, 1, 0)).reshape(a.shape[2], -1)

    def tails(a, k):
        f = feats(a)
        return f[:k][None, None], f[k:].reshape(1, NB, k, -1)

    y = feats(r["y_t"])
    kv = feats(r["kv_t"]).reshape(NT, 3, 2, G, P)
    rows, win = kv[:, 0:2].reshape(NT, 4, G, P), kv[:, 2]
    old = r["win_old"].reshape(NB, PAST, 2, G, P)
    win_s = np.concatenate([old, win[TP:].reshape(NB, TS, 2, G, P)], axis=1)
    ca, gv = tails(r["tail_a"], 2), tails(r["tail_g"], 3)
    tf = r["tail_f"].reshape(P, FC, 2, 18).transpose(0, 2, 1, 3).reshape(P, 2 * FC, 18)
    ff = tails(tf, 2)
    sp = r["gdn_sp"].reshape(P, GH, P).transpose(1, 0, 2)[None, None]
    ss = r["gdn_ss"].transpose(1, 2, 0, 3)[None]
    c = np.ascontiguousarray
    return (c(y[:TP][None]), c(y[TP:].reshape(NB, TS, DM)), c(rows[:TP][None, None]), c(rows[TP:].reshape(1, NB, TS, 4, G, P)),
            c(win[:TP][None, None]), c(win_s[None]), c(ca[0]), c(ca[1]), c(gv[0]), c(gv[1]), c(sp), c(ss), c(ff[0]), c(ff[1]))


def kernel(**inputs):
    import concourse.bacc as bacc
    from concourse.bass_utils import run_bass_kernel_spmd

    nc = bacc.Bacc("TRN2", target_bir_lowering=False, num_devices=1)
    arrays, ins, outs = {}, {}, {}
    for name, a in lay_out(inputs).items():
        arrays[f"in_{name}"] = a
        ins[name] = nc.dram_tensor(f"in_{name}", a.shape, mybir.dt.from_np(a.dtype), kind="ExternalInput").ap()
    for name, shape in _OUTS.items():
        outs[name] = nc.dram_tensor(f"out_{name}", shape, F32, kind="ExternalOutput").ap()
    build(nc, ins, outs)
    r = run_bass_kernel_spmd(nc, [arrays], core_ids=[0])
    return take_back({name: r.results[0][f"out_{name}"] for name in _OUTS})
```
